# Optimizing a Trainium2 kernel written in Bass

```python
import math
import jax, jax.numpy as jnp
from jax import lax
import numpy as np
import jax
import jax.numpy as jnp

D_MODEL = 2048
BATCH = 1
SEQ = 256
DEPTH = 2

N_MIXERS = 4
WIDTH = D_MODEL
EPS = 1e-6
CONV_WIDTH = 31
HG_HEAD_DIM = 128
HG_HEADS = WIDTH // HG_HEAD_DIM
HG_CHUNK = 64
DA_HEAD_DIM = 128
DA_HEADS = WIDTH // (2 * DA_HEAD_DIM)
DA_V_DIM = 2 * DA_HEAD_DIM
ROPE_THETA = 500000.0
ROPE_DIM = DA_HEAD_DIM // 4
Q_BLOCK = 128
FN_GROUPS = 8
FN_GROUP_DIM = WIDTH // FN_GROUPS
N_CONV = len(range(0, DEPTH, N_MIXERS))
N_HGRN = len(range(1, DEPTH, N_MIXERS))
N_DIFF = len(range(2, DEPTH, N_MIXERS))
N_FNET = len(range(3, DEPTH, N_MIXERS))


def rms_norm(x, g):
    xf = x.astype(jnp.float32)
    y = xf * lax.rsqrt(jnp.mean(xf * xf, axis=-1, keepdims=True) + EPS)
    return (y * g.astype(jnp.float32)).astype(x.dtype)

def layer_norm(x, g, b):
    xf = x.astype(jnp.float32)
    mu = jnp.mean(xf, axis=-1, keepdims=True)
    var = jnp.mean(jnp.square(xf - mu), axis=-1, keepdims=True)
    y = (xf - mu) * lax.rsqrt(var + EPS)
    return (y * g.astype(jnp.float32) + b.astype(jnp.float32)).astype(x.dtype)

def conformer_conv(h, w_in, dw, dw_b, ln_g, ln_b, w_out):
    u = h @ w_in
    a, b, z = jnp.split(u, 3, axis=-1)
    v = a * jax.nn.sigmoid(b)
    pad = CONV_WIDTH // 2
    v = lax.conv_general_dilated(
        v, dw[:, None, :].astype(v.dtype), window_strides=(1,), padding=[(pad, pad)],
        dimension_numbers=("NWC", "WIO", "NWC"), feature_group_count=WIDTH) + dw_b
    v = jax.nn.silu(layer_norm(v, ln_g, ln_b))
    return (v * jax.nn.silu(z)) @ w_out

def hgrn_lower_bounds(table):
    lb = jnp.cumsum(jax.nn.softmax(table.astype(jnp.float32), axis=0), axis=0)
    return lb - lb[0:1]

def hgrn_direction(q, k, v, log_f):
    B, H, S, _ = q.shape
    nc = S // HG_CHUNK

    def chunks(t):
        return jnp.moveaxis(t.reshape(B, H, nc, HG_CHUNK, t.shape[-1]), 2, 0)

    lower_tri = jnp.tril(jnp.ones((HG_CHUNK, HG_CHUNK), dtype=bool))[:, :, None]

    def step(state, inp):
        qb, kb, vb, fb = inp
        b = jnp.cumsum(fb, axis=2)
        o_inter = jnp.einsum("bhtk,bhkv->bhtv", qb * jnp.exp(b), state)
        diff = b[:, :, :, None, :] - b[:, :, None, :, :]
        decay = jnp.exp(jnp.where(lower_tri, diff, -jnp.inf))
        scores = jnp.einsum("bhtk,bhsk,bhtsk->bhts", qb, kb, decay)
        o_intra = jnp.einsum("bhts,bhsv->bhtv", scores, vb)
        b_last = b[:, :, -1:, :]
        new_state = state * jnp.exp(b_last)[:, :, 0, :, None] + jnp.einsum(
            "bhsk,bhsv->bhkv", kb * jnp.exp(b_last - b), vb)
        return new_state, o_inter + o_intra

    state0 = jnp.zeros((B, H, q.shape[-1], v.shape[-1]), jnp.float32)
    _, out = lax.scan(step, state0, (chunks(q), chunks(k), chunks(v), chunks(log_f)))
    return jnp.moveaxis(out, 0, 2).reshape(B, H, S, v.shape[-1])

def hgrn2_mixer(h, w_in, lb_fwd, lb_bwd, o_norm, w_out):
    B, S, _ = h.shape
    u = h @ w_in
    q, a_f, a_b, i, z = jnp.split(u, 5, axis=-1)

    def heads(t):
        return t.astype(jnp.float32).reshape(B, S, HG_HEADS, HG_HEAD_DIM).transpose(0, 2, 1, 3)

    def forget(a, lb):
        a = a.astype(jnp.float32)
        log_f = jnp.logaddexp(jnp.log(lb), jnp.log1p(-lb) + jax.nn.log_sigmoid(a))
        key = (1.0 - lb) * jax.nn.sigmoid(-a)
        return heads(log_f), heads(key)

    qh, vh = heads(q), heads(i)
    lf_f, k_f = forget(a_f, lb_fwd)
    lf_b, k_b = forget(a_b, lb_bwd)
    o_fwd = hgrn_direction(qh, k_f, vh, lf_f)
    flip = lambda t: jnp.flip(t, axis=2)
    o_bwd = flip(hgrn_direction(flip(qh), flip(k_b), flip(vh), flip(lf_b)))
    o = rms_norm(o_fwd + o_bwd, o_norm)
    o = o.transpose(0, 2, 1, 3).reshape(B, S, WIDTH).astype(h.dtype)
    return (o * jax.nn.silu(z)) @ w_out

def rope_tables(positions):
    inv = 1.0 / (ROPE_THETA ** (jnp.arange(0, ROPE_DIM, 2, dtype=jnp.float32) / ROPE_DIM))
    ang = positions.astype(jnp.float32)[..., None] * inv
    return jnp.cos(ang), jnp.sin(ang)

def apply_partial_rope(x, cos, sin):
    xr, xp = x[..., :ROPE_DIM], x[..., ROPE_DIM:]
    x1, x2 = jnp.split(xr.astype(jnp.float32), 2, axis=-1)
    c = cos[:, :, None, None, :]
    s = sin[:, :, None, None, :]
    rot = jnp.concatenate([x1 * c - x2 * s, x2 * c + x1 * s], axis=-1)
    return jnp.concatenate([rot.astype(x.dtype), xp], axis=-1)

def diff_attention(h, cos, sin, w_in, q_norm, k_norm, lam_q1, lam_k1, lam_q2, lam_k2,
                   sub_norm, w_out, lam_init):
    B, S, _ = h.shape
    u = h @ w_in
    q, k, v, z = jnp.split(u, 4, axis=-1)
    q = rms_norm(q.reshape(B, S, DA_HEADS, 2, DA_HEAD_DIM), q_norm)
    k = rms_norm(k.reshape(B, S, DA_HEADS, 2, DA_HEAD_DIM), k_norm)
    q = apply_partial_rope(q, cos, sin).transpose(0, 2, 3, 1, 4)
    k = apply_partial_rope(k, cos, sin).transpose(0, 2, 3, 1, 4)
    v = v.reshape(B, S, DA_HEADS, DA_V_DIM).transpose(0, 2, 1, 3)
    f32 = jnp.float32
    lam = (jnp.exp(jnp.sum(lam_q1.astype(f32) * lam_k1.astype(f32)))
           - jnp.exp(jnp.sum(lam_q2.astype(f32) * lam_k2.astype(f32))) + lam_init)
    scale = 1.0 / math.sqrt(DA_HEAD_DIM)
    nq = S // Q_BLOCK
    qb_all = q.reshape(B, DA_HEADS, 2, nq, Q_BLOCK, DA_HEAD_DIM).transpose(3, 0, 1, 2, 4, 5)

    def block(qb):
        s = jnp.einsum("bhmqd,bhmkd->bhmqk", qb, k).astype(f32) * scale
        p = jax.nn.softmax(s, axis=-1)
        w = p[:, :, 0] - lam * p[:, :, 1]
        return jnp.einsum("bhqk,bhkv->bhqv", w.astype(v.dtype), v)

    o = lax.map(block, qb_all)
    o = o.transpose(1, 2, 0, 3, 4).reshape(B, DA_HEADS, S, DA_V_DIM)
    o = rms_norm(o, sub_norm) * (1.0 - lam_init)
    o = o.transpose(0, 2, 1, 3).reshape(B, S, WIDTH).astype(h.dtype)
    return (o * jax.nn.silu(z)) @ w_out

def fourier_mixer(h, w_in, group_w, w_out):
    B, S, _ = h.shape
    u = h @ w_in
    v, z = jnp.split(u, 2, axis=-1)
    vg = v.astype(jnp.float32).reshape(B, S, FN_GROUPS, FN_GROUP_DIM)
    f = jnp.fft.fftn(vg, axes=(1, 3), norm="ortho").real
    y = jnp.einsum("bsgc,gce->bsge", f.astype(h.dtype), group_w).reshape(B, S, WIDTH)
    return (y * jax.nn.silu(z)) @ w_out

def first_inputs(seed: int = 0) -> dict:
    key = jax.random.key(seed)
    ks = iter(jax.random.split(key, 40))
    E, D = WIDTH, D_MODEL
    nrm = lambda shape, s: jax.random.normal(next(ks), shape, jnp.float32) * s
    gain = lambda shape: 1.0 + nrm(shape, 0.02)
    return {
        "x": nrm((BATCH, SEQ, D), 1.0),
        "positions": jnp.broadcast_to(jnp.arange(SEQ, dtype=jnp.int32)[None, :], (BATCH, SEQ)),
        "conv_norm": gain((N_CONV, D)),
        "conv_w_in": nrm((N_CONV, D, 3 * E), D ** -0.5),
        "conv_dw": nrm((N_CONV, CONV_WIDTH, E), CONV_WIDTH ** -0.5),
        "conv_dw_b": nrm((N_CONV, E), 0.02),
        "conv_ln_g": gain((N_CONV, E)),
        "conv_ln_b": nrm((N_CONV, E), 0.02),
        "conv_w_out": nrm((N_CONV, E, D), E ** -0.5),
        "hgrn_norm": gain((N_HGRN, D)),
        "hgrn_w_in": nrm((N_HGRN, D, 5 * E), D ** -0.5),
        "hgrn_lb_fwd": nrm((DEPTH, E), 0.1),
        "hgrn_lb_bwd": nrm((DEPTH, E), 0.1),
        "hgrn_o_norm": gain((N_HGRN, HG_HEAD_DIM)),
        "hgrn_w_out": nrm((N_HGRN, E, D), E ** -0.5),
        "diff_norm": gain((N_DIFF, D)),
        "diff_w_in": nrm((N_DIFF, D, 4 * E), D ** -0.5),
        "diff_q_norm": gain((N_DIFF, DA_HEAD_DIM)),
        "diff_k_norm": gain((N_DIFF, DA_HEAD_DIM)),
        "diff_lam_q1": nrm((N_DIFF, DA_HEAD_DIM), 0.1),
        "diff_lam_k1": nrm((N_DIFF, DA_HEAD_DIM), 0.1),
        "diff_lam_q2": nrm((N_DIFF, DA_HEAD_DIM), 0.1),
        "diff_lam_k2": nrm((N_DIFF, DA_HEAD_DIM), 0.1),
        "diff_sub_norm": gain((N_DIFF, DA_V_DIM)),
        "diff_w_out": nrm((N_DIFF, E, D), E ** -0.5),
        "fnet_norm": gain((N_FNET, D)),
        "fnet_w_in": nrm((N_FNET, D, 2 * E), D ** -0.5),
        "fnet_group_w": nrm((N_FNET, FN_GROUPS, FN_GROUP_DIM, FN_GROUP_DIM), FN_GROUP_DIM ** -0.5),
        "fnet_w_out": nrm((N_FNET, E, D), E ** -0.5),
    }

def first_block(x, positions, conv_norm, conv_w_in, conv_dw, conv_dw_b, conv_ln_g, conv_ln_b, conv_w_out,
              hgrn_norm, hgrn_w_in, hgrn_lb_fwd, hgrn_lb_bwd, hgrn_o_norm, hgrn_w_out,
              diff_norm, diff_w_in, diff_q_norm, diff_k_norm, diff_lam_q1, diff_lam_k1, diff_lam_q2,
              diff_lam_k2, diff_sub_norm, diff_w_out,
              fnet_norm, fnet_w_in, fnet_group_w, fnet_w_out):
    cos, sin = rope_tables(positions)
    lb_fwd = hgrn_lower_bounds(hgrn_lb_fwd)
    lb_bwd = hgrn_lower_bounds(hgrn_lb_bwd)
    for layer in range(DEPTH):
        m, j = layer % N_MIXERS, layer // N_MIXERS
        if m == 0:
            h = rms_norm(x, conv_norm[j])
            y = conformer_conv(h, conv_w_in[j], conv_dw[j], conv_dw_b[j], conv_ln_g[j], conv_ln_b[j],
                               conv_w_out[j])
        elif m == 1:
            h = rms_norm(x, hgrn_norm[j])
            y = hgrn2_mixer(h, hgrn_w_in[j], lb_fwd[layer], lb_bwd[layer], hgrn_o_norm[j], hgrn_w_out[j])
        elif m == 2:
            h = rms_norm(x, diff_norm[j])
            lam_init = 0.8 - 0.6 * math.exp(-0.3 * layer)
            y = diff_attention(h, cos, sin, diff_w_in[j], diff_q_norm[j], diff_k_norm[j], diff_lam_q1[j],
                               diff_lam_k1[j], diff_lam_q2[j], diff_lam_k2[j], diff_sub_norm[j],
                               diff_w_out[j], lam_init)
        else:
            h = rms_norm(x, fnet_norm[j])
            y = fourier_mixer(h, fnet_w_in[j], fnet_group_w[j], fnet_w_out[j])
        x = x + y.astype(x.dtype)
    return x


DEPTH_2 = 1

MEM_LEN = 256
NEG = -1e30
BIG = 1e30
NSA_HEADS = 8
NSA_KV_HEADS = 2
NSA_GROUP = NSA_HEADS // NSA_KV_HEADS
NSA_DK = 128
NSA_DV = 128
CMP_LEN = 32
CMP_STRIDE = 16
CMP_HIDDEN = 256
SEL_BLOCK = 64
SEL_TOP = 16
WINDOW = 512
NSA_QBLOCK = 64
GLA_HEADS = 4
GLA_DK = 128
GLA_DV = 256
GLA_GATE_RANK = 16
GLA_GATE_NORM = 16.0
GLA_CHUNK = 64
D_MIX = NSA_HEADS * NSA_DV + GLA_HEADS * GLA_DV
MEM_HEADS = 4
MEM_DH = 128
D_FF = -(-8 * D_MODEL // (3 * 256)) * 256
IN_SIZES = (
    NSA_HEADS * NSA_DK,
    NSA_KV_HEADS * NSA_DK, NSA_KV_HEADS * NSA_DV,
    NSA_KV_HEADS * NSA_DK, NSA_KV_HEADS * NSA_DV,
    NSA_KV_HEADS * NSA_DK, NSA_KV_HEADS * NSA_DV,
    3 * NSA_HEADS,
    GLA_HEADS * GLA_DK, GLA_HEADS * GLA_DK,
    GLA_HEADS * GLA_DV,
    GLA_GATE_RANK,
    GLA_HEADS * GLA_DV,
)
D_IN = sum(IN_SIZES)


def rms_norm_2(u, g):
    uf = u.astype(jnp.float32)
    y = uf * lax.rsqrt(jnp.mean(uf * uf, axis=-1, keepdims=True) + EPS)
    return (y * g.astype(jnp.float32)).astype(u.dtype)

def alibi_slopes(n):
    return jnp.exp2(-8.0 * jnp.arange(1, n + 1, dtype=jnp.float32) / n)

def split_points():
    return np.cumsum(np.array(IN_SIZES))[:-1].tolist()

def nsa_mixer(q, k_cmp, v_cmp, k_slc, v_slc, k_win, v_win, gates,
              g_q, g_kc, g_ks, g_kw, pe_k, pe_v, w_ck1, w_ck2, w_cv1, w_cv2):
    f32 = jnp.float32
    B, T = q.shape[0], q.shape[1]
    HKV, G, QB = NSA_KV_HEADS, NSA_GROUP, NSA_QBLOCK
    n_cmp = (T - CMP_LEN) // CMP_STRIDE + 1
    n_sel = T // SEL_BLOCK
    n_top = min(SEL_TOP, n_sel)
    n_qb = T // QB
    ratio = SEL_BLOCK // CMP_STRIDE
    lead = CMP_LEN // CMP_STRIDE - 1

    tok = jnp.arange(n_cmp)[:, None] * CMP_STRIDE + jnp.arange(CMP_LEN)[None, :]

    def compress(u, pe, w1, w2):
        blk = u[:, tok] + pe[None, None, :, None, :]
        blk = blk.transpose(0, 1, 3, 2, 4).reshape(B, n_cmp, HKV, -1)
        return (jax.nn.silu(blk @ w1) @ w2).transpose(0, 2, 1, 3)

    kc = rms_norm_2(compress(k_cmp, pe_k, w_ck1, w_ck2), g_kc)
    vc = compress(v_cmp, pe_v, w_cv1, w_cv2)
    cmp_end = jnp.arange(n_cmp) * CMP_STRIDE + (CMP_LEN - 1)
    cmp_mid = jnp.arange(n_cmp).astype(f32) * CMP_STRIDE + 0.5 * (CMP_LEN - 1)

    r = np.arange(ratio + lead)
    st = CMP_STRIDE * (r - lead)
    ov = jnp.asarray((np.minimum(st + CMP_LEN, SEL_BLOCK) - np.maximum(st, 0)) / CMP_STRIDE, f32)
    sel_idx = jnp.arange(n_sel)[:, None] * ratio + jnp.asarray(r)[None, :]

    ksb = rms_norm_2(k_slc, g_ks).reshape(B, n_sel, SEL_BLOCK, HKV, NSA_DK).transpose(0, 3, 1, 2, 4)
    vsb = v_slc.reshape(B, n_sel, SEL_BLOCK, HKV, NSA_DV).transpose(0, 3, 1, 2, 4)
    pad_t = ((0, 0), (0, 0), (WINDOW, 0), (0, 0))
    kwp = jnp.pad(rms_norm_2(k_win, g_kw).transpose(0, 2, 1, 3), pad_t)
    vwp = jnp.pad(v_win.transpose(0, 2, 1, 3), pad_t)

    slopes = alibi_slopes(NSA_HEADS).reshape(HKV, G)
    sl5 = slopes[None, :, :, None, None]
    sl6 = slopes[None, :, :, None, None, None]
    jb = jnp.arange(n_sel)
    bi = jnp.arange(B)[:, None, None, None]
    hi = jnp.arange(HKV)[None, :, None, None]

    qn = rms_norm_2(q, g_q) * (NSA_DK ** -0.5)
    qs = qn.reshape(B, n_qb, QB, HKV, G, NSA_DK).transpose(1, 0, 3, 4, 2, 5)
    gs = gates.reshape(B, n_qb, QB, HKV, G, 3).transpose(1, 0, 3, 4, 2, 5)

    def block(args):
        c, qb, gb = args
        t = c * QB + jnp.arange(QB)
        s = jnp.einsum('bkgtd,bknd->bkgtn', qb, kc).astype(f32)
        vis = t[:, None] >= cmp_end[None, :]
        s = jnp.where(vis, s - sl5 * (t[:, None].astype(f32) - cmp_mid[None, :]), NEG)
        p = jax.nn.softmax(s, axis=-1)
        p = jnp.where(jnp.any(vis, axis=-1)[:, None], p, 0.0)
        o_cmp = jnp.einsum('bkgtn,bknd->bkgtd', p.astype(vc.dtype), vc)
        imp = jnp.pad(p.sum(2), ((0, 0), (0, 0), (0, 0), (lead, lead)))
        imp = jnp.einsum('bktjr,r->bktj', imp[..., sel_idx], ov)
        cur = (t // SEL_BLOCK)[:, None]
        forced = (jb == 0) | (jb == cur) | (jb == cur - 1)
        score = jnp.where(forced, BIG, jnp.where(jb <= cur, imp, NEG))
        top_s, top_i = lax.top_k(score, n_top)
        ks_g = ksb[bi, hi, top_i]
        vs_g = vsb[bi, hi, top_i]
        pos = top_i[..., None] * SEL_BLOCK + jnp.arange(SEL_BLOCK)
        tt = t[:, None, None]
        ok = (top_s > 0.5 * NEG)[..., None] & (pos <= tt)
        s = jnp.einsum('bkgtd,bktnsd->bkgtns', qb, ks_g).astype(f32)
        s = jnp.where(ok[:, :, None], s - sl6 * (tt - pos).astype(f32)[:, :, None], NEG)
        p = jax.nn.softmax(s.reshape(s.shape[:4] + (-1,)), axis=-1).reshape(s.shape)
        o_slc = jnp.einsum('bkgtns,bktnsd->bkgtd', p.astype(vs_g.dtype), vs_g)
        kw = lax.dynamic_slice_in_dim(kwp, c * QB, QB + WINDOW, axis=2)
        vw = lax.dynamic_slice_in_dim(vwp, c * QB, QB + WINDOW, axis=2)
        pos_w = c * QB - WINDOW + jnp.arange(QB + WINDOW)
        dw = t[:, None] - pos_w[None, :]
        okw = (dw >= 0) & (dw < WINDOW) & (pos_w >= 0)[None, :]
        s = jnp.einsum('bkgtd,bksd->bkgts', qb, kw).astype(f32)
        s = jnp.where(okw, s - sl5 * dw.astype(f32), NEG)
        p = jax.nn.softmax(s, axis=-1)
        o_win = jnp.einsum('bkgts,bksd->bkgtd', p.astype(vw.dtype), vw)
        return gb[..., 0:1] * o_cmp + gb[..., 1:2] * o_slc + gb[..., 2:3] * o_win

    out = lax.map(block, (jnp.arange(n_qb), qs, gs))
    return out.transpose(1, 0, 4, 2, 3, 5).reshape(B, T, NSA_HEADS, NSA_DV)

def gla_mixer(q, k, v, log_a):
    B, T, H, DK = q.shape
    DV = v.shape[-1]
    C = GLA_CHUNK
    n = T // C

    def chunks(u):
        return u.astype(jnp.float32).reshape(B, n, C, H, -1).transpose(1, 0, 3, 2, 4)

    causal = jnp.tril(jnp.ones((C, C), bool))[:, :, None]

    def step(S, inp):
        qc, kc, vc, ac = inp
        b = jnp.cumsum(ac, axis=2)
        decay = jnp.exp(jnp.where(causal, b[:, :, :, None, :] - b[:, :, None, :, :], -jnp.inf))
        attn = jnp.einsum('bhid,bhjd,bhijd->bhij', qc, kc, decay)
        o = (jnp.einsum('bhij,bhjv->bhiv', attn, vc)
             + jnp.einsum('bhid,bhdv->bhiv', qc * jnp.exp(b), S))
        b_end = b[:, :, -1:, :]
        S = (S * jnp.exp(b_end[:, :, 0, :, None])
             + jnp.einsum('bhjd,bhjv->bhdv', kc * jnp.exp(b_end - b), vc))
        return S, o

    S0 = jnp.zeros((B, H, DK, DV), jnp.float32)
    _, o = lax.scan(step, S0, (chunks(q), chunks(k), chunks(v), chunks(log_a)))
    return o.transpose(1, 0, 3, 2, 4).reshape(B, T, H, DV)

def hybrid_layer(x, mem, g_mix, w_in, b_nsa_gate, g_q, g_kc, g_ks, g_kw, pe_k, pe_v,
                 w_ck1, w_ck2, w_cv1, w_cv2, g_nsa_out, w_gk2, b_gk, g_gla_out, w_out,
                 g_cross, g_mem, w_cq, w_ck, w_cv, g_cq, g_ck, w_co, g_ffn, w_gu, w_down):
    B, T, _ = x.shape
    M = mem.shape[1]
    h = rms_norm_2(x, g_mix)
    (q, k_c, v_c, k_s, v_s, k_w, v_w, g_logit,
     q_l, k_l, v_l, a_l, r_l) = jnp.split(h @ w_in, split_points(), axis=-1)

    def heads(u, nh):
        return u.reshape(B, T, nh, -1)

    hkv = NSA_KV_HEADS
    gates = jax.nn.sigmoid(g_logit + b_nsa_gate).reshape(B, T, NSA_HEADS, 3)
    o_nsa = nsa_mixer(heads(q, NSA_HEADS), heads(k_c, hkv), heads(v_c, hkv), heads(k_s, hkv),
                      heads(v_s, hkv), heads(k_w, hkv), heads(v_w, hkv), gates,
                      g_q, g_kc, g_ks, g_kw, pe_k, pe_v, w_ck1, w_ck2, w_cv1, w_cv2)
    o_nsa = rms_norm_2(o_nsa, g_nsa_out).reshape(B, T, -1)

    log_a = jax.nn.log_sigmoid((a_l @ w_gk2 + b_gk).astype(jnp.float32)) / GLA_GATE_NORM
    o_gla = gla_mixer(heads(q_l, GLA_HEADS) * (GLA_DK ** -0.5), heads(k_l, GLA_HEADS),
                      heads(v_l, GLA_HEADS), heads(log_a, GLA_HEADS))
    o_gla = rms_norm_2(o_gla, g_gla_out).astype(x.dtype).reshape(B, T, -1) * jax.nn.silu(r_l)
    x = x + jnp.concatenate([o_nsa, o_gla], axis=-1) @ w_out

    hq = rms_norm_2(x, g_cross)
    hm = rms_norm_2(mem, g_mem)
    cq = rms_norm_2((hq @ w_cq).reshape(B, T, MEM_HEADS, MEM_DH), g_cq) * (MEM_DH ** -0.5)
    ck = rms_norm_2((hm @ w_ck).reshape(B, M, MEM_HEADS, MEM_DH), g_ck)
    cv = (hm @ w_cv).reshape(B, M, MEM_HEADS, MEM_DH)
    s = jnp.einsum('bthd,bmhd->bhtm', cq, ck).astype(jnp.float32)
    p = jax.nn.softmax(s, axis=-1).astype(cv.dtype)
    x = x + jnp.einsum('bhtm,bmhd->bthd', p, cv).reshape(B, T, -1) @ w_co

    hf = rms_norm_2(x, g_ffn)
    gg, uu = jnp.split(hf @ w_gu, 2, axis=-1)
    return x + (jax.nn.silu(gg) * uu) @ w_down

def second_inputs(seed: int = 0) -> dict:
    key = jax.random.key(seed)
    keys = iter(jax.random.split(key, 40))
    L = DEPTH_2

    def nrm(shape, scale):
        return scale * jax.random.normal(next(keys), shape, jnp.float32)

    def gain(n):
        return 1.0 + nrm((L, n), 0.05)

    return {
        'x': nrm((BATCH, SEQ, D_MODEL), 1.0),
        'mem': nrm((BATCH, MEM_LEN, D_MODEL), 1.0),
        'g_mix': gain(D_MODEL),
        'w_in': nrm((L, D_MODEL, D_IN), D_MODEL ** -0.5),
        'b_nsa_gate': nrm((L, 3 * NSA_HEADS), 0.1),
        'g_q': gain(NSA_DK),
        'g_kc': gain(NSA_DK),
        'g_ks': gain(NSA_DK),
        'g_kw': gain(NSA_DK),
        'pe_k': nrm((L, CMP_LEN, NSA_DK), 0.5),
        'pe_v': nrm((L, CMP_LEN, NSA_DV), 0.5),
        'w_ck1': nrm((L, CMP_LEN * NSA_DK, CMP_HIDDEN), (CMP_LEN * NSA_DK) ** -0.5),
        'w_ck2': nrm((L, CMP_HIDDEN, NSA_DK), CMP_HIDDEN ** -0.5),
        'w_cv1': nrm((L, CMP_LEN * NSA_DV, CMP_HIDDEN), (CMP_LEN * NSA_DV) ** -0.5),
        'w_cv2': nrm((L, CMP_HIDDEN, NSA_DV), CMP_HIDDEN ** -0.5),
        'g_nsa_out': gain(NSA_DV),
        'w_gk2': nrm((L, GLA_GATE_RANK, GLA_HEADS * GLA_DK), GLA_GATE_RANK ** -0.5),
        'b_gk': nrm((L, GLA_HEADS * GLA_DK), 0.1),
        'g_gla_out': gain(GLA_DV),
        'w_out': nrm((L, D_MIX, D_MODEL), D_MIX ** -0.5),
        'g_cross': gain(D_MODEL),
        'g_mem': gain(D_MODEL),
        'w_cq': nrm((L, D_MODEL, MEM_HEADS * MEM_DH), D_MODEL ** -0.5),
        'w_ck': nrm((L, D_MODEL, MEM_HEADS * MEM_DH), D_MODEL ** -0.5),
        'w_cv': nrm((L, D_MODEL, MEM_HEADS * MEM_DH), D_MODEL ** -0.5),
        'g_cq': gain(MEM_DH),
        'g_ck': gain(MEM_DH),
        'w_co': nrm((L, MEM_HEADS * MEM_DH, D_MODEL), (MEM_HEADS * MEM_DH) ** -0.5),
        'g_ffn': gain(D_MODEL),
        'w_gu': nrm((L, D_MODEL, 2 * D_FF), D_MODEL ** -0.5),
        'w_down': nrm((L, D_FF, D_MODEL), D_FF ** -0.5),
    }

def second_block(x, mem, g_mix, w_in, b_nsa_gate, g_q, g_kc, g_ks, g_kw, pe_k, pe_v,
              w_ck1, w_ck2, w_cv1, w_cv2, g_nsa_out, w_gk2, b_gk, g_gla_out, w_out,
              g_cross, g_mem, w_cq, w_ck, w_cv, g_cq, g_ck, w_co, g_ffn, w_gu, w_down):
    for l in range(DEPTH_2):
        x = hybrid_layer(x, mem, g_mix[l], w_in[l], b_nsa_gate[l], g_q[l], g_kc[l], g_ks[l],
                         g_kw[l], pe_k[l], pe_v[l], w_ck1[l], w_ck2[l], w_cv1[l], w_cv2[l],
                         g_nsa_out[l], w_gk2[l], b_gk[l], g_gla_out[l], w_out[l],
                         g_cross[l], g_mem[l], w_cq[l], w_ck[l], w_cv[l], g_cq[l], g_ck[l],
                         w_co[l], g_ffn[l], w_gu[l], w_down[l])
    return x


def setup_inputs(seed=0):
    out = dict(first_inputs(seed))
    for name, value in second_inputs(seed + 1).items():
        if name != "x":
            out[name + "_2"] = value
    return out


def reference(
    x, positions, conv_norm, conv_w_in, conv_dw, conv_dw_b, conv_ln_g, conv_ln_b, conv_w_out,
    hgrn_norm, hgrn_w_in, hgrn_lb_fwd, hgrn_lb_bwd, hgrn_o_norm, hgrn_w_out, diff_norm,
    diff_w_in, diff_q_norm, diff_k_norm, diff_lam_q1, diff_lam_k1, diff_lam_q2, diff_lam_k2,
    diff_sub_norm, diff_w_out, fnet_norm, fnet_w_in, fnet_group_w, fnet_w_out, mem_2, g_mix_2,
    w_in_2, b_nsa_gate_2, g_q_2, g_kc_2, g_ks_2, g_kw_2, pe_k_2, pe_v_2, w_ck1_2, w_ck2_2,
    w_cv1_2, w_cv2_2, g_nsa_out_2, w_gk2_2, b_gk_2, g_gla_out_2, w_out_2, g_cross_2, g_mem_2,
    w_cq_2, w_ck_2, w_cv_2, g_cq_2, g_ck_2, w_co_2, g_ffn_2, w_gu_2, w_down_2,
):
    x = first_block(
        x, positions, conv_norm, conv_w_in, conv_dw, conv_dw_b, conv_ln_g, conv_ln_b,
        conv_w_out, hgrn_norm, hgrn_w_in, hgrn_lb_fwd, hgrn_lb_bwd, hgrn_o_norm, hgrn_w_out,
        diff_norm, diff_w_in, diff_q_norm, diff_k_norm, diff_lam_q1, diff_lam_k1, diff_lam_q2,
        diff_lam_k2, diff_sub_norm, diff_w_out, fnet_norm, fnet_w_in, fnet_group_w, fnet_w_out,
    )
    return second_block(
        x, mem_2, g_mix_2, w_in_2, b_nsa_gate_2, g_q_2, g_kc_2, g_ks_2, g_kw_2, pe_k_2, pe_v_2,
        w_ck1_2, w_ck2_2, w_cv1_2, w_cv2_2, g_nsa_out_2, w_gk2_2, b_gk_2, g_gla_out_2, w_out_2,
        g_cross_2, g_mem_2, w_cq_2, w_ck_2, w_cv_2, g_cq_2, g_ck_2, w_co_2, g_ffn_2, w_gu_2,
        w_down_2,
    )


_drawn_inputs = setup_inputs


def setup_inputs(seed=0):
    import zlib

    import numpy as np

    out = dict(_drawn_inputs(seed))
    spreads = {}
    factors = {'conv_norm': 3.038,
     'conv_ln_g': 3.765,
     'conv_ln_b': 4.4,
     'hgrn_o_norm': 4.997,
     'b_nsa_gate_2': 3.002,
     'g_q_2': 3.324,
     'g_kc_2': 8.0,
     'g_ks_2': 6.338,
     'g_kw_2': 6.245,
     'g_nsa_out_2': 3.0,
     'b_gk_2': 4.192,
     'g_gla_out_2': 3.59,
     'g_cross_2': 8.0,
     'g_mem_2': 8.0,
     'g_cq_2': 8.0,
     'g_ck_2': 8.0,
     'g_ffn_2': 8.0}
    for name, (base, spread) in spreads.items():
        noise = np.random.default_rng([zlib.crc32(name.encode()), seed]).standard_normal(out[name].shape)
        drawn = base * np.exp(spread * noise) if base else spread * noise
        out[name] = jnp.asarray(drawn.astype(out[name].dtype))
    for name, factor in factors.items():
        out[name] = (out[name] * factor).astype(out[name].dtype)
    return out
```

```python
from contextlib import ExitStack

import concourse.bass as bass
from concourse import mybir
import numpy as np
import math

F32 = mybir.dt.float32
F32R = mybir.dt.float32r
ACT = mybir.ActivationFunctionType
ALU = mybir.AluOpType
AX_X = mybir.AxisListType.X

P = 128
T = 256
D = 2048
KT = D // P
GRP = 4
CW = KT * P
TAPS = 31
PAD = TAPS // 2
HEADS = 16
CH = 64
NCH = T // CH
NG = 2
EPS = 1e-6
BIG = 1e30
N_CMP, CMP_LEN, CMP_STRIDE = 15, 32, 16
DFF = 5632
FK = DFF // P
MEMH = 4
ATT_SCALE = 128 ** -0.5

C_CONV = 0
C_CONVO = C_CONV + 3 * KT
C_HG = C_CONVO + KT
C_HGO = C_HG + 5 * KT
C_MIXA = C_HGO + KT
C_MIXB = C_MIXA + 21
C_MEM = C_MIXB + 32
C_MIXO = C_MEM + 8
C_CQ = C_MIXO + KT
C_CO = C_CQ + MEMH
C_FF = C_CO + 4
FF_PARTS = [16, 16, 12]
C_END = C_FF + sum(2 * n + KT for n in FF_PARTS)

MIXA = ["kc0", "kc1", "vc0", "vc1", "K0", "ks0", "K1", "ks1", "K2", "vs0", "K3", "vs1",
        "V0", "kw0", "V1", "kw1", "V2", "vw0", "V3", "vw1", "gate"]

R_CONV = 0
R_CONVO = R_CONV + 3 * KT
R_HG = R_CONVO + KT
R_HGO = R_HG + 5 * KT
R_MIXA = R_HGO + KT
R_MIXB = R_MIXA + 13
R_MEM = R_MIXB + 32
R_MIXO = R_MEM + 8
R_CQ = R_MIXO + KT
R_FF = R_CQ + MEMH

H_CONV, H_CONVY, H_HG, H_HGY, H_MIX, H_MEM, H_MIXY, H_CROSS, H_CO, H_FF = [4 * n for n in range(9)] + [33]

V_NAMES = [("conv_norm", 16), ("dw", 16 * TAPS), ("dw_b", 16), ("ln_g", 16), ("ln_b", 16),
           ("hgrn_norm", 16), ("lbf0", 16), ("lbb0", 16), ("lbf1", 16), ("lbb1", 16), ("o_norm", 1),
           ("g_mix", 16), ("b_gate", 1), ("g_q", 1), ("g_kc", 1), ("g_ks", 1), ("g_kw", 1),
           ("g_nsa", 1), ("b_gk", 4), ("g_gla", 2), ("g_cross", 16), ("g_mem", 16), ("g_cq", 1),
           ("g_ck", 1), ("g_ffn", 16), ("pe_k", 32), ("pe_v", 32), ("ck2", 256), ("cv2", 256), ("gk2", 512)]
V_AT, n_ = {}, 0
for name_, w_ in V_NAMES:
    V_AT[name_] = n_
    n_ += w_
V_COLS = n_

K_NAMES = [("ident", 128), ("ones", 128), ("keep", 2 * T), ("tri", 4 * P), ("dist1", 2 * T),
           ("dist0", T), ("distc", 2 * 16), ("slope", 8), ("rowok", 1), ("eps", 1), ("lnsc", 1)]
K_AT, n_ = {}, 0
for name_, w_ in K_NAMES:
    K_AT[name_] = n_
    n_ += w_
K_COLS = n_


def make_constants():
    c = np.zeros((P, K_COLS), np.float32)

    def put(name, a):
        c[:, K_AT[name]:K_AT[name] + a.shape[1]] = a
    p = np.arange(P)
    t = np.arange(T)
    put("ident", np.eye(P))
    put("ones", np.ones((P, P)))
    put("keep", np.tile(np.concatenate([(t % CH != 0), (t % CH != CH - 1)]).astype(float), (P, 1)))
    same = (p[:, None] // CH) == (p[None, :] // CH)
    fwd = same & (p[:, None] <= p[None, :])
    bwd = same & (p[:, None] >= p[None, :])
    put("tri", np.concatenate([fwd, fwd, bwd, bwd], 1).astype(float))
    far = -1e30
    d1 = np.where(t[None, :] <= (P + p)[:, None], t[None, :] - (P + p)[:, None], far)
    d0 = np.where(p[None, :] <= p[:, None], p[None, :] - p[:, None], far)
    put("dist1", np.concatenate([d1, d1], 1))
    put("dist0", np.concatenate([d0, d0], 1))
    n = np.arange(N_CMP)
    for tile in range(2):
        tt = tile * P + p
        dc = np.where(tt[:, None] >= (n * CMP_STRIDE + CMP_LEN - 1)[None, :],
                      n[None, :] * CMP_STRIDE + 0.5 * (CMP_LEN - 1) - tt[:, None], far)
        c[:, K_AT["distc"] + 16 * tile:K_AT["distc"] + 16 * tile + N_CMP] = dc
    put("slope", np.tile(2.0 ** (-np.arange(1, 9)), (P, 1)))
    put("rowok", (p >= CMP_LEN - 1).astype(float)[:, None])
    put("eps", np.full((P, 1), EPS))
    put("lnsc", np.full((P, 1), math.log(ATT_SCALE)))
    return c


class At:

    def __init__(self, a, b=0, i=0):
        self.a, self.b, self.i = a, b, i

    def __add__(self, n):
        return At(self.a + n, self.b, self.i)

    def __sub__(self, n):
        return At(self.a - n, self.b, self.i)

    def times(self, n):
        return At(self.a * n, self.b * n, self.i)

    def slot(self, m):
        assert self.b % m == 0 or isinstance(self.i, int)
        return (self.a + (self.b * self.i if isinstance(self.i, int) else 0)) % m

    def turn(self, m):
        if isinstance(self.i, int):
            return At((self.a + self.b * self.i) // m)
        return At(self.a // m, self.b // m, self.i)

    @property
    def v(self):
        if self.b == 0:
            return self.a
        return self.i * self.b + self.a


def wait(eng, sem, at):
    v = at.v if isinstance(at, At) else at
    if isinstance(v, int) and v <= 0:
        return
    eng.wait_ge(sem, v)


class Steps:

    def __init__(self, eng, sem, per=0, i=0, base=0):
        self.eng, self.sem, self.per, self.i, self.base, self.n = eng, sem, per, i, base, 0

    def done(self, ins):
        ins.then_inc(self.sem, 1)
        self.n += 1
        return self.n

    def wait(self, n):
        wait(self.eng, self.sem, At(self.base + n, self.per, self.i))

    def link(self, ins):
        self.wait(self.done(ins))

    def end(self):
        assert not self.per or self.n == self.per, (self.n, self.per)


def build(nc, x_in, mem_in, stream, vectors, constants, out):
    with ExitStack() as ctx:
        def sb(name, shape, dt=F32):
            return ctx.enter_context(nc.sbuf_tensor(name, shape, dt))

        def sem(name):
            return ctx.enter_context(nc.semaphore(name))

        RAW = sb("RAW", [P, 2, CW])
        HI = sb("HI", [P, 4, CW], F32R)
        LO = sb("LO", [P, 4, CW], F32R)
        X = sb("X", [P, KT, T])
        HH = sb("HH", [P, KT, T], F32R)
        HL = sb("HL", [P, KT, T], F32R)
        VEC = sb("VEC", [P, V_COLS])
        CON = sb("CON", [P, K_COLS])
        SQ = sb("SQ", [P, 2, T])
        LR = sb("LR", [P, T])
        RR = sb("RR", [P, T])

        class Layout:
            def __init__(self, at):
                self.at = at

            def __call__(self, name, shape, dt=F32):
                t = nc.alloc_sbuf_tensor_at(name, shape, dt, offset=self.at)
                size = 4
                for s in shape[1:]:
                    size *= s
                self.at += -(-size // 32) * 32
                assert self.at <= nc.sbuf_usable_end, (name, self.at)
                return t

        WORK = -(-nc.sbuf_base // 32) * 32

        at = Layout(WORK)
        HN = at("HN", [P, 2, GRP, T])
        AFTER_HN = at.at
        CV = at("CV", [P, KT, T])
        SZ = at("SZ", [P, KT, T])
        VP = at("VP", [P, 2, T + 2 * PAD])
        SG = at("SG", [P, 2, T])
        CA = at("CA", [P, 2, T])
        SC = at("SC", [P, 2, T])
        MU = at("MU", [P, T])
        MM = at("MM", [P, T])
        VA = at("VA", [P, T])

        G = ctx.enter_context(nc.psum_tensor("G", [P, NG, 512], F32))
        A = [ctx.enter_context(nc.psum_tensor(f"A{n}", [P, 512], F32)) for n in range(6)]

        raw_ready = [sem(f"raw_ready{s}") for s in range(2)]
        hi_ready = sem("hi_ready")
        lo_ready = sem("lo_ready")
        mm_done = sem("mm_done")
        g_free = [sem(f"g_free{s}") for s in range(NG)]
        h_ready = sem("h_ready")
        s_in = sem("s_in")
        s_mem = sem("s_mem")
        s_out = sem("s_out")

        def con(name, a=0, b=None):
            w = dict(K_NAMES)[name]
            return CON[:, K_AT[name] + a:K_AT[name] + (w if b is None else b)]

        def vec(name, a=0, rows=P):
            if isinstance(a, At):
                a = a.v
            if isinstance(a, int):
                return VEC[0:rows, V_AT[name] + a:V_AT[name] + a + 1]
            return VEC[0:rows, bass.ds(a + V_AT[name], 1)]

        def tile(buf, at):
            return buf[:, at.v if isinstance(at, At) else at, :]

        IDENT, ONES, EPSC = con("ident"), con("ones"), con("eps")

        def split_hi(act, c):
            if isinstance(c.v, int) and c.v >= C_END:
                return
            act.wait_ge(raw_ready[c.slot(2)], (c.turn(2) + 1).times(16).v)
            wait(act, mm_done, c - 3)
            nc.scalar.activation(HI[:, c.slot(4), :], RAW[:, c.slot(2), :], ACT.Copy).then_inc(hi_ready, 1)

        def split_lo(dve, c):
            if isinstance(c.v, int) and c.v >= C_END:
                return
            wait(dve, hi_ready, c + 1)
            nc.vector.tensor_tensor(LO[:, c.slot(4), :], RAW[:, c.slot(2), :],
                                    HI[:, c.slot(4), :].bitcast(F32), ALU.subtract).then_inc(lo_ready, 1)

        def gemm(pe, c, r, h=None, kt=KT, operand=None):
            wait(pe, lo_ready, c + 1)
            wait(pe, g_free[r.slot(NG)], r.turn(NG))
            res = G[:, r.slot(NG), 0:T]
            high, low = operand or (HH, HL)
            for k in range(kt):
                if h is not None and k % GRP == 0:
                    pe.wait_ge(h_ready, h + k // GRP + 1)
                w = slice(k * P, (k + 1) * P)
                wh, wl = HI[:, c.slot(4), w], LO[:, c.slot(4), w]
                nc.tensor.matmul(res, wh, high[:, k, :], start=(k == 0), stop=False)
                nc.tensor.matmul(res, wh, low[:, k, :], start=False, stop=False)
                mm = nc.tensor.matmul(res, wl, high[:, k, :], start=False, stop=(k == kt - 1))
            mm.then_inc(mm_done, 1)

        def taken(eng, r):
            wait(eng, g_free[r.slot(NG)], r.turn(NG) + 1)

        def gres(r):
            return G[:, r.slot(NG), 0:T]

        n_sq, n_ss, n_ln, n_rr, n_hn, n_hh = (sem(f"n_{s}") for s in ("sq", "ss", "ln", "rr", "hn", "hh"))

        class Norm:

            made = 0

            def __init__(self, gain, fill, last_chunk, bank):
                self.gain, self.fill, self.last, self.bank = gain, fill, last_chunk, bank
                self.n = Norm.made
                Norm.made += 1

            def sq(self, k):
                return k + KT * self.n

            def hn(self, k):
                return k + KT // GRP * self.n

            def roots(self):
                return self.n - (self.n > 3)

            def root(self, act):
                act.wait_ge(n_ss, self.sq(KT))
                nc.scalar.activation(LR[:], A[self.bank][:, 0:T], ACT.Ln, bias=EPSC, scale=1.0 / D).then_inc(n_ln, 1)
                act.wait_ge(n_ln, self.roots() + 1)
                nc.scalar.activation(RR[:], LR[:], ACT.Exp, scale=-0.5).then_inc(n_rr, 1)

            def scale(self, dve):
                dve.wait_ge(n_rr, self.roots() + 1)
                wait(dve, mm_done, self.last + 1)
                for g in range(KT // GRP + 1):
                    if g < KT // GRP:
                        if g >= 2:
                            dve.wait_ge(h_ready, self.fill + g - 1)
                        for k in range(GRP):
                            ft = g * GRP + k
                            ins = nc.vector.scalar_tensor_tensor(
                                HN[:, g % 2, k, :], X[:, ft, :], vec(self.gain, ft), RR[:], ALU.mult, ALU.mult)
                        ins.then_inc(n_hn, 1)
                    if g >= 1:
                        lo_part(dve, n_hh, HN[:, (g - 1) % 2], g - 1, self.hn(0))

            def high(self, act):
                for g in range(KT // GRP):
                    act.wait_ge(n_hn, self.hn(g + 1))
                    nc.scalar.activation(HH[:, g * GRP:(g + 1) * GRP, :], HN[:, g % 2], ACT.Copy).then_inc(n_hh, 1)

        def lo_part(dve, hh, src, g, before=0):
            dve.wait_ge(hh, before + g + 1)
            nc.vector.tensor_tensor(HL[:, g * GRP:(g + 1) * GRP, :], src,
                                    HH[:, g * GRP:(g + 1) * GRP, :].bitcast(F32), ALU.subtract).then_inc(h_ready, 1)

        def squares_all(act, n):
            for ft in range(KT):
                wait(act, n_ss, n.sq(ft - 1))
                nc.scalar.activation(SQ[:, ft % 2, :], X[:, ft, :], ACT.Square).then_inc(n_sq, 1)

        def sums_all(pe, n):
            for ft in range(KT):
                sum_square(pe, n, At(ft))

        def sum_square(pe, n, ft):
            wait(pe, n_sq, ft + n.sq(1))
            f = ft.v
            nc.tensor.matmul(A[n.bank][:, 0:T], ONES, SQ[:, ft.slot(2), :], start=(isinstance(f, int) and f == 0),
                             stop=(isinstance(f, int) and f == KT - 1), skip_group_check=True).then_inc(n_ss, 1)

        class Project:

            def __init__(self, c0, r0, n, fill, kt=KT, operand=None, ready=0):
                self.c0, self.r0, self.n, self.fill, self.kt = c0, r0, n, fill, kt
                self.operand, self.ready = operand, ready
                self.ends = int(c0 + KT == C_END)

            def pe(self, pe):
                if self.operand:
                    pe.wait_ge(ff_lo, self.ready)

                def tiles(i, first):
                    for j in range(4):
                        ft = At(j, 4, i)
                        gemm(pe, At(self.c0 + j, 4, i), At(self.r0 + j, 4, i),
                             self.fill if first and j == 0 else None, self.kt, self.operand)
                        if self.n and not (first and j == 0):
                            sum_square(pe, self.n, ft - 1)
                tiles(0, True)
                with pe.Fori(1, 4) as i:
                    tiles(i, False)
                if self.n:
                    sum_square(pe, self.n, At(KT - 1))

            def act(self, act):
                def tiles(i):
                    for j in range(4):
                        r, ft = At(self.r0 + j, 4, i), At(j, 4, i)
                        split_hi(act, At(self.c0 + j + 2, 4, i))
                        if self.n:
                            taken(act, r)
                            wait(act, n_ss, ft + self.n.sq(-1))
                            nc.scalar.activation(SQ[:, ft.slot(2), :], tile(X, ft), ACT.Square).then_inc(n_sq, 1)
                tiles(0)
                with act.Fori(1, 4 - self.ends) as i:
                    tiles(i)
                if self.ends:
                    tiles(3)

            def dve(self, dve):
                def tiles(i):
                    for j in range(4):
                        c, r, ft = At(self.c0 + j, 4, i), At(self.r0 + j, 4, i), At(j, 4, i)
                        split_lo(dve, c + 2)
                        wait(dve, mm_done, c + 1)
                        nc.vector.tensor_tensor(tile(X, ft), tile(X, ft), gres(r), ALU.add).then_inc(g_free[r.slot(NG)], 1)
                with dve.Fori(0, 4 - self.ends) as i:
                    tiles(i)
                if self.ends:
                    tiles(3)

        cv_tap, cv_done, cv_sq, cv_sums, cv_ln, cv_rr, cv_mu, cv_t, cv_act, cv_hh, cv_pad = (
            sem(f"cv_{s}") for s in ("tap", "done", "sq", "sums", "ln", "rr", "mu", "t", "act", "hh", "pad"))
        norm_conv = Norm("conv_norm", H_CONV, -1, 5)
        norm_hg = Norm("hgrn_norm", H_HG, C_HG - 1, 5)
        conv_out = Project(C_CONVO, R_CONVO, norm_hg, H_CONVY)

        def conv_pe(pe):
            def tiles(i, first):
                for j in range(4):
                    for m in range(3):
                        n = 3 * j + m
                        gemm(pe, At(C_CONV + n, 12, i), At(R_CONV + n, 12, i), H_CONV if first and n == 0 else None)
                    if not (first and j == 0):
                        conv_sums(pe, At(j - 1, 4, i))
            tiles(0, True)
            with pe.Fori(1, 4) as i:
                tiles(i, False)
            conv_sums(pe, At(KT - 1))

        def conv_sums(pe, ft):
            f = ft.v if isinstance(ft.v, int) else 1
            wait(pe, cv_done, ft + 1)
            nc.tensor.matmul(A[4][:, 0:T], ONES, tile(CV, ft), start=(f == 0), stop=(f == KT - 1), skip_group_check=True)
            wait(pe, cv_sq, ft + 1)
            nc.tensor.matmul(A[3][:, 0:T], ONES, SC[:, ft.slot(2), :], start=(f == 0), stop=(f == KT - 1),
                             skip_group_check=True).then_inc(cv_sums, 1)

        def conv_act(act):
            def square(ft):
                wait(act, cv_done, ft + 1)
                wait(act, cv_sums, ft - 1)
                nc.scalar.activation(SC[:, ft.slot(2), :], tile(CV, ft), ACT.Square).then_inc(cv_sq, 1)

            def tiles(i, first):
                for j in range(4):
                    ft, c, r = At(j, 4, i), At(C_CONV + 3 * j, 12, i), At(R_CONV + 3 * j, 12, i)
                    split_hi(act, c + 2)
                    wait(act, mm_done, c + 1)
                    if not (first and j < 2):
                        taken(act, r - 5)
                    nc.scalar.activation(SG[:, ft.slot(2), :], gres(r), ACT.Sigmoid).then_inc(g_free[r.slot(NG)], 1)
                    split_hi(act, c + 3)
                    split_hi(act, c + 4)
                    if not (first and j == 0):
                        square(ft - 1)
                    wait(act, mm_done, c + 3)
                    nc.scalar.activation(tile(SZ, ft), gres(r + 2), ACT.Silu).then_inc(g_free[(r + 2).slot(NG)], 1)
            tiles(0, True)
            with act.Fori(1, 4) as i:
                tiles(i, False)
            square(At(KT - 1))
            act.wait_ge(cv_mu, 4)
            nc.scalar.activation(LR[:], VA[:], ACT.Ln, bias=EPSC).then_inc(cv_ln, 1)
            act.wait_ge(cv_ln, 1)
            nc.scalar.activation(RR[:], LR[:], ACT.Exp, scale=-0.5).then_inc(cv_rr, 1)
            for g in range(KT // GRP):
                for k in range(GRP):
                    ft = g * GRP + k
                    act.wait_ge(cv_t, 2 * g + 2)
                    ins = nc.scalar.activation(CV[:, ft, :], CV[:, ft, :], ACT.Silu, bias=vec("ln_b", ft), scale=vec("ln_g", ft))
                ins.then_inc(cv_act, 1)
            for g in range(KT // GRP):
                act.wait_ge(cv_pad, 3 + g)
                nc.scalar.activation(HH[:, g * GRP:(g + 1) * GRP, :], CV[:, g * GRP:(g + 1) * GRP, :], ACT.Copy).then_inc(cv_hh, 1)

        def conv_dve(dve):
            nc.vector.memset(VP[:, :, 0:PAD], 0.0).then_inc(cv_pad, 1)
            nc.vector.memset(VP[:, :, PAD + T:], 0.0).then_inc(cv_pad, 1)
            dve.wait_ge(cv_pad, 2)

            def tap(ft, k, acc, first):
                src = VP[:, ft.slot(2), k:k + T]
                w = vec("dw", ft.times(TAPS) + k)
                if first:
                    return nc.vector.tensor_scalar(acc, src, w, vec("dw_b", ft) if k == 0 else None, ALU.mult,
                                                   ALU.add if k == 0 else ALU.bypass)
                return nc.vector.scalar_tensor_tensor(acc, src, w, acc, ALU.mult, ALU.add)

            def tiles(i):
                st = Steps(dve, cv_tap, 4 * TAPS, i)
                for j in range(4):
                    ft, c, r = At(j, 4, i), At(C_CONV + 3 * j, 12, i), At(R_CONV + 3 * j, 12, i)
                    accs = [tile(CV, ft), CA[:, ft.slot(2), :]]

                    def taps(a, b):
                        for k in range(a, b):
                            if k >= 2:
                                st.wait(st.n - 1)
                            st.done(tap(ft, k, accs[k % 2], k < 2))
                    split_lo(dve, c + 2)
                    split_lo(dve, c + 3)
                    taken(dve, r)
                    wait(dve, mm_done, c + 2)
                    nc.vector.tensor_tensor(VP[:, ft.slot(2), PAD:PAD + T], gres(r + 1), SG[:, ft.slot(2), :],
                                            ALU.mult).then_inc(g_free[(r + 1).slot(NG)], 1)
                    taken(dve, r + 1)
                    taps(0, 16)
                    split_lo(dve, c + 4)
                    taps(16, TAPS)
                    st.wait(st.n)
                    nc.vector.tensor_tensor(tile(CV, ft), tile(CV, ft), CA[:, ft.slot(2), :], ALU.add).then_inc(cv_done, 1)
                st.end()
            with dve.Fori(0, 4) as i:
                tiles(i)
            dve.wait_ge(cv_sums, KT)
            nc.vector.tensor_scalar(MU[:], A[4][:, 0:T], 1.0 / D, None, ALU.mult).then_inc(cv_mu, 1)
            dve.wait_ge(cv_mu, 1)
            nc.vector.tensor_tensor(MM[:], MU[:], MU[:], ALU.mult).then_inc(cv_mu, 1)
            dve.wait_ge(cv_mu, 2)
            nc.vector.scalar_tensor_tensor(VA[:], A[3][:, 0:T], 1.0 / D, MM[:], ALU.mult, ALU.subtract).then_inc(cv_mu, 1)
            dve.wait_ge(cv_mu, 3)
            nc.vector.tensor_scalar(VA[:], VA[:], 0.0, None, ALU.max).then_inc(cv_mu, 1)
            dve.wait_ge(cv_rr, 1)

            def wide(v):
                return v.unsqueeze(1).broadcast_to([P, GRP, T])

            for g in range(KT // GRP):
                grp = CV[:, g * GRP:(g + 1) * GRP, :]
                nc.vector.tensor_tensor(grp, grp, wide(MU[:]), ALU.subtract).then_inc(cv_t, 1)
                dve.wait_ge(cv_t, 2 * g + 1)
                nc.vector.tensor_tensor(grp, grp, wide(RR[:]), ALU.mult).then_inc(cv_t, 1)
            for g in range(KT // GRP):
                grp = CV[:, g * GRP:(g + 1) * GRP, :]
                dve.wait_ge(cv_act, g + 1)
                nc.vector.tensor_tensor(grp, grp, SZ[:, g * GRP:(g + 1) * GRP, :], ALU.mult).then_inc(cv_pad, 1)
                lo_part(dve, cv_hh, grp, g)

        at = Layout(AFTER_HN)
        Y = at("Y", [P, KT, T])
        OML = at("OML", [P, 2, HEADS])
        OMN = at("OMN", [P, 2, HEADS])
        SA = at("SA", [P, 2, T])
        LF = at("LF", [P, 2, T])
        BC = at("BC", [P, 2, T])
        DB = at("DB", [P, 2, T])
        EQ = at("EQ", [P, 2, T])
        EK = at("EK", [P, 2, T])
        E2 = at("E2", [P, 2, NCH, 2])
        QC = at("QC", [P, T])
        QT = at("QT", [P, 2, T])
        KD = at("KD", [P, 2, T])
        VF = at("VF", [P, T])
        VT = at("VT", [P, 2, P])
        KX = at("KX", [P, 2, 2, P])
        SM = at("SM", [P, 2, 2, P])
        ST = at("ST", [P, 2, 3, P])
        SD = at("SD", [P, 2, P])
        SP_ = at("SP_", [P, 2, 3, P])
        SZH = at("SZH", [P, T])
        ZG = at("ZG", [P, T])
        OG = at("OG", [P, T])

        (hg_lb, hg_oml, hg_lf, hg_sc, hg_d, hg_exp, hg_qt, hg_kx, hg_vt, hg_tr, hg_s, hg_sm, hg_kv,
         hg_st, hg_stp, hg_o, hg_sq, hg_ss, hg_ln, hg_rr, hg_og, hg_y, hg_hh) = (
            sem(f"hg_{s}") for s in ("lb", "oml", "lf", "scan", "d", "exp", "qt", "kx", "vt", "tr", "s", "sm", "kv",
                                     "st", "stp", "o", "sq", "ss", "ln", "rr", "og", "y", "hh"))
        norm_mix = Norm("g_mix", H_MIX, C_MIXA - 1, 5)
        hgrn_out = Project(C_HGO, R_HGO, norm_mix, H_HGY)
        STEPS_ST = 15

        def order(d, s):
            return s if d == 0 else NCH - 1 - s

        def kv_product(d, s):
            n = {(0, 0): 0, (0, 2): 1, (1, 1): 2, (0, 1): 0, (1, 0): 1, (1, 2): 2}[d, s]
            return A[2 + order(d, s) % 2][:, n * P:(n + 1) * P]

        def mid(d):
            return CH // 2 - 1 if d == 0 else CH // 2

        def end(d):
            return CH - 1 if d == 0 else 0

        def head_chunk(h, m):
            return h.times(5) + (C_HG + m)

        def head_result(h, m):
            return h.times(5) + (R_HG + m)

        def hgrn_pe(pe):
            def kv(p):
                wait(pe, hg_kx, p + 1)
                wait(pe, hg_vt, p + 1)
                wait(pe, hg_st, p)
                for d in range(2):
                    for s in range(3):
                        c = order(d, s)
                        rows = slice((c % 2) * CH, (c % 2) * CH + CH)
                        mm = nc.tensor.matmul(kv_product(d, s), KX[rows, d, c // 2, :],
                                              VT[rows, c // 2, :], start=True, stop=True)
                mm.then_inc(hg_kv, 1)

            def output(p):
                wait(pe, hg_sm, p + 1)
                wait(pe, hg_st, p + 1)
                wait(pe, hg_og, p)
                for tt in range(2):
                    o = A[5][:, tt * P:(tt + 1) * P]
                    nc.tensor.matmul(o, VT[:, tt, :], SM[:, 0, tt, :], start=True, stop=False)
                    for d, s in [(d, s) for s in range(3) for d in range(2) if order(d, s + 1) // 2 == tt]:
                        c = order(d, s + 1)
                        nc.tensor.matmul(A[5][:, c * CH:(c + 1) * CH], SP_[:, d, s, :],
                                         QT[:, d, c * CH:(c + 1) * CH], start=False, stop=False)
                    mm = nc.tensor.matmul(o, VT[:, tt, :], SM[:, 1, tt, :], start=False, stop=True)
                mm.then_inc(hg_o, 1)

            def sums(p):
                wait(pe, hg_sq, p + 1)
                wait(pe, hg_vt, p + 1)
                nc.tensor.matmul(A[4][:, T:2 * T], ONES, SQ[:, 0, :], start=True, stop=True).then_inc(hg_ss, 1)

            def turn(h):
                taken(pe, head_result(h, 3))
                wait(pe, hg_ln, h)
                for tt in range(2):
                    nc.tensor.transpose(A[4][:, tt * P:(tt + 1) * P], VF[:, tt * P:(tt + 1) * P], IDENT)
                wait(pe, hg_qt, h + 1)
                wait(pe, hg_kx, h)
                for d in range(2):
                    for tt in range(2):
                        n = 2 * d + tt
                        tr = nc.tensor.transpose(A[1][:, n * P:(n + 1) * P], KD[:, d, tt * P:(tt + 1) * P], IDENT)
                tr.then_inc(hg_tr, 1)
                wait(pe, hg_sm, h)
                for d in range(2):
                    for tt in range(2):
                        n = 2 * d + tt
                        w = slice(tt * P, (tt + 1) * P)
                        mm = nc.tensor.matmul(A[0][:, n * P:(n + 1) * P], KD[:, d, w], QT[:, d, w], start=True, stop=True)
                mm.then_inc(hg_s, 1)

            def head(h, p, fill):
                gemm(pe, head_chunk(h, 0), head_result(h, 0), fill)
                if p:
                    kv(p)
                gemm(pe, head_chunk(h, 1), head_result(h, 1))
                gemm(pe, head_chunk(h, 2), head_result(h, 2))
                if p:
                    output(p)
                gemm(pe, head_chunk(h, 3), head_result(h, 3))
                if p:
                    sums(p)
                gemm(pe, head_chunk(h, 4), head_result(h, 4))
                turn(h)

            for j in range(4):
                head(At(j), At(j - 1) if j else None, None if j else H_HG)
            with pe.Fori(1, 4) as i:
                for j in range(4):
                    head(At(j, 4, i), At(j - 1, 4, i), None)
            last = At(HEADS - 1)
            kv(last)
            output(last)
            sums(last)

        def hgrn_act(act):
            def gate(p):
                r = head_result(p, 4)
                wait(act, mm_done, head_chunk(p, 4) + 1)
                taken(act, r - 5)
                nc.scalar.activation(SZH[:], gres(r), ACT.Sigmoid).then_inc(hg_sc, 1)

            def keys(p):
                wait(act, hg_tr, p + 1)
                wait(act, hg_kv, p)
                nc.scalar.activation(KX[:], A[1][:].rearrange("p (d t m) -> p d t m", d=2, t=2), ACT.Copy).then_inc(hg_kx, 1)

            def square(p):
                wait(act, hg_o, p + 1)
                wait(act, hg_ss, p)
                nc.scalar.activation(SQ[:, 0, :], A[5][:, 0:T], ACT.Square).then_inc(hg_sq, 1)

            def root(p):
                wait(act, hg_ss, p + 1)
                wait(act, hg_rr, p)
                nc.scalar.activation(LR[:], A[4][:, T:2 * T], ACT.Ln, bias=EPSC, scale=1.0 / P).then_inc(hg_ln, 1)
                wait(act, hg_ln, p + 1)
                wait(act, hg_og, p)
                nc.scalar.activation(RR[:], LR[:], ACT.Exp, scale=-0.5).then_inc(hg_rr, 1)

            def head(h, p):
                c, r = head_chunk(h, 0), head_result(h, 0)
                split_hi(act, c + 2)
                if p:
                    gate(p)
                    keys(p)
                for d in range(2):
                    split_hi(act, c + 3 + d)
                    wait(act, mm_done, c + 1 + d)
                    wait(act, hg_qt, h)
                    nc.scalar.activation(SA[:, d, :], gres(r + d), ACT.Sigmoid, scale=-1.0).then_inc(g_free[(r + d).slot(NG)], 1)
                split_hi(act, c + 5)
                wait(act, mm_done, c + 3)
                wait(act, hg_qt, h)
                nc.scalar.activation(QC[:], gres(r + 2), ACT.Copy).then_inc(g_free[(r + 2).slot(NG)], 1)
                for d in range(2):
                    taken(act, r + d)
                    wait(act, hg_d, h.times(4))
                    nc.scalar.activation(LF[:, d, :], SA[:, d, :], ACT.Ln, bias=1.0,
                                         scale=omn(d, h)).then_inc(hg_lf, 1)
                if p:
                    square(p)
                wait(act, hg_d, h.times(4) + 4)
                wait(act, hg_st, h)
                nc.scalar.activation(EQ[:], DB[:], ACT.Exp).then_inc(hg_exp, 1)
                nc.scalar.activation(EK[:], DB[:], ACT.Exp, scale=-1.0).then_inc(hg_exp, 1)
                for d in range(2):
                    src = BC[:, d, :].rearrange("p (c n) -> p c n", c=NCH)[:, :, (mid(d), end(d))[d]::CH // 2]
                    ins = nc.scalar.activation(E2[:, d, :, :], src, ACT.Exp)
                ins.then_inc(hg_exp, 1)
                split_hi(act, c + 6)
                wait(act, mm_done, c + 4)
                wait(act, hg_tr, h)
                nc.scalar.activation(VF[:], gres(r + 3), ACT.Copy).then_inc(g_free[(r + 3).slot(NG)], 1)
                if p:
                    root(p)

            def omn(d, h):
                v = h.v
                return OMN[:, d, v:v + 1] if isinstance(v, int) else OMN[:, d, bass.ds(v, 1)]

            act.wait_ge(hg_lb, 2)
            nc.scalar.activation(OML[:], OMN[:], ACT.Sigmoid).then_inc(hg_oml, 1)
            act.wait_ge(hg_oml, 2)
            for j in range(4):
                head(At(j), At(j - 1) if j else None)
            with act.Fori(1, 4) as i:
                for j in range(4):
                    head(At(j, 4, i), At(j - 1, 4, i))
            last = At(HEADS - 1)
            gate(last)
            keys(last)
            square(last)
            root(last)
            for g in range(KT // GRP):
                act.wait_ge(hg_y, HEADS)
                nc.scalar.activation(HH[:, g * GRP:(g + 1) * GRP, :], Y[:, g * GRP:(g + 1) * GRP, :], ACT.Copy).then_inc(hg_hh, 1)

        def hgrn_dve(dve):
            def values(p):
                wait(dve, hg_tr, p + 1)
                wait(dve, hg_o, p)
                nc.vector.tensor_copy(VT[:], A[4][:, 0:T].rearrange("p (t m) -> p t m", t=2)).then_inc(hg_vt, 1)

            def mask(p):
                wait(dve, hg_s, p + 1)
                nc.vector.scalar_tensor_tensor(SM[:].rearrange("p d t m -> p (d t m)"), A[0][:], BIG, con("tri"),
                                               ALU.min, ALU.mult).then_inc(hg_sm, 1)

            def gate(p):
                r = head_result(p, 4)
                wait(dve, hg_sc, p + 1)
                wait(dve, hg_y, p)
                nc.vector.tensor_tensor(ZG[:], gres(r), SZH[:], ALU.mult).then_inc(g_free[r.slot(NG)], 1)

            def states(p, st):
                wait(dve, hg_kv, p + 1)
                wait(dve, hg_exp, p.times(3) + 3)
                at_end = [EQ[:, d, :].rearrange("p (c n) -> p c n", c=NCH)[:, :, end(d)] for d in range(2)]
                done = {}
                n_mid = [0, 1]
                for s in range(3):
                    for d in range(2):
                        c = order(d, s)
                        e = at_end[d][:, c:c + 1]
                        if s == 0:
                            done[d] = st.done(nc.vector.tensor_scalar(ST[:, d, 0, :], kv_product(d, 0), e, None, ALU.mult))
                        else:
                            st.wait(done[d])
                            done[d] = st.done(nc.vector.tensor_scalar(SD[:, d, :], ST[:, d, s - 1, :],
                                                                      E2[:, d, c, 1 - n_mid[d]:2 - n_mid[d]], None, ALU.mult))
                    if s:
                        for d in range(2):
                            c = order(d, s)
                            st.wait(done[d])
                            done[d] = st.done(nc.vector.scalar_tensor_tensor(ST[:, d, s, :], kv_product(d, s),
                                                                             at_end[d][:, c:c + 1], SD[:, d, :], ALU.mult, ALU.add))
                    for d in range(2):
                        c = order(d, s + 1)
                        st.wait(done[d])
                        ins = nc.vector.tensor_scalar(SP_[:, d, s, :], ST[:, d, s, :],
                                                      E2[:, d, c, n_mid[d]:n_mid[d] + 1], None, ALU.mult)
                        if s == 2 and d == 1:
                            ins.then_inc(hg_st, 1)
                        else:
                            st.done(ins)

            def sums(h):
                for d in range(2):
                    wait(dve, hg_lf, h.times(2) + 1 + d)
                    wait(dve, hg_exp, h.times(3))
                    keep = con("keep", d * T, (d + 1) * T)
                    rev = (lambda v: v) if d == 0 else (lambda v: v[:, ::-1])
                    nc.vector.tensor_tensor_scan(rev(BC[:, d, :]), rev(keep), rev(LF[:, d, :]), 0.0, ALU.mult, ALU.add).then_inc(hg_d, 1)
                for d in range(2):
                    wait(dve, hg_d, h.times(4) + 1 + d)
                    b = BC[:, d, :].rearrange("p (c n) -> p c n", c=NCH)
                    m = b[:, :, mid(d):mid(d) + 1].broadcast_to([P, NCH, CH])
                    nc.vector.tensor_tensor(DB[:, d, :].rearrange("p (c n) -> p c n", c=NCH), b, m, ALU.subtract).then_inc(hg_d, 1)

            def decayed(h):
                r = head_result(h, 2)
                taken(dve, r)
                wait(dve, hg_exp, h.times(3) + 3)
                wait(dve, hg_o, h)
                wait(dve, hg_s, h)
                nc.vector.tensor_tensor(QT[:], QC[:].unsqueeze(1).broadcast_to([P, 2, T]), EQ[:], ALU.mult)
                for d in range(2):
                    v = h.v
                    one = OML[:, d, v:v + 1] if isinstance(v, int) else OML[:, d, bass.ds(v, 1)]
                    ins = nc.vector.scalar_tensor_tensor(KD[:, d, :], SA[:, d, :], one, EK[:, d, :], ALU.mult, ALU.mult)
                ins.then_inc(hg_qt, 1)

            def finish(p):
                wait(dve, hg_rr, p + 1)
                nc.vector.scalar_tensor_tensor(OG[:], A[5][:, 0:T], vec("o_norm"), RR[:], ALU.mult, ALU.mult).then_inc(hg_og, 1)
                wait(dve, hg_og, p + 1)
                taken(dve, head_result(p, 4))
                nc.vector.tensor_tensor(tile(Y, p), OG[:], ZG[:], ALU.mult).then_inc(hg_y, 1)

            def head(h, p, st):
                c = head_chunk(h, 0)
                split_lo(dve, c + 2)
                if p:
                    gate(p)
                    mask(p)
                    values(p)
                split_lo(dve, c + 3)
                if p:
                    states(p, st)
                split_lo(dve, c + 4)
                split_lo(dve, c + 5)
                sums(h)
                split_lo(dve, c + 6)
                decayed(h)
                if p:
                    finish(p)

            for d, n in enumerate(("lbf", "lbb")):
                a0, a1 = V_AT[n + "0"], V_AT[n + "1"]
                nc.vector.tensor_tensor(OMN[:, d, :], VEC[:, a0:a0 + HEADS], VEC[:, a1:a1 + HEADS], ALU.subtract).then_inc(hg_lb, 1)
            dve.wait_ge(hg_oml, 1)
            nc.vector.tensor_scalar(OMN[:], OML[:], -1.0, None, ALU.mult).then_inc(hg_oml, 1)
            st = Steps(dve, hg_stp)
            for j in range(4):
                head(At(j), At(j - 1) if j else None, st)
            with dve.Fori(1, 4) as i:
                st2 = Steps(dve, hg_stp, 4 * STEPS_ST, i, st.n - 4 * STEPS_ST)
                for j in range(4):
                    head(At(j, 4, i), At(j - 1, 4, i), st2)
                st2.end()
            last = At(HEADS - 1)
            gate(last)
            mask(last)
            values(last)
            states(last, Steps(dve, hg_stp, base=st.n + 3 * 4 * STEPS_ST))
            finish(last)
            for g in range(KT // GRP):
                lo_part(dve, hg_hh, Y[:, g * GRP:(g + 1) * GRP, :], g)

        at = Layout(AFTER_HN)
        YN = at("YN", [P, 8, T])
        OTH_AT = at.at
        OTH = at("OTH", [P, 24, T])
        AFTER_OTH = at.at
        KN = at("KN", [P, 4, T])
        VW = at("VW", [P, 4, 2, P])
        VC = at("VC", [P, 2, P])
        KC = at("KC", [P, 2 * N_CMP])
        KCR = at("KCR", [P, 2, 2 * N_CMP])
        GT = at("GT", [P, 2, 24])
        PTC = at("PTC", [P, T])
        QCN = at("QCN", [P, T])
        QN = at("QN", [P, T])
        LO2 = at("LO2", [P, T])
        RO = at("RO", [P, T])
        ON = at("ON", [P, T])
        MX = at("MX", [P, 2, 3])
        NM = at("NM", [P, 2, 3])
        SL = at("SL", [P, 2, 3])
        RC = at("RC", [P, 2, 3])
        CF = at("CF", [P, 2, 3])
        HS = at("HS", [P, 2, 2, 2 * N_CMP])
        at = Layout(nc.sbuf_usable_end // 32 * 32 - 2 * T * 4)
        AL = at("AL", [P, T])
        RM = at("RM", [P, T])
        at = Layout(OTH_AT)
        BLH = at("BLH", [P, 2, CMP_LEN, 2 * N_CMP], F32R)
        BLL = at("BLL", [P, 2, CMP_LEN, 2 * N_CMP], F32R)
        UC = at("UC", [P, 4, T])
        LK = UC
        BT = at("BT", [P, 2, CMP_LEN, N_CMP])
        assert at.at <= AFTER_OTH
        at = Layout(AFTER_HN)
        VF4 = at("VF4", [P, 4, T])
        GF = at("GF", [P, T])
        at = Layout(WORK)
        PB = at("PB", [P, 2, 528])
        PTS = at("PTS", [P, 384])
        PTW = at("PTW", [P, 384])
        assert at.at <= AFTER_HN

        (mx_uc, mx_bt, mx_bh, mx_bl, mx_cmp, mx_hs, mx_c2, mx_kc, mx_vc, mx_ksq, mx_kss, mx_kln, mx_krr, mx_kn, mx_vtr,
         mx_vw, mx_gf, mx_gtr, mx_gt, mx_zero, mx_mr) = (
            sem(f"mx_{s}") for s in ("uc", "bt", "bh", "bl", "cmp", "hs", "c2", "kc", "vc", "ksq", "kss", "kln", "krr", "kn",
                                     "vtr", "vw", "gf", "gtr", "gt", "zero", "mr"))
        norm_mem = Norm("g_mem", H_MEM, C_MEM - 1, 5)
        raw_tiles = {"ks0": (KN, 0), "ks1": (KN, 1), "kw0": (KN, 2), "kw1": (KN, 3), "vs0": (VF4, 0), "vs1": (VF4, 1),
                     "vw0": (VF4, 2), "vw1": (VF4, 3), "kc0": (UC, 0), "kc1": (UC, 1), "vc0": (UC, 2), "vc1": (UC, 3)}
        results = [n for n in MIXA if n[0] not in "KV"]

        def mixa_chunk(name):
            return At(C_MIXA + MIXA.index(name))

        def mixa_result(name):
            return At(R_MIXA + results.index(name))

        def mixa_pe(pe):
            for n, name in enumerate(MIXA):
                c = At(C_MIXA + n)
                if name[0] not in "KV":
                    gemm(pe, c, mixa_result(name), None if n else H_MIX)
                else:
                    kv, part = "KV".index(name[0]), int(name[1])
                    wait(pe, lo_ready, c + 1)
                    wait(pe, mx_bl, 2 * kv + 2)
                    for pos in range(8):
                        for m in range(2):
                            w = slice((2 * pos + m) * P, (2 * pos + m + 1) * P)
                            res, l = A[2 * kv + m][:, 0:2 * N_CMP], 8 * part + pos
                            nc.tensor.matmul(res, HI[:, c.slot(4), w], BLH[:, kv, l, :], start=(l == 0), stop=False)
                            nc.tensor.matmul(res, HI[:, c.slot(4), w], BLL[:, kv, l, :], start=False, stop=False)
                            mm = nc.tensor.matmul(res, LO[:, c.slot(4), w], BLH[:, kv, l, :], start=False, stop=(l == CMP_LEN - 1))
                    mm.then_inc(mm_done, 1)
                if name == "kc1":
                    sums_all(pe, norm_mem)
                if name == "V0":
                    pe.wait_ge(mx_hs, 2)
                    for m in range(2):
                        mm = nc.tensor.matmul(A[4][:, 0:2 * N_CMP], vecs("ck2", m * P, P), HS[:, 0, m, :], start=(m == 0), stop=(m == 1))
                    mm.then_inc(mx_c2, 1)
                if name == "V2":
                    pe.wait_ge(mx_ksq, 1)
                    nc.tensor.matmul(A[4][:, 0:2 * N_CMP], ONES, KCR[:, 1, :], start=True, stop=True).then_inc(mx_kss, 1)
                    for n4 in range(4):
                        pe.wait_ge(mx_ksq, 2 + n4)
                        mm = nc.tensor.matmul(A[n4 // 2][:, (n4 % 2) * T:(n4 % 2 + 1) * T], ONES, SQ[:, n4 % 2, :],
                                              start=True, stop=True).then_inc(mx_kss, 1)
            pe.wait_ge(mx_hs, 4)
            for head in range(2):
                for m in range(2):
                    mm = nc.tensor.matmul(A[5][0:N_CMP, head * P:(head + 1) * P], HS[:, 1, m, head * N_CMP:(head + 1) * N_CMP],
                                          vecs("cv2", m * P, P), start=(m == 0), stop=(m == 1))
            mm.then_inc(mx_c2, 1)
            taken(pe, mixa_result("vw1"))
            for n4 in range(4):
                for tt in range(2):
                    tr = nc.tensor.transpose(A[2 + n4 // 2][:, ((n4 % 2) * 2 + tt) * P:((n4 % 2) * 2 + tt + 1) * P],
                                             VF4[:, n4, tt * P:(tt + 1) * P], IDENT)
            tr.then_inc(mx_vtr, 1)
            pe.wait_ge(mx_gf, 1)
            pe.wait_ge(mx_kln, 1)
            for tt in range(2):
                tr = nc.tensor.transpose(A[4][:, 32 * tt:32 * tt + 24], GF[0:24, tt * P:(tt + 1) * P], IDENT[0:24, 0:24])
            tr.then_inc(mx_gtr, 1)

        def vecs(name, a, n, rows=slice(0, P)):
            return VEC[rows, V_AT[name] + a:V_AT[name] + a + n]

        def mixa_act(act):
            def windows(kv):
                for head in range(2):
                    n = 2 * kv + head
                    act.wait_ge(mx_bt, n + 1)
                    nc.scalar.activation(BLH[:, kv, :, head * N_CMP:(head + 1) * N_CMP], BT[:, head], ACT.Copy).then_inc(mx_bh, 1)

            for n, name in enumerate(MIXA):
                c = At(C_MIXA + n)
                split_hi(act, c + 2)
                if name in raw_tiles:
                    buf, k = raw_tiles[name]
                    wait(act, mm_done, c + 1)
                    r = mixa_result(name)
                    nc.scalar.activation(buf[:, k, :], gres(r), ACT.Copy).then_inc(g_free[r.slot(NG)], 1)
                if name == "kc1":
                    windows(0)
                    for ft in range(KT):
                        if ft % GRP == 0:
                            act.wait_ge(s_mem, 16 * (ft // GRP + 1))
                        wait(act, n_ss, norm_mem.sq(ft - 1))
                        nc.scalar.activation(SQ[:, ft % 2, :], HN[:, (ft // GRP) % 2, ft % GRP, :], ACT.Square).then_inc(n_sq, 1)
                    act.wait_ge(n_ss, norm_mem.sq(KT))
                    nc.scalar.activation(LR[:], A[5][:, 0:T], ACT.Ln, bias=EPSC, scale=1.0 / D).then_inc(mx_mr, 1)
                    act.wait_ge(mx_mr, 1)
                    nc.scalar.activation(RM[:], LR[:], ACT.Exp, scale=-0.5).then_inc(mx_mr, 1)
                if name == "vc1":
                    windows(1)
                if name in ("V0", "gate"):
                    kv = int(name == "gate")
                    wait(act, mm_done, mixa_chunk("KV"[kv] + "3") + 1)
                    for m in range(2):
                        nc.scalar.activation(HS[:, kv, m, :], A[2 * kv + m][:, 0:2 * N_CMP], ACT.Silu).then_inc(mx_hs, 1)
                if name == "V1":
                    act.wait_ge(mx_c2, 1)
                    nc.scalar.activation(KCR[:, 0, :], A[4][:, 0:2 * N_CMP], ACT.Copy).then_inc(mx_kc, 1)
                    act.wait_ge(mx_kc, 1)
                    nc.scalar.activation(KCR[:, 1, :], KCR[:, 0, :], ACT.Square).then_inc(mx_ksq, 1)
                if name == "kw1":
                    for n4, t in enumerate(("ks0", "ks1", "kw0", "kw1")):
                        taken(act, mixa_result(t))
                        wait(act, mx_kss, n4)
                        nc.scalar.activation(SQ[:, n4 % 2, :], KN[:, n4, :], ACT.Square).then_inc(mx_ksq, 1)
            r = mixa_result("gate")
            wait(act, mm_done, mixa_chunk("gate") + 1)
            nc.scalar.activation(GF[0:24, :], G[0:24, r.slot(NG), 0:T], ACT.Sigmoid, bias=vec("b_gate", 0, 24)).then_inc(mx_gf, 1)
            nc.scalar.activation(AL[32:48, :], G[32:48, r.slot(NG), 0:T], ACT.Copy).then_inc(g_free[r.slot(NG)], 1)
            act.wait_ge(mx_kss, 5)
            nc.scalar.activation(KCR[:, 1, :], A[4][:, 0:2 * N_CMP], ACT.Ln, bias=EPSC, scale=1.0 / P).then_inc(mx_kln, 1)
            for b in range(2):
                nc.scalar.activation(LK[:, 2 * b:2 * b + 2, :], A[b][:].rearrange("p (a t) -> p a t", a=2), ACT.Ln, bias=EPSC,
                                     scale=1.0 / P).then_inc(mx_kln, 1)
            act.wait_ge(mx_kln, 3)
            nc.scalar.activation(KCR[:, 1, :], KCR[:, 1, :], ACT.Exp, scale=-0.5).then_inc(mx_krr, 1)
            nc.scalar.activation(LK[:], LK[:], ACT.Exp, scale=-0.5).then_inc(mx_krr, 1)

        def mixa_dve(dve):
            nc.vector.memset(VC[:], 0.0).then_inc(mx_zero, 1)
            nc.vector.memset(PTC[:], 0.0).then_inc(mx_zero, 1)

            def windows(kv):
                for head in range(2):
                    n = 2 * kv + head
                    taken(dve, mixa_result("kv"[kv] + f"c{head}"))
                    wait(dve, mx_bl, n - 1)
                    u = UC[:, 2 * kv + head, :]
                    view = bass.AP(tensor=u.tensor, offset=u.offset, ap=[list(u.ap[0]), [1, CMP_LEN], [CMP_STRIDE, N_CMP]])
                    pe_ = vecs("pe_k" if kv == 0 else "pe_v", 0, CMP_LEN).unsqueeze(2).broadcast_to([P, CMP_LEN, N_CMP])
                    nc.vector.tensor_tensor(BT[:, head], view, pe_, ALU.add).then_inc(mx_bt, 1)
                    dve.wait_ge(mx_bh, n + 1)
                    dst = slice(head * N_CMP, (head + 1) * N_CMP)
                    nc.vector.tensor_tensor(BLL[:, kv, :, dst], BT[:, head], BLH[:, kv, :, dst].bitcast(F32), ALU.subtract).then_inc(mx_bl, 1)

            for n, name in enumerate(MIXA):
                split_lo(dve, At(C_MIXA + n + 2))
                if name == "kc1":
                    windows(0)
                if name == "vc1":
                    windows(1)
            dve.wait_ge(mx_c2, 2)
            nc.vector.tensor_copy(VC[0:N_CMP, :, :], A[5][0:N_CMP, 0:2 * P].rearrange("p (a m) -> p a m", a=2)).then_inc(mx_vc, 1)
            dve.wait_ge(mx_vtr, 1)
            for b in range(2):
                nc.vector.tensor_copy(VW[:, 2 * b:2 * b + 2, :, :].rearrange("p a t m -> p (a t m)"), A[2 + b][:]).then_inc(mx_vw, 1)
            dve.wait_ge(mx_gtr, 1)
            for tt in range(2):
                nc.vector.tensor_copy(GT[:, tt, :], A[4][:, 32 * tt:32 * tt + 24]).then_inc(mx_gt, 1)
            dve.wait_ge(mx_gt, 2)
            nc.vector.tensor_scalar(GT[:, 0, 0:24:3], GT[:, 0, 0:24:3], con("rowok"), None, ALU.mult).then_inc(mx_gt, 1)
            dve.wait_ge(mx_krr, 2)
            nc.vector.scalar_tensor_tensor(KC[:], KCR[:, 0, :], vec("g_kc"), KCR[:, 1, :], ALU.mult, ALU.mult).then_inc(mx_kn, 1)
            for n4 in range(4):
                nc.vector.scalar_tensor_tensor(KN[:, n4, :], KN[:, n4, :], vec("g_ks" if n4 < 2 else "g_kw"), LK[:, n4, :],
                                               ALU.mult, ALU.mult).then_inc(mx_kn, 1)

        def mem_pool(pool):
            pool.wait_ge(h_ready, H_MIX + 4)
            for g in range(KT // GRP):
                if g >= 2:
                    pool.wait_ge(n_sq, norm_mem.sq(GRP * (g - 1)))
                pool.dma_start(HN[:, g % 2], mem_in[:, g * GRP:(g + 1) * GRP, :]).then_inc(s_mem, 16)
                pool.wait_ge(s_mem, 16 * (g + 1))

        (ns_sqq, ns_ssq, ns_lq, ns_rq, ns_qn, ns_s, ns_st, ns_nm, ns_e, ns_p, ns_tr, ns_pta, ns_ptd, ns_o, ns_sqo, ns_sso,
         ns_lo, ns_ro, ns_y) = (
            sem(f"ns_{s}") for s in ("sqq", "ssq", "lq", "rq", "qn", "s", "st", "nm", "e", "p", "tr", "pta", "ptd", "o", "sqo",
                                     "sso", "lo", "ro", "y"))
        NS_STEPS = 6

        def mixb_chunk(j, m):
            return j.times(4) + (C_MIXB + m)

        def mixb_result(j, m):
            return j.times(4) + (R_MIXB + m)

        def mixb_pe(pe):
            def turn(p):
                wait(pe, ns_p, p + 1)
                wait(pe, ns_pta, p)
                wait(pe, ns_ptd, p)
                for b in range(2):
                    nc.tensor.transpose(A[2 + b][:, 0:P], PB[:, 0, b * P:(b + 1) * P], IDENT)
                    for tt in range(2):
                        nc.tensor.transpose(A[2 + b][:, (1 + tt) * P:(2 + tt) * P], PB[:, 1, b * T + tt * P:b * T + (tt + 1) * P], IDENT)
                    tr = nc.tensor.transpose(A[2 + b][0:N_CMP, 3 * P:4 * P], PB[:, b, 512:512 + N_CMP], IDENT)
                tr.then_inc(ns_tr, 1)

            def values(p, kvh):
                wait(pe, ns_pta, p + 1)
                wait(pe, ns_ptd, p + 1)
                wait(pe, ns_y, p)
                o, o1 = A[5][:, 0:T], A[5][:, P:T]
                nc.tensor.matmul(o, VW[:, kvh, 0, :], PTS[:, 0:T], start=True, stop=False)
                nc.tensor.matmul(o1, VW[:, kvh, 1, :], PTS[:, T:T + P], start=False, stop=False)
                nc.tensor.matmul(o1, VW[:, 2 + kvh, 1, :], PTW[:, T:T + P], start=False, stop=False)
                nc.tensor.matmul(o, VC[:, kvh, :], PTC[:], start=False, stop=False)
                nc.tensor.matmul(o, VW[:, 2 + kvh, 0, :], PTW[:, 0:T], start=False, stop=True).then_inc(ns_o, 1)

            def sum_q(j):
                wait(pe, ns_sqq, j + 1)
                wait(pe, ns_lo, j - 1)
                nc.tensor.matmul(A[4][:, 0:T], ONES, SQ[:, 0, :], start=True, stop=True).then_inc(ns_ssq, 1)

            def sum_o(p, j):
                wait(pe, ns_sqo, p + 1)
                wait(pe, ns_lq, j)
                nc.tensor.matmul(A[4][:, T:2 * T], ONES, SQ[:, 1, :], start=True, stop=True).then_inc(ns_sso, 1)

            def scores(j, kvh):
                wait(pe, ns_qn, j + 1)
                wait(pe, ns_nm, j)
                for tt in range(2):
                    q = QN[:, tt * P:(tt + 1) * P]
                    n = P * (tt + 1)
                    nc.tensor.matmul(A[tt][:, 0:n], q, KN[:, kvh, 0:n], start=True, stop=True)
                    nc.tensor.matmul(A[tt][:, n:2 * n], q, KN[:, 2 + kvh, 0:n], start=True, stop=True)
                    mm = nc.tensor.matmul(A[0][:, T + 16 * tt:T + 16 * tt + N_CMP], q, KC[:, kvh * N_CMP:(kvh + 1) * N_CMP],
                                          start=True, stop=True)
                mm.then_inc(ns_s, 1)

            def head(j, p, kvh, kvp):
                gemm(pe, mixb_chunk(j, 0), mixb_result(j, 0))
                if p:
                    turn(p)
                gemm(pe, mixb_chunk(j, 1), mixb_result(j, 1))
                if p:
                    values(p, kvp)
                sum_q(j)
                gemm(pe, mixb_chunk(j, 2), mixb_result(j, 2))
                if p:
                    sum_o(p, j + 1)
                scores(j, kvh)
                gemm(pe, mixb_chunk(j, 3), mixb_result(j, 3))

            pe.wait_ge(mx_kn, 5)
            pe.wait_ge(mx_vw, 2)
            pe.wait_ge(mx_vc, 1)
            pe.wait_ge(mx_gt, 2)
            for kvh in range(2):
                head(At(4 * kvh), At(3) if kvh else None, kvh, 0)
                with pe.Fori(4 * kvh + 1, 4 * kvh + 4) as i:
                    head(At(0, 1, i), At(-1, 1, i), kvh, kvh)
            turn(At(7))
            values(At(7), 1)
            sum_o(At(7), 8)

        def mixb_act(act):
            def other(j, m):
                r = mixb_result(j, m)
                wait(act, mm_done, mixb_chunk(j, m) + 1)
                nc.scalar.activation(tile(OTH, j.times(3) + (m - 1)), gres(r), ACT.Copy).then_inc(g_free[r.slot(NG)], 1)

            def turned(p):
                wait(act, ns_tr, p + 1)
                wait(act, ns_o, p)
                nc.scalar.activation(PTS[:], A[2][:, 0:384], ACT.Copy)
                nc.scalar.activation(PTC[0:N_CMP, 0:P], A[2][0:N_CMP, 384:512], ACT.Copy).then_inc(ns_pta, 1)

            def square_o(p):
                wait(act, ns_o, p + 1)
                nc.scalar.activation(SQ[:, 1, :], A[5][:, 0:T], ACT.Square).then_inc(ns_sqo, 1)

            def root(src, ln, lbuf, rr, rbuf, n, bias):
                nc.scalar.activation(lbuf, src, ACT.Ln, bias=EPSC, scale=1.0 / P).then_inc(ln, 1)
                wait(act, ln, n + 1)
                nc.scalar.activation(rbuf, lbuf, ACT.Exp, scale=-0.5, bias=bias).then_inc(rr, 1)

            def root_o(p):
                wait(act, ns_sso, p + 1)
                wait(act, ns_y, p)
                root(A[4][:, T:2 * T], ns_lo, LO2[:], ns_ro, RO[:], p, 0.0)

            def head(j, p):
                c = mixb_chunk(j, 0)
                r = mixb_result(j, 0)
                split_hi(act, c + 2)
                if p:
                    other(p, 3)
                split_hi(act, c + 3)
                wait(act, mm_done, c + 1)
                wait(act, ns_qn, j)
                nc.scalar.activation(QCN[:], gres(r), ACT.Copy).then_inc(g_free[r.slot(NG)], 1)
                taken(act, r)
                wait(act, ns_ssq, j)
                nc.scalar.activation(SQ[:, 0, :], QCN[:], ACT.Square).then_inc(ns_sqq, 1)
                if p:
                    turned(p)
                split_hi(act, c + 4)
                other(j, 1)
                wait(act, ns_ssq, j + 1)
                wait(act, ns_rq, j)
                root(A[4][:, 0:T], ns_lq, LR[:], ns_rq, RR[:], j, con("lnsc"))
                if p:
                    square_o(p)
                split_hi(act, c + 5)
                other(j, 2)
                if p:
                    root_o(p)
                wait(act, ns_nm, j + 1)
                wait(act, ns_p, j)
                for tt in range(2):
                    n = P * (tt + 1)
                    for b, w in enumerate((slice(512, 512 + N_CMP), slice(0, n), slice(n, 2 * n))):
                        e = nc.scalar.activation(PB[:, tt, w], PB[:, tt, w], ACT.Exp, bias=NM[:, tt, b:b + 1], accum_out=SL[:, tt, b:b + 1])
                e.then_inc(ns_e, 1)

            for kvh in range(2):
                head(At(4 * kvh), At(3) if kvh else None)
                with act.Fori(4 * kvh + 1, 4 * kvh + 4) as i:
                    head(At(0, 1, i), At(-1, 1, i))
            last = At(7)
            other(last, 3)
            turned(last)
            square_o(last)
            root_o(last)

        def mixb_dve(dve):
            def turned(p):
                wait(dve, ns_tr, p + 1)
                wait(dve, ns_o, p)
                nc.vector.tensor_copy(PTW[:], A[3][:, 0:384])
                nc.vector.tensor_copy(PTC[0:N_CMP, P:T], A[3][0:N_CMP, 384:512]).then_inc(ns_ptd, 1)

            def finish(p):
                wait(dve, ns_ro, p + 1)
                nc.vector.scalar_tensor_tensor(tile(YN, p), A[5][:, 0:T], vec("g_nsa"), RO[:], ALU.mult, ALU.mult).then_inc(ns_y, 1)

            def softmax(j, st):
                slope = con_at("slope", j)
                wait(dve, ns_s, j + 1)
                wait(dve, ns_tr, j)
                for tt in range(2):
                    n2 = 2 * P * (tt + 1)
                    nc.vector.scalar_tensor_tensor(PB[:, tt, 0:n2], con(f"dist{tt}"), slope, A[tt][:, 0:n2], ALU.mult, ALU.add)
                    k = st.done(nc.vector.scalar_tensor_tensor(PB[:, tt, 512:512 + N_CMP], con("distc", 16 * tt, 16 * tt + N_CMP), slope,
                                                               A[0][:, T + 16 * tt:T + 16 * tt + N_CMP], ALU.mult, ALU.add))
                st.wait(k)
                for tt in range(2):
                    n = P * (tt + 1)
                    nc.vector.tensor_reduce(MX[:, tt, 1:3], PB[:, tt, 0:2 * n].rearrange("p (b n) -> p b n", b=2), AX_X, ALU.max)
                    k = st.done(nc.vector.tensor_reduce(MX[:, tt, 0:1], PB[:, tt, 512:512 + N_CMP], AX_X, ALU.max))
                st.wait(k)
                nc.vector.tensor_scalar(NM[:], MX[:], -1.0, None, ALU.mult).then_inc(ns_nm, 1)

            def weigh(j, st):
                wait(dve, ns_e, j + 1)
                st.link(nc.vector.reciprocal(RC[:], SL[:]))
                v = j.v
                gates = GT[:, :, 3 * v:3 * v + 3] if isinstance(v, int) else GT[:, :, bass.ds(v * 3, 3)]
                st.link(nc.vector.tensor_tensor(CF[:], RC[:], gates, ALU.mult))
                for tt in range(2):
                    n = P * (tt + 1)
                    for b, w in enumerate((slice(512, 512 + N_CMP), slice(0, n), slice(n, 2 * n))):
                        ins = nc.vector.tensor_scalar(PB[:, tt, w], PB[:, tt, w], CF[:, tt, b:b + 1], None, ALU.mult)
                ins.then_inc(ns_p, 1)

            def head(j, p, st):
                c = mixb_chunk(j, 0)
                split_lo(dve, c + 2)
                split_lo(dve, c + 3)
                if p:
                    turned(p)
                split_lo(dve, c + 4)
                wait(dve, ns_rq, j + 1)
                wait(dve, ns_s, j)
                nc.vector.scalar_tensor_tensor(QN[:], QCN[:], vec("g_q"), RR[:], ALU.mult, ALU.mult).then_inc(ns_qn, 1)
                split_lo(dve, c + 5)
                if p:
                    finish(p)
                softmax(j, st)
                weigh(j, st)
                st.end()

            dve.wait_ge(mx_gt, 3)
            for kvh in range(2):
                head(At(4 * kvh), At(3) if kvh else None, Steps(dve, ns_st, 0, 0, 4 * kvh * NS_STEPS))
                with dve.Fori(4 * kvh + 1, 4 * kvh + 4) as i:
                    head(At(0, 1, i), At(-1, 1, i), Steps(dve, ns_st, NS_STEPS, i))
            turned(At(7))
            finish(At(7))

        def con_at(name, a):
            v = a.v
            return con(name, v, v + 1) if isinstance(v, int) else CON[:, bass.ds(v + K_AT[name], 1)]

        at = Layout(AFTER_OTH)
        GQT = at("GQT", [P, 2, T])
        GA = at("GA", [P, T])
        GL = RM
        GB = at("GB", [P, T])
        GD = at("GD", [P, T])
        GE = at("GE", [P, T])
        GM = at("GM", [P, 2, NCH, 3])
        GKD = at("GKD", [P, T])
        GKX = at("GKX", [P, 2, P])
        GVT = at("GVT", [P, 2, 2, P])
        GSM = at("GSM", [P, 2, T])
        GST = at("GST", [P, 2 * P])
        GSP = at("GSP", [P, 3, 2 * P])
        GO = at("GO", [P, 2, T])
        GSD = GO[:, 0, :]
        assert at.at <= nc.sbuf_usable_end // 32 * 32 - 2 * T * 4, at.at

        (gl_gk, gl_t, gl_ab, gl_ex, gl_ln, gl_la, gl_sc, gl_db, gl_exp, gl_ek, gl_qt, gl_tr, gl_s, gl_kx, gl_vt, gl_sm, gl_kv, gl_step,
         gl_st, gl_o, gl_sq, gl_ss, gl_lr, gl_rr, gl_og, gl_y, gl_r, mm_h, mk_sq, mk_ss, mk_ln, mk_rr, mk_ck, mk_tr, mk_cv, my_hh, gl_zero) = (
            sem(s) for s in ("gl_gk gl_t gl_ab gl_ex gl_ln gl_la gl_sc gl_db gl_exp gl_ek gl_qt gl_tr gl_s gl_kx gl_vt gl_sm gl_kv gl_step "
                             "gl_st gl_o gl_sq gl_ss gl_lr gl_rr gl_og gl_y gl_r mm_h mk_sq mk_ss mk_ln mk_rr mk_ck mk_tr mk_cv my_hh gl_zero").split())
        norm_cross = Norm("g_cross", H_CROSS, C_CQ - 1, 5)
        mix_out = Project(C_MIXO, R_MIXO, norm_cross, H_MIXY)
        CK = OTH[:, 0:4, :]
        CVR = OTH[:, 4:8, :]
        CVT = OTH[:, 8:12, :].rearrange("p h (t m) -> p h t m", t=2)
        CL = OTH[:, 12:16, :]

        def gla_product(s):
            return A[3][:, (s // 2) * T:(s // 2 + 1) * T] if s % 2 == 0 else A[4][:, T:2 * T]

        def gla_pe(pe):
            def gate(h):
                wait(pe, gl_t, h)
                if h:
                    wait(pe, gl_st, h)
                nc.tensor.matmul(A[4][:, 0:T], vecs("gk2", h * P, P, slice(32, 48)), AL[32:48, :], start=True, stop=True).then_inc(gl_gk, 1)

            def turn(h):
                wait(pe, gl_qt, h + 1)
                wait(pe, gl_rr, h - 1)
                for tt in range(2):
                    w = slice(tt * P, (tt + 1) * P)
                    nc.tensor.transpose(A[1][:, w], GKD[:, w], IDENT)
                    for m in range(2):
                        tr = nc.tensor.transpose(A[2][:, (2 * tt + m) * P:(2 * tt + m + 1) * P], OTH[:, 8 + 2 * h + m, w], IDENT)
                tr.then_inc(gl_tr, 1)
                for tt in range(2):
                    w = slice(tt * P, (tt + 1) * P)
                    mm = nc.tensor.matmul(A[0][:, w], GKD[:, w], GQT[:, h % 2, w], start=True, stop=True)
                mm.then_inc(gl_s, 1)

            def kv(h):
                wait(pe, gl_kx, h + 1)
                wait(pe, gl_vt, h + 1)
                wait(pe, gl_t, h + 1)
                for s in range(3):
                    rows = slice((s % 2) * CH, (s % 2) * CH + CH)
                    mm = nc.tensor.matmul(gla_product(s), GKX[rows, s // 2, :], GVT[rows, s // 2, :, :].rearrange("p m n -> p (m n)"),
                                          start=True, stop=True)
                mm.then_inc(gl_kv, 1)

            def output(h):
                wait(pe, gl_sm, h + 1)
                wait(pe, gl_st, h + 1)
                wait(pe, gl_og, h)
                for m in range(2):
                    o = A[5][:, m * T:(m + 1) * T]
                    nc.tensor.matmul(o, GVT[:, 0, m, :], GSM[:, 0, :], start=True, stop=False)
                    for c in range(1, NCH):
                        nc.tensor.matmul(A[5][:, m * T + c * CH:m * T + (c + 1) * CH], GSP[:, c - 1, m * P:(m + 1) * P],
                                         GQT[:, h % 2, c * CH:(c + 1) * CH], start=False, stop=False)
                    mm = nc.tensor.matmul(o, GVT[:, 1, m, :], GSM[:, 1, :], start=False, stop=True)
                mm.then_inc(gl_o, 1)

            def sums(h):
                wait(pe, gl_sq, h + 1)
                wait(pe, gl_kx, min(h + 2, MEMH))
                for m in range(2):
                    mm = nc.tensor.matmul(A[1][:, T:2 * T], ONES, SQ[:, m, :], start=(m == 0), stop=(m == 1))
                mm.then_inc(gl_ss, 1)

            pe.wait_ge(ns_lo, 8)
            gate(0)
            for h in range(MEMH):
                gemm(pe, At(C_MEM + 2 * h), At(R_MEM + 2 * h), None if h else H_MEM)
                if h:
                    output(h - 1)
                turn(h)
                if h:
                    sums(h - 1)
                gemm(pe, At(C_MEM + 2 * h + 1), At(R_MEM + 2 * h + 1))
                kv(h)
                if h + 1 < MEMH:
                    gate(h + 1)
            output(MEMH - 1)
            sums(MEMH - 1)
            for h in range(MEMH):
                wait(pe, mk_sq, h + 1)
                if h == 0:
                    wait(pe, gl_rr, MEMH)
                nc.tensor.matmul(A[h // 2][:, (h % 2) * T:(h % 2 + 1) * T], ONES, SQ[:, h % 2, :], start=True, stop=True).then_inc(mk_ss, 1)
            for h in range(MEMH):
                for tt in range(2):
                    tr = nc.tensor.transpose(A[2 + h // 2][:, ((h % 2) * 2 + tt) * P:((h % 2) * 2 + tt + 1) * P],
                                             CVR[:, h, tt * P:(tt + 1) * P], IDENT)
            tr.then_inc(mk_tr, 1)

        def gla_act(act):
            def gates(h):
                wait(act, gl_t, h + 1)
                wait(act, gl_la, h)
                nc.scalar.activation(GL[:], GA[:], ACT.Abs).then_inc(gl_ab, 1)
                wait(act, gl_ab, h + 1)
                nc.scalar.activation(GL[:], GL[:], ACT.Exp, scale=-1.0).then_inc(gl_ex, 1)
                wait(act, gl_ex, h + 1)
                nc.scalar.activation(GL[:], GL[:], ACT.Ln, bias=1.0).then_inc(gl_ln, 1)

            def decays(h):
                wait(act, gl_db, h + 1)
                wait(act, gl_st, h - 1)
                b = GB[:].rearrange("p (c n) -> p c n", c=NCH)
                d = GD[:].rearrange("p (c n) -> p c n", c=NCH)
                nc.scalar.activation(GE[:], GD[:], ACT.Exp, scale=1.0 / 16)
                nc.scalar.activation(GM[:, h % 2, :, 0:2], b[:, :, CH // 2 - 1::CH // 2], ACT.Exp, scale=1.0 / 16)
                nc.scalar.activation(GM[:, h % 2, :, 2:3], d[:, :, CH - 1:CH], ACT.Exp, scale=1.0 / 16).then_inc(gl_exp, 1)
                wait(act, gl_exp, h + 1)
                nc.scalar.activation(GD[:], GD[:], ACT.Exp, scale=-1.0 / 16).then_inc(gl_ek, 1)

            def keep(h, m):
                r = At(R_MEM + 2 * h + m)
                wait(act, mm_done, C_MEM + 2 * h + m + 1)
                wait(act, gl_qt, h + 1)
                nc.scalar.activation(OTH[:, 4 * m + h, :], gres(r), ACT.Copy).then_inc(g_free[r.slot(NG)], 1)

            def square(h):
                wait(act, gl_o, h + 1)
                wait(act, gl_ss, h)
                nc.scalar.activation(SQ[:], A[5][:].rearrange("p (m t) -> p m t", m=2), ACT.Square).then_inc(gl_sq, 1)

            def root(h):
                wait(act, gl_ss, h + 1)
                wait(act, gl_og, h)
                nc.scalar.activation(LR[:], A[1][:, T:2 * T], ACT.Ln, bias=EPSC, scale=1.0 / T).then_inc(gl_lr, 1)
                wait(act, gl_lr, h + 1)
                nc.scalar.activation(RR[:], LR[:], ACT.Exp, scale=-0.5).then_inc(gl_rr, 1)

            taken(act, mixb_result(At(7), 3))
            nc.scalar.activation(OTH[:, 16:24, :], OTH[:, 16:24, :], ACT.Silu).then_inc(gl_r, 1)
            for g in range(KT // GRP):
                act.wait_ge(n_hn, norm_mem.hn(g + 1))
                nc.scalar.activation(HH[:, g * GRP:(g + 1) * GRP, :], HN[:, g % 2], ACT.Copy).then_inc(n_hh, 1)
            gates(0)
            decays(0)
            for h in range(MEMH):
                split_hi(act, At(C_MEM + 2 * h + 2))
                keep(h, 0)
                wait(act, gl_tr, h + 1)
                nc.scalar.activation(GVT[:], A[2][:].rearrange("p (t m n) -> p t m n", t=2, m=2), ACT.Copy).then_inc(gl_vt, 1)
                if h:
                    square(h - 1)
                split_hi(act, At(C_MEM + 2 * h + 3))
                keep(h, 1)
                if h:
                    root(h - 1)
                if h + 1 < MEMH:
                    gates(h + 1)
                    decays(h + 1)
            square(MEMH - 1)
            root(MEMH - 1)
            for h in range(MEMH):
                taken(act, At(R_MEM + 2 * h))
                wait(act, mk_ss, h - 1)
                nc.scalar.activation(SQ[:, h % 2, :], CK[:, h, :], ACT.Square).then_inc(mk_sq, 1)
            wait(act, mk_ss, MEMH)
            for b in range(2):
                nc.scalar.activation(CL[:, 2 * b:2 * b + 2, :], A[b][:].rearrange("p (a t) -> p a t", a=2), ACT.Ln, bias=EPSC,
                                     scale=1.0 / P).then_inc(mk_ln, 1)
            act.wait_ge(mk_ln, 2)
            nc.scalar.activation(CL, CL, ACT.Exp, scale=-0.5).then_inc(mk_rr, 1)
            for g in range(KT // GRP):
                if g == 2:
                    act.wait_ge(gl_y, 2 * MEMH)
                nc.scalar.activation(HH[:, g * GRP:(g + 1) * GRP, :], mix_source(g), ACT.Copy).then_inc(my_hh, 1)

        def mix_source(g):
            return YN[:, g * GRP:(g + 1) * GRP, :] if g < 2 else OTH[:, 8 + g * GRP:8 + (g + 1) * GRP, :]

        def gla_dve(dve):
            def gates(h):
                wait(dve, gl_gk, h + 1)
                wait(dve, gl_sc, h)
                nc.vector.tensor_scalar(GA[:], A[4][:, 0:T], vec("b_gk", h), None, ALU.add).then_inc(gl_t, 1)

            def decays(h):
                wait(dve, gl_ln, h + 1)
                nc.vector.scalar_tensor_tensor(GA[:], GA[:], 0.0, GL[:], ALU.min, ALU.subtract).then_inc(gl_la, 1)
                wait(dve, gl_la, h + 1)
                wait(dve, gl_exp, h)
                nc.vector.tensor_tensor_scan(GB[:], con("keep", 0, T), GA[:], 0.0, ALU.mult, ALU.add).then_inc(gl_sc, 1)
                wait(dve, gl_sc, h + 1)
                wait(dve, gl_qt, h)
                b = GB[:].rearrange("p (c n) -> p c n", c=NCH)
                nc.vector.tensor_tensor(GD[:].rearrange("p (c n) -> p c n", c=NCH), b,
                                        b[:, :, CH // 2 - 1:CH // 2].broadcast_to([P, NCH, CH]), ALU.subtract).then_inc(gl_db, 1)

            def decayed(h):
                wait(dve, gl_ek, h + 1)
                wait(dve, gl_o, h - 1)
                wait(dve, gl_s, h)
                nc.vector.scalar_tensor_tensor(GQT[:, h % 2, :], OTH[:, h, :], ATT_SCALE, GE[:], ALU.mult, ALU.mult)
                nc.vector.tensor_tensor(GKD[:], OTH[:, 4 + h, :], GD[:], ALU.mult).then_inc(gl_qt, 1)

            def turned(h):
                wait(dve, gl_tr, h + 1)
                nc.vector.tensor_copy(GKX[:], A[1][:, 0:T].rearrange("p (t m) -> p t m", t=2)).then_inc(gl_kx, 1)
                wait(dve, gl_s, h + 1)
                wait(dve, gl_o, h)
                for tt in range(2):
                    w = slice(tt * P, (tt + 1) * P)
                    ins = nc.vector.scalar_tensor_tensor(GSM[:, tt, w], A[0][:, w], BIG, con("tri", tt * P, (tt + 1) * P), ALU.min, ALU.mult)
                ins.then_inc(gl_sm, 1)

            def states(h, st):
                wait(dve, gl_kv, h + 1)
                wait(dve, gl_o, h)
                wait(dve, gl_y, 2 * (h - 1))
                e = GM[:, h % 2]
                for s in range(3):
                    if s == 0:
                        st.link(nc.vector.tensor_scalar(GST[:], gla_product(0), e[:, 0, 2:3], None, ALU.mult))
                    else:
                        st.link(nc.vector.tensor_scalar(GSD, GST[:], e[:, s, 1:2], None, ALU.mult))
                        st.link(nc.vector.scalar_tensor_tensor(GST[:], gla_product(s), e[:, s, 2:3], GSD, ALU.mult, ALU.add))
                    ins = nc.vector.tensor_scalar(GSP[:, s, :], GST[:], e[:, s + 1, 0:1], None, ALU.mult)
                    if s == 2:
                        ins.then_inc(gl_st, 1)
                    else:
                        st.link(ins)

            def finish(h):
                wait(dve, gl_rr, h + 1)
                wait(dve, gl_y, 2 * h)
                for m in range(2):
                    ins = nc.vector.scalar_tensor_tensor(GO[:, m, :], A[5][:, m * T:(m + 1) * T], vec("g_gla", m), RR[:], ALU.mult, ALU.mult)
                ins.then_inc(gl_og, 1)
                wait(dve, gl_og, h + 1)
                for m in range(2):
                    r = OTH[:, 16 + 2 * h + m, :]
                    nc.vector.tensor_tensor(r, r, GO[:, m, :], ALU.mult).then_inc(gl_y, 1)

            for g in range(KT // GRP + 1):
                if g < KT // GRP:
                    dve.wait_ge(s_mem, 16 * (KT // GRP + g + 1))
                    for k in range(GRP):
                        ins = nc.vector.scalar_tensor_tensor(HN[:, g % 2, k, :], HN[:, g % 2, k, :], vec("g_mem", g * GRP + k), RM[:],
                                                             ALU.mult, ALU.mult)
                    ins.then_inc(n_hn, 1)
                if g >= 1:
                    lo_part(dve, n_hh, HN[:, (g - 1) % 2], g - 1, norm_mem.hn(0))
            for tt in range(2):
                nc.vector.memset(GSM[:, tt, (1 - tt) * P:(2 - tt) * P], 0.0).then_inc(gl_zero, 1)
            dve.wait_ge(gl_zero, 2)
            st = Steps(dve, gl_step)
            gates(0)
            decays(0)
            decayed(0)
            dve.wait_ge(gl_r, 1)
            for h in range(MEMH):
                split_lo(dve, At(C_MEM + 2 * h + 2))
                turned(h)
                split_lo(dve, At(C_MEM + 2 * h + 3))
                states(h, st)
                if h:
                    finish(h - 1)
                if h + 1 < MEMH:
                    gates(h + 1)
                    decays(h + 1)
                    decayed(h + 1)
            finish(MEMH - 1)
            dve.wait_ge(mk_tr, 1)
            for b in range(2):
                nc.vector.tensor_copy(CVT[:, 2 * b:2 * b + 2, :, :].rearrange("p a t m -> p (a t m)"), A[2 + b][:]).then_inc(mk_cv, 1)
            for g in range(KT // GRP):
                lo_part(dve, my_hh, mix_source(g), g)
            dve.wait_ge(mk_rr, 1)
            for h in range(MEMH):
                nc.vector.scalar_tensor_tensor(CK[:, h, :], CK[:, h, :], vec("g_ck"), CL[:, h, :], ALU.mult, ALU.mult).then_inc(mk_ck, 1)

        def mem_again_pool(pool):
            for g in range(KT // GRP):
                if g == 0:
                    pool.wait_ge(ns_o, 8)
                    pool.wait_ge(mm_done, C_MEM)
                if g >= 2:
                    pool.wait_ge(h_ready, H_MEM + g - 1)
                pool.dma_start(HN[:, g % 2], mem_in[:, g * GRP:(g + 1) * GRP, :]).then_inc(s_mem, 16)
                pool.wait_ge(s_mem, 16 * (KT // GRP + g + 1))

        at = Layout(AFTER_HN)
        QX = at("QX", [P, MEMH, T])
        LX = at("LX", [P, MEMH, T])
        at = Layout(AFTER_OTH)
        PX = at("PX", [P, 2, 2, T])
        PXT = at("PXT", [P, 2, 2, T])
        MX2 = at("MX2", [P, 2, 2])
        NX = at("NX", [P, 2, 2])
        SX = at("SX", [P, 2, 2])
        RX = at("RX", [P, 2, 2])
        (cr_sq, cr_ss, cr_ln, cr_rr, cr_qn, cr_s, cr_mx, cr_nx, cr_e, cr_rx, cr_p, cr_tr, cr_pt, cr_o, cr_hh, cr_x) = (
            sem(f"cr_{s}") for s in "sq ss ln rr qn s mx nx e rx p tr pt o hh x".split())
        norm_ff = Norm("g_ffn", H_FF, C_FF - 1, 0)

        def cross_pe(pe):
            def scores(h):
                wait(pe, cr_qn, h + 1)
                wait(pe, cr_e, h - 1)
                for tt in range(2):
                    mm = nc.tensor.matmul(A[2 + h % 2][:, tt * T:(tt + 1) * T], QX[:, h, tt * P:(tt + 1) * P], CK[:, h, :], start=True, stop=True)
                mm.then_inc(cr_s, 1)

            def turn(h):
                wait(pe, cr_p, h + 1)
                wait(pe, cr_pt, h - 1)
                for tt in range(2):
                    for mt in range(2):
                        tr = nc.tensor.transpose(A[4 + h % 2][:, mt * T + tt * P:mt * T + (tt + 1) * P], PX[:, h % 2, tt, mt * P:(mt + 1) * P], IDENT)
                tr.then_inc(cr_tr, 1)

            def values(h):
                wait(pe, cr_pt, h + 1)
                for mt in range(2):
                    mm = nc.tensor.matmul(A[h // 2][:, (h % 2) * T:(h % 2 + 1) * T], CVT[:, h, mt, :], PXT[:, h % 2, mt, :],
                                          start=(mt == 0), stop=(mt == 1))
                mm.then_inc(cr_o, 1)

            def sums(h):
                wait(pe, cr_sq, h + 1)
                nc.tensor.matmul(A[h // 2][:, (h % 2) * T:(h % 2 + 1) * T], ONES, SQ[:, h % 2, :], start=True, stop=True).then_inc(cr_ss, 1)

            for h in range(MEMH):
                gemm(pe, At(C_CQ + h), At(R_CQ + h), None if h else H_CROSS)
                if h:
                    sums(h - 1)
            sums(MEMH - 1)
            pe.wait_ge(mk_ck, MEMH)
            scores(0)
            scores(1)
            for h in range(MEMH):
                turn(h)
                if h + 2 < MEMH:
                    scores(h + 2)
                values(h)
            for cc in range(4):
                c = At(C_CO + cc)
                wait(pe, lo_ready, c + 1)
                if cc == 0:
                    pe.wait_ge(h_ready, H_CO + 1)
                wait(pe, cr_x, 2 * (cc - 1))
                for f in range(4):
                    res = A[2 + 2 * (cc % 2) + f // 2][:, (f % 2) * T:(f % 2 + 1) * T]
                    for k in range(4):
                        w = slice((f * 4 + k) * P, (f * 4 + k + 1) * P)
                        nc.tensor.matmul(res, HI[:, c.slot(4), w], HH[:, k, :], start=(k == 0), stop=False)
                        nc.tensor.matmul(res, HI[:, c.slot(4), w], HL[:, k, :], start=False, stop=False)
                        mm = nc.tensor.matmul(res, LO[:, c.slot(4), w], HH[:, k, :], start=False, stop=(k == 3))
                mm.then_inc(mm_done, 1)
                if cc:
                    for f in range(4):
                        sum_square(pe, norm_ff, At(4 * (cc - 1) + f))
            for f in range(4):
                sum_square(pe, norm_ff, At(12 + f))

        def cross_act(act):
            for h in range(MEMH):
                r = At(R_CQ + h)
                split_hi(act, At(C_CQ + h + 2))
                wait(act, mm_done, C_CQ + h + 1)
                nc.scalar.activation(QX[:, h, :], gres(r), ACT.Copy).then_inc(g_free[r.slot(NG)], 1)
                taken(act, r)
                wait(act, cr_ss, h - 1)
                nc.scalar.activation(SQ[:, h % 2, :], QX[:, h, :], ACT.Square).then_inc(cr_sq, 1)
            act.wait_ge(cr_ss, MEMH)
            for b in range(2):
                nc.scalar.activation(LX[:, 2 * b:2 * b + 2, :], A[b][:].rearrange("p (a t) -> p a t", a=2), ACT.Ln, bias=EPSC,
                                     scale=1.0 / P).then_inc(cr_ln, 1)
            act.wait_ge(cr_ln, 2)
            nc.scalar.activation(LX[:], LX[:], ACT.Exp, scale=-0.5, bias=con("lnsc")).then_inc(cr_rr, 1)
            for h in range(MEMH):
                wait(act, cr_nx, h + 1)
                wait(act, cr_tr, h - 1)
                for tt in range(2):
                    e = nc.scalar.activation(PX[:, h % 2, tt, :], A[2 + h % 2][:, tt * T:(tt + 1) * T], ACT.Exp,
                                             bias=NX[:, h % 2, tt:tt + 1], accum_out=SX[:, h % 2, tt:tt + 1])
                e.then_inc(cr_e, 1)
                wait(act, cr_tr, h + 1)
                wait(act, cr_o, h - 1)
                nc.scalar.activation(PXT[:, h % 2], A[4 + h % 2][:].rearrange("p (a t) -> p a t", a=2), ACT.Copy).then_inc(cr_pt, 1)
            for b in range(2):
                act.wait_ge(cr_o, 2 * b + 2)
                ins = nc.scalar.activation(HH[:, 2 * b:2 * b + 2, :], A[b][:].rearrange("p (a t) -> p a t", a=2), ACT.Copy)
                ins.then_inc(cr_hh, 1)
            for cc in range(4):
                split_hi(act, At(C_CO + cc + 2))
                wait(act, cr_x, 2 * cc + 2)
                for f in range(4):
                    ft = 4 * cc + f
                    wait(act, n_ss, norm_ff.sq(ft - 1))
                    nc.scalar.activation(SQ[:, ft % 2, :], X[:, ft, :], ACT.Square).then_inc(n_sq, 1)

        def cross_dve(dve):
            for h in range(MEMH):
                split_lo(dve, At(C_CQ + h + 2))
            dve.wait_ge(cr_rr, 1)
            for h in range(MEMH):
                nc.vector.scalar_tensor_tensor(QX[:, h, :], QX[:, h, :], vec("g_cq"), LX[:, h, :], ALU.mult, ALU.mult).then_inc(cr_qn, 1)

            def largest(h):
                wait(dve, cr_s, h + 1)
                wait(dve, cr_nx, h - 1)
                nc.vector.tensor_reduce(MX2[:, h % 2, :], A[2 + h % 2][:].rearrange("p (a t) -> p a t", a=2), AX_X, ALU.max).then_inc(cr_mx, 1)
                wait(dve, cr_mx, h + 1)
                wait(dve, cr_e, h - 1)
                nc.vector.tensor_scalar(NX[:, h % 2, :], MX2[:, h % 2, :], -1.0, None, ALU.mult).then_inc(cr_nx, 1)
            largest(0)
            for h in range(MEMH):
                if h + 1 < MEMH:
                    largest(h + 1)
                wait(dve, cr_e, h + 1)
                wait(dve, cr_p, h - 1)
                nc.vector.reciprocal(RX[:, h % 2, :], SX[:, h % 2, :]).then_inc(cr_rx, 1)
                wait(dve, cr_rx, h + 1)
                for tt in range(2):
                    ins = nc.vector.tensor_scalar(PX[:, h % 2, tt, :], PX[:, h % 2, tt, :], RX[:, h % 2, tt:tt + 1], None, ALU.mult)
                ins.then_inc(cr_p, 1)
            dve.wait_ge(cr_hh, 2)
            for b in range(2):
                ins = nc.vector.tensor_tensor(HL[:, 2 * b:2 * b + 2, :], A[b][:].rearrange("p (a t) -> p a t", a=2),
                                              HH[:, 2 * b:2 * b + 2, :].bitcast(F32), ALU.subtract)
            ins.then_inc(h_ready, 1)
            for cc in range(4):
                split_lo(dve, At(C_CO + cc + 2))
                wait(dve, mm_done, C_CO + cc + 1)
                for b in range(2):
                    x = X[:, 4 * cc + 2 * b:4 * cc + 2 * b + 2, :]
                    nc.vector.tensor_tensor(x, x, A[2 + 2 * (cc % 2) + b][:].rearrange("p (a t) -> p a t", a=2), ALU.add).then_inc(cr_x, 1)

        at = Layout(AFTER_HN)
        FHI = at("FHI", [P, KT, T], F32R)
        FLO = at("FLO", [P, KT, T], F32R)
        FT = at("FT", [P, 2, T])
        SF = at("SF", [P, 2, T])
        ff_hi, ff_lo = sem("ff_hi"), sem("ff_lo")

        class Part:

            def __init__(self, n, f0, c, r):
                self.n, self.f0, self.c, self.r = n, f0, c, r
                self.down = Project(c + 2 * n, r + 2 * n, None, None, n, (FHI, FLO), f0 + n)

            def loops(self, eng, pair):
                for j in range(2):
                    pair(At(j), j == 0)
                with eng.Fori(1, self.n // 2) as i:
                    for j in range(2):
                        pair(At(j, 2, i), False)

            def pe(self, pe):
                def pair(k, first):
                    for m in range(2):
                        gemm(pe, k.times(2) + (self.c + m), k.times(2) + (self.r + m), H_FF if first and self.f0 == 0 and m == 0 else None)
                self.loops(pe, pair)
                self.down.pe(pe)

            def act(self, act):
                def high(k):
                    taken(act, k.times(2) + (self.r + 1))
                    nc.scalar.activation(tile(FHI, k), FT[:, k.slot(2), :], ACT.Copy).then_inc(ff_hi, 1)

                def pair(k, first):
                    c, r = k.times(2) + self.c, k.times(2) + self.r
                    split_hi(act, c + 2)
                    split_hi(act, c + 3)
                    wait(act, mm_done, c + 1)
                    if not (isinstance(k.v, int) and k.v < 2):
                        taken(act, r - 3)
                    nc.scalar.activation(SF[:, k.slot(2), :], gres(r), ACT.Silu).then_inc(g_free[r.slot(NG)], 1)
                    if not first:
                        high(k - 1)
                self.loops(act, pair)
                high(At(self.n - 1))
                self.down.act(act)

            def dve(self, dve):
                def gated(k):
                    c, r, g = k.times(2) + self.c, k.times(2) + self.r, k + self.f0
                    taken(dve, r)
                    wait(dve, mm_done, c + 2)
                    wait(dve, ff_lo, g - 1)
                    nc.vector.tensor_tensor(FT[:, k.slot(2), :], SF[:, k.slot(2), :], gres(r + 1), ALU.mult).then_inc(g_free[(r + 1).slot(NG)], 1)

                def low(k):
                    g = k + self.f0
                    wait(dve, ff_hi, g + 1)
                    nc.vector.tensor_tensor(tile(FLO, k), FT[:, k.slot(2), :], tile(FHI, k).bitcast(F32), ALU.subtract).then_inc(ff_lo, 1)

                def pair(k, first):
                    c = k.times(2) + self.c
                    split_lo(dve, c + 2)
                    if not first:
                        gated(k - 1)
                    split_lo(dve, c + 3)
                    if not first:
                        low(k - 1)
                self.loops(dve, pair)
                gated(At(self.n - 1))
                low(At(self.n - 1))
                self.down.dve(dve)

        parts, f0, c0, r0 = [], 0, C_FF, R_FF
        for n in FF_PARTS:
            parts.append(Part(n, f0, c0, r0))
            f0, c0, r0 = f0 + n, c0 + 2 * n + KT, r0 + 2 * n + KT
        R_END = r0

        block = ctx.enter_context(nc.Block())

        @block.sync
        def _(sp):
            sp.dma_start(CON[:], constants).then_inc(s_in, 16)
            sp.dma_start(VEC[:], vectors).then_inc(s_in, 16)
            sp.dma_start(X[:], x_in).then_inc(s_in, 16)
            for s in range(2):
                sp.dma_start(RAW[:, s, :], stream[s]).then_inc(raw_ready[s], 16)
            with sp.Fori(1, C_END // 2) as i:
                for s in range(2):
                    c = At(s, 2, i)
                    wait(sp, lo_ready, c - 1)
                    sp.dma_start(RAW[:, s, :], stream[c.v]).then_inc(raw_ready[s], 16)
            if C_END % 2:
                sp.wait_ge(lo_ready, C_END - 2)
                sp.dma_start(RAW[:, 0, :], stream[C_END - 1]).then_inc(raw_ready[0], 16)
            taken(sp, At(R_END - 1))
            taken(sp, At(R_END - 2))
            sp.dma_start(out, X[:]).then_inc(s_out, 16)
            sp.wait_ge(s_out, 16)

        @block.tensor
        def _(pe):
            pe.wait_ge(s_in, 48)
            sums_all(pe, norm_conv)
            conv_pe(pe)
            conv_out.pe(pe)
            hgrn_pe(pe)
            hgrn_out.pe(pe)
            mixa_pe(pe)
            mixb_pe(pe)
            gla_pe(pe)
            mix_out.pe(pe)
            cross_pe(pe)
            for part in parts:
                part.pe(pe)

        @block.scalar
        def _(act):
            act.wait_ge(s_in, 48)
            squares_all(act, norm_conv)
            norm_conv.root(act)
            for c in range(2):
                split_hi(act, At(c))
            norm_conv.high(act)
            conv_act(act)
            conv_out.act(act)
            norm_hg.root(act)
            norm_hg.high(act)
            hgrn_act(act)
            hgrn_out.act(act)
            norm_mix.root(act)
            norm_mix.high(act)
            mixa_act(act)
            mixb_act(act)
            gla_act(act)
            mix_out.act(act)
            norm_cross.root(act)
            norm_cross.high(act)
            cross_act(act)
            norm_ff.root(act)
            norm_ff.high(act)
            for part in parts:
                part.act(act)

        @block.vector
        def _(dve):
            dve.wait_ge(s_in, 48)
            for c in range(2):
                split_lo(dve, At(c))
            norm_conv.scale(dve)
            conv_dve(dve)
            conv_out.dve(dve)
            norm_hg.scale(dve)
            hgrn_dve(dve)
            hgrn_out.dve(dve)
            norm_mix.scale(dve)
            mixa_dve(dve)
            mixb_dve(dve)
            gla_dve(dve)
            mix_out.dve(dve)
            norm_cross.scale(dve)
            cross_dve(dve)
            norm_ff.scale(dve)
            for part in parts:
                part.dve(dve)

        @block.gpsimd
        def _(pool):
            mem_pool(pool)
            mem_again_pool(pool)


def _stream(g):
    def tiles(w, k=KT):
        w = np.asarray(w)
        f = w.shape[1] // P
        out = np.zeros((f, P, KT, P), np.float32)
        out[:, :, :k] = w.reshape(k, P, f, P).transpose(2, 1, 0, 3)
        return out.reshape(f, P, CW)

    out = np.empty((C_END, P, CW), np.float32)
    w = tiles(g["conv_w_in"][0])
    for n, part in enumerate((1, 0, 2)):
        out[C_CONV + n:C_CONVO:3] = w[part * KT:(part + 1) * KT]
    out[C_CONVO:C_HG] = tiles(g["conv_w_out"][0])
    w = tiles(g["hgrn_w_in"][0])
    for n, part in enumerate((1, 2, 0, 3, 4)):
        out[C_HG + n:C_HGO:5] = w[part * KT:(part + 1) * KT]
    out[C_HGO:C_MIXA] = tiles(g["hgrn_w_out"][0])
    w = np.asarray(g["w_in_2"][0])
    at = np.cumsum([0, 1024, 256, 256, 256, 256, 256, 256, 24, 512, 512, 1024, 16, 1024])
    part = {n: w[:, a:b] for n, a, b in zip(
        ["q", "kc", "vc", "ks", "vs", "kw", "vw", "gate", "ql", "kl", "vl", "al", "rl"], at, at[1:])}
    gate = np.zeros((D, P), np.float32)
    gate[:, 0:24] = part["gate"]
    gate[:, 32:48] = part["al"]
    for n, name in enumerate(MIXA):
        if name[0] in "KV":
            x = np.asarray(g["w_ck1_2" if name[0] == "K" else "w_cv1_2"][0]).reshape(4, 8, P, 256)
            out[C_MIXA + n] = x[int(name[1])].transpose(1, 0, 2).reshape(P, CW)
        elif name == "gate":
            out[C_MIXA + n] = tiles(gate)[0]
        else:
            k = int(name[2])
            out[C_MIXA + n] = tiles(part[name[:2]][:, k * P:(k + 1) * P])[0]
    q = tiles(part["q"])
    rest = np.concatenate([tiles(part[n]) for n in ("ql", "kl", "vl", "rl")])
    for j in range(8):
        out[C_MIXB + 4 * j] = q[j]
        out[C_MIXB + 4 * j + 1:C_MIXB + 4 * j + 4] = rest[3 * j:3 * j + 3]
    out[C_MEM:C_MIXO:2] = tiles(g["w_ck_2"][0])
    out[C_MEM + 1:C_MIXO:2] = tiles(g["w_cv_2"][0])
    out[C_MIXO:C_CQ] = tiles(g["w_out_2"][0])
    out[C_CQ:C_CO] = tiles(g["w_cq_2"][0])
    out[C_CO:C_FF] = np.asarray(g["w_co_2"][0]).reshape(4, P, 4, 4, P).transpose(2, 1, 3, 0, 4).reshape(4, P, CW)
    gu, down = np.asarray(g["w_gu_2"][0]), np.asarray(g["w_down_2"][0])
    c, f0 = C_FF, 0
    for n in FF_PARTS:
        out[c:c + 2 * n:2] = tiles(gu[:, f0 * P:(f0 + n) * P])
        out[c + 1:c + 2 * n:2] = tiles(gu[:, DFF + f0 * P:DFF + (f0 + n) * P])
        out[c + 2 * n:c + 2 * n + KT] = tiles(down[f0 * P:(f0 + n) * P], n)
        c += 2 * n + KT
        f0 += n
    return out


def _vectors(g):
    v = np.zeros((P, V_COLS), np.float32)

    def put(name, a):
        a = np.asarray(a, np.float32)
        v[:a.shape[0], V_AT[name]:V_AT[name] + a.shape[1]] = a

    def cols(a):
        return np.asarray(a).reshape(-1, P).T
    for name, src in [("conv_norm", "conv_norm"), ("dw_b", "conv_dw_b"), ("ln_g", "conv_ln_g"),
                      ("ln_b", "conv_ln_b"), ("hgrn_norm", "hgrn_norm"), ("o_norm", "hgrn_o_norm"),
                      ("g_mix", "g_mix_2"), ("g_q", "g_q_2"), ("g_kc", "g_kc_2"), ("g_ks", "g_ks_2"),
                      ("g_kw", "g_kw_2"), ("g_nsa", "g_nsa_out_2"), ("b_gk", "b_gk_2"),
                      ("g_gla", "g_gla_out_2"), ("g_cross", "g_cross_2"), ("g_mem", "g_mem_2"),
                      ("g_cq", "g_cq_2"), ("g_ck", "g_ck_2"), ("g_ffn", "g_ffn_2")]:
        put(name, cols(g[src][0]))
    put("dw", np.asarray(g["conv_dw"][0]).reshape(TAPS, KT, P).transpose(2, 1, 0).reshape(P, -1))
    for n in range(2):
        put(f"lbf{n}", cols(g["hgrn_lb_fwd"][n]))
        put(f"lbb{n}", cols(g["hgrn_lb_bwd"][n]))
    put("b_gate", np.asarray(g["b_nsa_gate_2"][0])[:, None])
    put("pe_k", np.asarray(g["pe_k_2"][0]).T)
    put("pe_v", np.asarray(g["pe_v_2"][0]).T)
    put("ck2", np.asarray(g["w_ck2_2"][0]).reshape(2, P, P).transpose(1, 0, 2).reshape(P, 256))
    put("cv2", np.asarray(g["w_cv2_2"][0]).reshape(2, P, P).transpose(1, 0, 2).reshape(P, 256))
    v[32:48, V_AT["gk2"]:V_AT["gk2"] + 512] = np.asarray(g["w_gk2_2"][0])
    return v


def _feature_major(a):
    return np.ascontiguousarray(np.asarray(a)[0].T.reshape(KT, P, T).transpose(1, 0, 2))


def kernel(**inputs):
    import concourse.bacc as _bacc
    from concourse.bass_utils import run_bass_kernel_spmd as _run

    nc = _bacc.Bacc("TRN2", target_bir_lowering=False, num_devices=1)
    arrays = {"x_dram": _feature_major(inputs["x"]), "mem_dram": _feature_major(inputs["mem_2"]),
              "stream_dram": _stream(inputs), "vectors_dram": _vectors(inputs),
              "constants_dram": make_constants()}
    args = [nc.dram_tensor(n, a.shape, F32, kind="ExternalInput").ap() for n, a in arrays.items()]
    out = nc.dram_tensor("out_dram", (P, KT, T), F32, kind="ExternalOutput").ap()
    build(nc, *args, out)
    r = _run(nc, [arrays], core_ids=[0])
    got = np.asarray(r.results[0]["out_dram"])
    return np.ascontiguousarray(got.transpose(1, 0, 2).reshape(D, T).T)[None]
```

```python
from contextlib import ExitStack

import concourse.bass as bass
from concourse import mybir
import numpy as np
import math

F32 = mybir.dt.float32
F32R = mybir.dt.float32r
ACT = mybir.ActivationFunctionType
ALU = mybir.AluOpType
AX_X = mybir.AxisListType.X

P = 128
T = 256
D = 2048
KT = D // P
GRP = 4
CW = KT * P
TAPS = 31
PAD = TAPS // 2
HEADS = 16
CH = 64
NCH = T // CH
NG = 2
EPS = 1e-6
BIG = 1e30
N_CMP, CMP_LEN, CMP_STRIDE = 15, 32, 16
DFF = 5632
FK = DFF // P
MEMH = 4
ATT_SCALE = 128 ** -0.5

C_CONV = 0
C_CONVO = C_CONV + 3 * KT
C_HG = C_CONVO + KT
C_HGO = C_HG + 5 * KT
C_MIXA = C_HGO + KT
C_MIXB = C_MIXA + 21
C_MEM = C_MIXB + 32
C_MIXO = C_MEM + 8
C_CQ = C_MIXO + KT
C_CO = C_CQ + MEMH
C_FF = C_CO + 4
FF_PARTS = [16, 16, 12]
C_END = C_FF + sum(2 * n + KT for n in FF_PARTS)

MIXA = ["kc0", "kc1", "vc0", "vc1", "K0", "ks0", "K1", "ks1", "K2", "vs0", "K3", "vs1",
        "V0", "kw0", "V1", "kw1", "V2", "vw0", "V3", "vw1", "gate"]

R_CONV = 0
R_CONVO = R_CONV + 3 * KT
R_HG = R_CONVO + KT
R_HGO = R_HG + 5 * KT
R_MIXA = R_HGO + KT
R_MIXB = R_MIXA + 13
R_MEM = R_MIXB + 32
R_MIXO = R_MEM + 8
R_CQ = R_MIXO + KT
R_FF = R_CQ + MEMH

H_CONV, H_CONVY, H_HG, H_HGY, H_MIX, H_MEM, H_MIXY, H_CROSS, H_CO, H_FF = [4 * n for n in range(9)] + [33]

V_NAMES = [("conv_norm", 16), ("dw", 16 * TAPS), ("dw_b", 16), ("ln_g", 16), ("ln_b", 16),
           ("hgrn_norm", 16), ("lbf0", 16), ("lbb0", 16), ("lbf1", 16), ("lbb1", 16), ("o_norm", 1),
           ("g_mix", 16), ("b_gate", 1), ("g_q", 1), ("g_kc", 1), ("g_ks", 1), ("g_kw", 1),
           ("g_nsa", 1), ("b_gk", 4), ("g_gla", 2), ("g_cross", 16), ("g_mem", 16), ("g_cq", 1),
           ("g_ck", 1), ("g_ffn", 16), ("pe_k", 32), ("pe_v", 32), ("ck2", 256), ("cv2", 256), ("gk2", 512)]
V_AT, n_ = {}, 0
for name_, w_ in V_NAMES:
    V_AT[name_] = n_
    n_ += w_
V_COLS = n_

K_NAMES = [("ones", 128), ("eps", 1), ("ident", 128), ("keep", 2 * T), ("tri", 4 * P), ("dist1", 2 * T),
           ("dist0", T), ("distc", 2 * 16), ("slope", 8), ("rowok", 1), ("lnsc", 1)]
K_AT, n_ = {}, 0
for name_, w_ in K_NAMES:
    K_AT[name_] = n_
    n_ += w_
K_COLS = n_
K_FIRST = K_AT["ident"]
V_FIRST = V_AT["hgrn_norm"]


def make_constants():
    c = np.zeros((P, K_COLS), np.float32)

    def put(name, a):
        c[:, K_AT[name]:K_AT[name] + a.shape[1]] = a
    p = np.arange(P)
    t = np.arange(T)
    put("ident", np.eye(P))
    put("ones", np.ones((P, P)))
    put("keep", np.tile(np.concatenate([(t % CH != 0), (t % CH != CH - 1)]).astype(float), (P, 1)))
    same = (p[:, None] // CH) == (p[None, :] // CH)
    fwd = same & (p[:, None] <= p[None, :])
    bwd = same & (p[:, None] >= p[None, :])
    put("tri", np.concatenate([fwd, fwd, bwd, bwd], 1).astype(float))
    far = -1e30
    d1 = np.where(t[None, :] <= (P + p)[:, None], t[None, :] - (P + p)[:, None], far)
    d0 = np.where(p[None, :] <= p[:, None], p[None, :] - p[:, None], far)
    put("dist1", np.concatenate([d1, d1], 1))
    put("dist0", np.concatenate([d0, d0], 1))
    n = np.arange(N_CMP)
    for tile in range(2):
        tt = tile * P + p
        dc = np.where(tt[:, None] >= (n * CMP_STRIDE + CMP_LEN - 1)[None, :],
                      n[None, :] * CMP_STRIDE + 0.5 * (CMP_LEN - 1) - tt[:, None], far)
        c[:, K_AT["distc"] + 16 * tile:K_AT["distc"] + 16 * tile + N_CMP] = dc
    put("slope", np.tile(2.0 ** (-np.arange(1, 9)), (P, 1)))
    put("rowok", (p >= CMP_LEN - 1).astype(float)[:, None])
    put("eps", np.full((P, 1), EPS))
    put("lnsc", np.full((P, 1), math.log(ATT_SCALE)))
    return c


class At:

    def __init__(self, a, b=0, i=0):
        self.a, self.b, self.i = a, b, i

    def __add__(self, n):
        return At(self.a + n, self.b, self.i)

    def __sub__(self, n):
        return At(self.a - n, self.b, self.i)

    def times(self, n):
        return At(self.a * n, self.b * n, self.i)

    def slot(self, m):
        assert self.b % m == 0 or isinstance(self.i, int)
        return (self.a + (self.b * self.i if isinstance(self.i, int) else 0)) % m

    def turn(self, m):
        if isinstance(self.i, int):
            return At((self.a + self.b * self.i) // m)
        return At(self.a // m, self.b // m, self.i)

    @property
    def v(self):
        if self.b == 0:
            return self.a
        return self.i * self.b + self.a


def wait(eng, sem, at):
    v = at.v if isinstance(at, At) else at
    if isinstance(v, int) and v <= 0:
        return
    eng.wait_ge(sem, v)


class Steps:

    def __init__(self, eng, sem, per=0, i=0, base=0):
        self.eng, self.sem, self.per, self.i, self.base, self.n = eng, sem, per, i, base, 0

    def done(self, ins):
        ins.then_inc(self.sem, 1)
        self.n += 1
        return self.n

    def wait(self, n):
        wait(self.eng, self.sem, At(self.base + n, self.per, self.i))

    def link(self, ins):
        self.wait(self.done(ins))

    def end(self):
        assert not self.per or self.n == self.per, (self.n, self.per)


def build(nc, x_in, mem_in, stream, vectors, constants, out):
    with ExitStack() as ctx:
        def sb(name, shape, dt=F32):
            return ctx.enter_context(nc.sbuf_tensor(name, shape, dt))

        def sem(name):
            return ctx.enter_context(nc.semaphore(name))

        RING = 4
        HI = sb("HI", [P, RING, CW], F32R)
        X = sb("X", [P, KT, T])
        HH = sb("HH", [P, KT, T], F32R)
        HL = sb("HL", [P, KT, T], F32R)
        VEC = sb("VEC", [P, V_COLS])
        CON = sb("CON", [P, K_COLS])
        SQ = sb("SQ", [P, 2, T])
        LR = sb("LR", [P, T])
        RR = sb("RR", [P, T])

        class Layout:
            def __init__(self, at):
                self.at = at

            def __call__(self, name, shape, dt=F32):
                t = nc.alloc_sbuf_tensor_at(name, shape, dt, offset=self.at)
                size = 4
                for s in shape[1:]:
                    size *= s
                self.at += -(-size // 32) * 32
                assert self.at <= nc.sbuf_usable_end, (name, self.at)
                return t

        WORK = -(-nc.sbuf_base // 32) * 32

        at = Layout(WORK)
        RAW = at("RAW", [P, RING, CW])
        at = Layout(WORK)
        LO = at("LO", [P, RING, CW], F32R)
        WORK = at.at

        at = Layout(WORK)
        HN = at("HN", [P, 2, GRP, T])
        AFTER_HN = at.at
        CV = at("CV", [P, KT, T])
        SZ = at("SZ", [P, KT, T])
        VP = at("VP", [P, 2, T + 2 * PAD])
        SG = at("SG", [P, 2, T])
        CA = at("CA", [P, 2, T])
        DW = at("DW", [P, 2, 4])
        SC = at("SC", [P, 2, T])
        MU = at("MU", [P, T])
        MM = at("MM", [P, T])
        VA = at("VA", [P, T])

        G = ctx.enter_context(nc.psum_tensor("G", [P, NG, 512], F32))
        A = [ctx.enter_context(nc.psum_tensor(f"A{n}", [P, 512], F32)) for n in range(6)]

        raw_ready = [sem(f"raw_ready{s}") for s in range(RING)]
        hi_ready = sem("hi_ready")
        lo_ready = sem("lo_ready")
        mm_done = sem("mm_done")
        g_free = [sem(f"g_free{s}") for s in range(NG)]
        h_ready = sem("h_ready")
        s_x = [sem(f"s_x{g}") for g in range(KT // GRP)]
        s_mem = sem("s_mem")
        s_vec = sem("s_vec")
        s_rest = sem("s_rest")
        s_out = sem("s_out")

        def con(name, a=0, b=None):
            w = dict(K_NAMES)[name]
            return CON[:, K_AT[name] + a:K_AT[name] + (w if b is None else b)]

        def vec(name, a=0, rows=P):
            if isinstance(a, At):
                a = a.v
            if isinstance(a, int):
                return VEC[0:rows, V_AT[name] + a:V_AT[name] + a + 1]
            return VEC[0:rows, bass.ds(a + V_AT[name], 1)]

        def tile(buf, at):
            return buf[:, at.v if isinstance(at, At) else at, :]

        IDENT, ONES, EPSC = con("ident"), con("ones"), con("eps")

        def split_hi(act, c):
            if isinstance(c.v, int) and c.v >= C_END:
                return
            act.wait_ge(raw_ready[c.slot(RING)], (c.turn(RING) + 1).times(16).v)
            wait(act, mm_done, c - 3)
            nc.scalar.activation(HI[:, c.slot(RING), :], RAW[:, c.slot(RING), :], ACT.Copy).then_inc(hi_ready, 1)

        def split_lo(dve, c):
            if isinstance(c.v, int) and c.v >= C_END:
                return
            wait(dve, hi_ready, c + 1)
            nc.vector.tensor_tensor(LO[:, c.slot(RING), :], RAW[:, c.slot(RING), :],
                                    HI[:, c.slot(RING), :].bitcast(F32), ALU.subtract).then_inc(lo_ready, 1)

        def split_lo_pool(pool, c):
            wait(pool, hi_ready, c + 1)
            wait(pool, lo_ready, c)
            nc.gpsimd.tensor_tensor(LO[:, c.slot(RING), :], RAW[:, c.slot(RING), :],
                                    HI[:, c.slot(RING), :].bitcast(F32), ALU.subtract).then_inc(lo_ready, 1)

        def gemm(pe, c, r, kt=KT, operand=None):
            wait(pe, lo_ready, c + 1)
            wait(pe, g_free[r.slot(NG)], r.turn(NG))
            res = G[:, r.slot(NG), 0:T]
            high, low = operand or (HH, HL)
            for k in range(kt):
                w = slice(k * P, (k + 1) * P)
                wh, wl = HI[:, c.slot(RING), w], LO[:, c.slot(RING), w]
                nc.tensor.matmul(res, wh, high[:, k, :], start=(k == 0), stop=False)
                nc.tensor.matmul(res, wh, low[:, k, :], start=False, stop=False)
                mm = nc.tensor.matmul(res, wl, high[:, k, :], start=False, stop=(k == kt - 1))
            mm.then_inc(mm_done, 1)

        def gemm_two(pe, c, r, h):
            for g in range(KT // GRP):
                pe.wait_ge(h_ready, h + g + 1)
                for m in range(2):
                    if g == 0:
                        wait(pe, lo_ready, c + m + 1)
                        wait(pe, g_free[(r + m).slot(NG)], (r + m).turn(NG))
                    res = G[:, (r + m).slot(NG), 0:T]
                    for k in range(g * GRP, (g + 1) * GRP):
                        w = slice(k * P, (k + 1) * P)
                        wh, wl = HI[:, (c + m).slot(RING), w], LO[:, (c + m).slot(RING), w]
                        nc.tensor.matmul(res, wh, HH[:, k, :], start=(k == 0), stop=False)
                        nc.tensor.matmul(res, wh, HL[:, k, :], start=False, stop=False)
                        mm = nc.tensor.matmul(res, wl, HH[:, k, :], start=False, stop=(k == KT - 1))
                    if g == KT // GRP - 1:
                        mm.then_inc(mm_done, 1)

        def taken(eng, r):
            wait(eng, g_free[r.slot(NG)], r.turn(NG) + 1)

        def gres(r):
            return G[:, r.slot(NG), 0:T]

        n_zero = sem("n_zero")
        n_sq, n_ss, n_ln, n_rr, n_hn, n_hh = (sem(f"n_{s}") for s in ("sq", "ss", "ln", "rr", "hn", "hh"))

        class Norm:

            made = 0

            def __init__(self, gain, fill, last_chunk, bank):
                self.gain, self.fill, self.last, self.bank = gain, fill, last_chunk, bank
                self.n = Norm.made
                Norm.made += 1

            def sq(self, k):
                return k + KT * self.n

            def hn(self, k):
                return k + KT // GRP * self.n

            def roots(self):
                return self.n - (self.n > 3)

            def root(self, act):
                act.wait_ge(n_ss, self.sq(KT))
                nc.scalar.activation(LR[:], A[self.bank][:, 0:T], ACT.Ln, bias=EPSC, scale=1.0 / D).then_inc(n_ln, 1)
                act.wait_ge(n_ln, self.roots() + 1)
                nc.scalar.activation(RR[:], LR[:], ACT.Exp, scale=-0.5).then_inc(n_rr, 1)

            def scale(self, dve, between=None):
                dve.wait_ge(n_rr, self.roots() + 1)
                wait(dve, mm_done, self.last + 1)
                for g in range(KT // GRP + 1):
                    if g < KT // GRP:
                        if g >= 2:
                            dve.wait_ge(h_ready, self.fill + g - 1)
                        for k in range(GRP):
                            ft = g * GRP + k
                            ins = nc.vector.scalar_tensor_tensor(
                                HN[:, g % 2, k, :], X[:, ft, :], vec(self.gain, ft), RR[:], ALU.mult, ALU.mult)
                        ins.then_inc(n_hn, 1)
                    if g >= 1:
                        lo_part(dve, n_hh, HN[:, (g - 1) % 2], g - 1, self.hn(0))
                    if g == 1 and between:
                        between()

            def high(self, act, between=None):
                for g in range(KT // GRP):
                    act.wait_ge(n_hn, self.hn(g + 1))
                    nc.scalar.activation(HH[:, g * GRP:(g + 1) * GRP, :], HN[:, g % 2], ACT.Copy).then_inc(n_hh, 1)
                    if g == 1 and between:
                        between()

        def lo_part(dve, hh, src, g, before=0):
            dve.wait_ge(hh, before + g + 1)
            nc.vector.tensor_tensor(HL[:, g * GRP:(g + 1) * GRP, :], src,
                                    HH[:, g * GRP:(g + 1) * GRP, :].bitcast(F32), ALU.subtract).then_inc(h_ready, 1)

        def squares_first(act, n):
            for g in range(KT // GRP):
                act.wait_ge(s_x[g], 16 if g else 32)
                wait(act, n_ss, n.sq(GRP * (g - 1)))
                nc.scalar.activation(HN[:, g % 2], X[:, g * GRP:(g + 1) * GRP, :], ACT.Square).then_inc(n_sq, GRP)

        def sums_first(pe, n):
            pe.wait_ge(s_x[0], 32)
            for ft in range(KT):
                pe.wait_ge(n_sq, n.sq(GRP * (ft // GRP + 1)))
                nc.tensor.matmul(A[n.bank][:, 0:T], ONES, HN[:, (ft // GRP) % 2, ft % GRP, :], start=(ft == 0),
                                 stop=(ft == KT - 1)).then_inc(n_ss, 1)

        class Project:

            def __init__(self, c0, r0, n, fill, kt=KT, operand=None, ready=0, aside=(None, None, None)):
                self.aside = aside
                self.c0, self.r0, self.n, self.fill, self.kt = c0, r0, n, fill, kt
                self.operand, self.ready = operand, ready
                self.ends = int(c0 + KT == C_END)

            def pe(self, pe):
                if self.operand:
                    pe.wait_ge(ff_lo, self.ready)

                def tiles(i, first):
                    for j in range(4):
                        if first and j < 2 and self.fill is not None:
                            if j == 0:
                                gemm_two(pe, At(self.c0), At(self.r0), self.fill)
                        else:
                            gemm(pe, At(self.c0 + j, 4, i), At(self.r0 + j, 4, i), self.kt, self.operand)
                        if first and j == 1 and self.aside[0]:
                            self.aside[0](pe)
                tiles(0, True)
                with pe.Fori(1, 4) as i:
                    tiles(i, False)
                if self.n:
                    n, mean = self.n, A[self.n.bank][:, 0:T]
                    pe.wait_ge(n_ss, n.sq(KT - 1))
                    nc.tensor.matmul(mean, ONES, LR[:], start=True, stop=False)
                    pe.wait_ge(n_sq, n.sq(KT))
                    nc.tensor.matmul(mean, ONES, SQ[:, (KT - 1) % 2, :], start=False, stop=True).then_inc(n_ss, 1)

            def act(self, act):
                def square(r, ft):
                    taken(act, r)
                    wait(act, n_ss, ft + self.n.sq(-1))
                    nc.scalar.activation(SQ[:, ft.slot(2), :], tile(X, ft), ACT.Square).then_inc(n_sq, 1)

                def tiles(i, first=False):
                    for j in range(4):
                        if first and j == 2 and self.aside[1]:
                            self.aside[1](act)
                        split_hi(act, At(self.c0 + j + 2, 4, i))
                        if self.n and not (first and j == 0):
                            square(At(self.r0 + j - 1, 4, i), At(j - 1, 4, i))
                tiles(0, True)
                with act.Fori(1, 4 - self.ends) as i:
                    tiles(i)
                if self.ends:
                    tiles(3)
                if self.n:
                    square(At(self.r0 + KT - 1), At(KT - 1))

            def dve(self, dve):
                def tiles(i, first=False):
                    for j in range(4):
                        if first and j == 2 and self.aside[2]:
                            self.aside[2](dve)
                        c, r, ft = At(self.c0 + j, 4, i), At(self.r0 + j, 4, i), At(j, 4, i)
                        split_lo(dve, c + 2)
                        wait(dve, mm_done, c + 1)
                        nc.vector.tensor_tensor(tile(X, ft), tile(X, ft), gres(r), ALU.add).then_inc(g_free[r.slot(NG)], 1)
                        if self.n and not (first and j == 0):
                            wait(dve, n_sq, ft + self.n.sq(0))
                            wait(dve, n_ss, ft + self.n.sq(-1))
                            nc.vector.tensor_tensor(LR[:], LR[:], SQ[:, (ft - 1).slot(2), :], ALU.add).then_inc(n_ss, 1)
                apart = int(self.n is not None)
                if apart:
                    nc.vector.memset(LR[:], 0.0).then_inc(n_zero, 1)
                    dve.wait_ge(n_zero, {1: 1, 2: 2, 4: 3}[self.n.n])
                    tiles(0, True)
                with dve.Fori(apart, 4 - self.ends) as i:
                    tiles(i)
                if self.ends:
                    tiles(3)

        cv_tap, cv_done, cv_sq, cv_sums, cv_ln, cv_rr, cv_mu, cv_t, cv_act, cv_hh, cv_pad, cv_tap0, cv_dw = (
            sem(f"cv_{s}") for s in ("tap", "done", "sq", "sums", "ln", "rr", "mu", "t", "act", "hh", "pad", "tap0", "dw"))
        norm_conv = Norm("conv_norm", H_CONV, -1, 5)
        norm_hg = Norm("hgrn_norm", H_HG, C_HG - 1, 5)
        conv_out = Project(C_CONVO, R_CONVO, norm_hg, H_CONVY)

        SUMS = 3

        def tap_sum(ft, n):
            return CA[:, ft.slot(2), :] if n == 2 else A[ft.slot(2)][:, n * T:(n + 1) * T]

        def conv_pe(pe):
            def tiles(i, first):
                for j in range(4):
                    for m in range(3):
                        n = 3 * j + m
                        if not (first and n < 2):
                            gemm(pe, At(C_CONV + n, 12, i), At(R_CONV + n, 12, i))
                        elif n == 0:
                            gemm_two(pe, At(C_CONV), At(R_CONV), H_CONV)
                    if not (first and j == 0):
                        conv_sums(pe, At(j - 1, 4, i))
            tiles(0, True)
            with pe.Fori(1, 4) as i:
                tiles(i, False)
            conv_sums(pe, At(KT - 1))

        def conv_sums(pe, ft):
            f = ft.v if isinstance(ft.v, int) else 1
            wait(pe, cv_done, ft + 1)
            nc.tensor.matmul(A[4][:, 0:T], ONES, tile(CV, ft), start=(f == 0), stop=(f == KT - 1), skip_group_check=True)
            wait(pe, cv_sq, ft + 1)
            nc.tensor.matmul(A[3][:, 0:T], ONES, SC[:, ft.slot(2), :], start=(f == 0), stop=(f == KT - 1),
                             skip_group_check=True).then_inc(cv_sums, 1)

        def conv_act(act):
            def square(ft):
                wait(act, cv_done, ft + 1)
                wait(act, cv_sums, ft - 1)
                nc.scalar.activation(SC[:, ft.slot(2), :], tile(CV, ft), ACT.Square).then_inc(cv_sq, 1)

            def first_taps(ft, r):
                wait(act, cv_dw, ft + 1)
                taken(act, r + 1)
                wait(act, cv_done, ft - 1)
                for k in range(SUMS):
                    ins = nc.scalar.activation(tap_sum(ft, k), VP[:, ft.slot(2), k:k + T], ACT.Identity,
                                               bias=DW[:, ft.slot(2), SUMS:] if k == 0 else 0.0, scale=DW[:, ft.slot(2), k:k + 1])
                ins.then_inc(cv_tap0, 1)

            def tiles(i, peeled, last=False):
                for j in range(4):
                    ft, c, r = At(j, 4, i), At(C_CONV + 3 * j, 12, i), At(R_CONV + 3 * j, 12, i)
                    split_hi(act, c + 3)
                    wait(act, cv_tap0, ft - 1)
                    wait(act, mm_done, c + 1)
                    if not (peeled and j < 2):
                        taken(act, r - 5)
                    nc.scalar.activation(SG[:, ft.slot(2), :], gres(r), ACT.Sigmoid).then_inc(g_free[r.slot(NG)], 1)
                    first = ft.times(TAPS).v
                    first = slice(V_AT["dw"] + first, V_AT["dw"] + first + SUMS) if isinstance(first, int) else bass.ds(
                        first + V_AT["dw"], SUMS)
                    nc.scalar.activation(DW[:, ft.slot(2), 0:SUMS], VEC[:, first], ACT.Copy)
                    nc.scalar.activation(DW[:, ft.slot(2), SUMS:], vec("dw_b", ft), ACT.Copy).then_inc(cv_dw, 1)
                    split_hi(act, c + 4)
                    first_taps(ft, r)
                    if not (peeled and j == 0):
                        square(ft - 1)
                    if not (last and j == 3):
                        split_hi(act, c + 5)
                    wait(act, mm_done, c + 3)
                    nc.scalar.activation(tile(SZ, ft), gres(r + 2), ACT.Silu).then_inc(g_free[(r + 2).slot(NG)], 1)
            tiles(0, True)
            with act.Fori(1, 3) as i:
                tiles(i, False)
            tiles(3, False, True)
            square(At(KT - 1))
            act.wait_ge(cv_mu, 4)
            nc.scalar.activation(LR[:], VA[:], ACT.Ln, bias=EPSC).then_inc(cv_ln, 1)
            act.wait_ge(cv_ln, 1)
            nc.scalar.activation(RR[:], LR[:], ACT.Exp, scale=-0.5).then_inc(cv_rr, 1)
            for g in range(KT // GRP):
                for k in range(GRP):
                    ft = g * GRP + k
                    act.wait_ge(cv_t, 2 * g + 2)
                    ins = nc.scalar.activation(CV[:, ft, :], CV[:, ft, :], ACT.Silu, bias=vec("ln_b", ft), scale=vec("ln_g", ft))
                ins.then_inc(cv_act, 1)
                act.wait_ge(cv_pad, 3 + g)
                nc.scalar.activation(HH[:, g * GRP:(g + 1) * GRP, :], CV[:, g * GRP:(g + 1) * GRP, :], ACT.Copy).then_inc(cv_hh, 1)

        def conv_dve(dve):
            nc.vector.memset(VP[:, :, 0:PAD], 0.0).then_inc(cv_pad, 1)
            nc.vector.memset(VP[:, :, PAD + T:], 0.0).then_inc(cv_pad, 1)
            dve.wait_ge(cv_pad, 2)

            def tap(ft, k, acc):
                src = VP[:, ft.slot(2), k:k + T]
                w = vec("dw", ft.times(TAPS) + k)
                return nc.vector.scalar_tensor_tensor(acc, src, w, acc, ALU.mult, ALU.add)

            def tiles(i):
                st = Steps(dve, cv_tap, 4 * (TAPS - 2), i)
                for j in range(4):
                    ft, c, r = At(j, 4, i), At(C_CONV + 3 * j, 12, i), At(R_CONV + 3 * j, 12, i)
                    accs = [tap_sum(ft, n) for n in range(SUMS)]

                    def taps(a, b):
                        for k in range(a, b):
                            if k >= 2 * SUMS:
                                st.wait(st.n - SUMS + 1)
                            st.done(tap(ft, k, accs[k % SUMS]))
                    wait(dve, lo_ready, c + 3)
                    split_lo(dve, c + 3)
                    taken(dve, r)
                    wait(dve, mm_done, c + 2)
                    nc.vector.tensor_tensor(VP[:, ft.slot(2), PAD:PAD + T], gres(r + 1), SG[:, ft.slot(2), :],
                                            ALU.mult).then_inc(g_free[(r + 1).slot(NG)], 1)
                    split_lo(dve, c + 4)
                    wait(dve, cv_tap0, ft + 1)
                    taps(SUMS, TAPS)
                    st.wait(st.n)
                    st.link(nc.vector.tensor_tensor(accs[2], accs[1], accs[2], ALU.add))
                    nc.vector.tensor_tensor(tile(CV, ft), accs[0], accs[2], ALU.add).then_inc(cv_done, 1)
                st.end()
            with dve.Fori(0, 4) as i:
                tiles(i)
            dve.wait_ge(cv_sums, KT)
            nc.vector.tensor_scalar(MU[:], A[4][:, 0:T], 1.0 / D, None, ALU.mult).then_inc(cv_mu, 1)
            dve.wait_ge(cv_mu, 1)
            nc.vector.tensor_tensor(MM[:], MU[:], MU[:], ALU.mult).then_inc(cv_mu, 1)
            dve.wait_ge(cv_mu, 2)
            nc.vector.scalar_tensor_tensor(VA[:], A[3][:, 0:T], 1.0 / D, MM[:], ALU.mult, ALU.subtract).then_inc(cv_mu, 1)
            dve.wait_ge(cv_mu, 3)
            nc.vector.tensor_scalar(VA[:], VA[:], 0.0, None, ALU.max).then_inc(cv_mu, 1)

            def wide(v):
                return v.unsqueeze(1).broadcast_to([P, GRP, T])

            def group(g):
                return CV[:, g * GRP:(g + 1) * GRP, :]

            def centre(g):
                nc.vector.tensor_tensor(group(g), group(g), wide(MU[:]), ALU.subtract).then_inc(cv_t, 1)

            def normalise(g):
                dve.wait_ge(cv_t, 2 * g + 1)
                nc.vector.tensor_tensor(group(g), group(g), wide(RR[:]), ALU.mult).then_inc(cv_t, 1)

            def gated(g):
                dve.wait_ge(cv_act, g + 1)
                nc.vector.tensor_tensor(group(g), group(g), SZ[:, g * GRP:(g + 1) * GRP, :], ALU.mult).then_inc(cv_pad, 1)

            last = KT // GRP - 1
            centre(0)
            dve.wait_ge(cv_rr, 1)
            normalise(0)
            centre(1)
            for g in range(last + 1):
                if g < last:
                    normalise(g + 1)
                gated(g)
                if g + 2 <= last:
                    centre(g + 2)
                lo_part(dve, cv_hh, group(g), g)

        def conv_pool(pool):
            with pool.Fori(0, 4) as i:
                for j in range(4):
                    split_lo_pool(pool, At(C_CONV + 3 * j + 2, 12, i))

        at = Layout(AFTER_HN)
        Y = at("Y", [P, KT, T])
        OML = at("OML", [P, 2, HEADS])
        OMN = at("OMN", [P, 2, HEADS])
        SA = at("SA", [P, 2, T])
        LF = at("LF", [P, 2, T])
        BC = at("BC", [P, 2, T])
        DB = at("DB", [P, 2, T])
        EQ = at("EQ", [P, 2, T])
        EK = at("EK", [P, 2, T])
        E2 = at("E2", [P, 2, NCH, 2])
        QC = at("QC", [P, T])
        QT = at("QT", [P, 2, T])
        KD = at("KD", [P, 2, T])
        VF = at("VF", [P, T])
        VT = at("VT", [P, 2, P])
        KX = at("KX", [P, 2, 2, P])
        SM = at("SM", [P, 2, 2, P])
        ST = at("ST", [P, 2, 3, P])
        SD = at("SD", [P, 2, P])
        SP_ = at("SP_", [P, 2, 3, P])
        SZH = at("SZH", [P, T])
        ZG = at("ZG", [P, T])
        OG = at("OG", [P, T])

        (hg_lb, hg_oml, hg_lf, hg_sc, hg_d, hg_exp, hg_qt, hg_kx, hg_vt, hg_tr, hg_s, hg_sm, hg_kv,
         hg_st, hg_stp, hg_o, hg_sq, hg_ss, hg_ln, hg_rr, hg_og, hg_y, hg_hh) = (
            sem(f"hg_{s}") for s in ("lb", "oml", "lf", "scan", "d", "exp", "qt", "kx", "vt", "tr", "s", "sm", "kv",
                                     "st", "stp", "o", "sq", "ss", "ln", "rr", "og", "y", "hh"))
        norm_mix = Norm("g_mix", H_MIX, C_MIXA - 1, 5)
        hgrn_out = Project(C_HGO, R_HGO, norm_mix, H_HGY)
        STEPS_ST = 15

        def order(d, s):
            return s if d == 0 else NCH - 1 - s

        def kv_product(d, s):
            n = {(0, 0): 0, (0, 2): 1, (1, 1): 2, (0, 1): 0, (1, 0): 1, (1, 2): 2}[d, s]
            return A[2 + order(d, s) % 2][:, n * P:(n + 1) * P]

        def mid(d):
            return CH // 2 - 1 if d == 0 else CH // 2

        def end(d):
            return CH - 1 if d == 0 else 0

        def head_chunk(h, m):
            return h.times(5) + (C_HG + m)

        def head_result(h, m):
            return h.times(5) + (R_HG + m)

        def hgrn_pe(pe):
            def kv(p):
                wait(pe, hg_kx, p + 1)
                wait(pe, hg_vt, p + 1)
                wait(pe, hg_st, p)
                for d in range(2):
                    for s in range(3):
                        c = order(d, s)
                        rows = slice((c % 2) * CH, (c % 2) * CH + CH)
                        mm = nc.tensor.matmul(kv_product(d, s), KX[rows, d, c // 2, :],
                                              VT[rows, c // 2, :], start=True, stop=True)
                mm.then_inc(hg_kv, 1)

            def output(p):
                wait(pe, hg_sm, p + 1)
                wait(pe, hg_st, p + 1)
                wait(pe, hg_og, p)
                for tt in range(2):
                    o = A[5][:, tt * P:(tt + 1) * P]
                    nc.tensor.matmul(o, VT[:, tt, :], SM[:, 0, tt, :], start=True, stop=False)
                    for d, s in [(d, s) for s in range(3) for d in range(2) if order(d, s + 1) // 2 == tt]:
                        c = order(d, s + 1)
                        nc.tensor.matmul(A[5][:, c * CH:(c + 1) * CH], SP_[:, d, s, :],
                                         QT[:, d, c * CH:(c + 1) * CH], start=False, stop=False)
                    mm = nc.tensor.matmul(o, VT[:, tt, :], SM[:, 1, tt, :], start=False, stop=True)
                mm.then_inc(hg_o, 1)

            def sums(p):
                wait(pe, hg_sq, p + 1)
                wait(pe, hg_vt, p + 1)
                nc.tensor.matmul(A[4][:, T:2 * T], ONES, SQ[:, 0, :], start=True, stop=True).then_inc(hg_ss, 1)

            def turn(h):
                taken(pe, head_result(h, 3))
                wait(pe, hg_ln, h)
                for tt in range(2):
                    nc.tensor.transpose(A[4][:, tt * P:(tt + 1) * P], VF[:, tt * P:(tt + 1) * P], IDENT)
                wait(pe, hg_qt, h + 1)
                wait(pe, hg_kx, h)
                for d in range(2):
                    for tt in range(2):
                        n = 2 * d + tt
                        tr = nc.tensor.transpose(A[1][:, n * P:(n + 1) * P], KD[:, d, tt * P:(tt + 1) * P], IDENT)
                tr.then_inc(hg_tr, 1)
                wait(pe, hg_sm, h)
                for d in range(2):
                    for tt in range(2):
                        n = 2 * d + tt
                        w = slice(tt * P, (tt + 1) * P)
                        mm = nc.tensor.matmul(A[0][:, n * P:(n + 1) * P], KD[:, d, w], QT[:, d, w], start=True, stop=True)
                mm.then_inc(hg_s, 1)

            def head(h, p):
                if p:
                    gemm(pe, head_chunk(h, 0), head_result(h, 0))
                    kv(p)
                    gemm(pe, head_chunk(h, 1), head_result(h, 1))
                else:
                    gemm_two(pe, head_chunk(h, 0), head_result(h, 0), H_HG)
                gemm(pe, head_chunk(h, 2), head_result(h, 2))
                if p:
                    output(p)
                gemm(pe, head_chunk(h, 3), head_result(h, 3))
                if p:
                    sums(p)
                gemm(pe, head_chunk(h, 4), head_result(h, 4))
                turn(h)

            for j in range(4):
                head(At(j), At(j - 1) if j else None)
            with pe.Fori(1, 4) as i:
                for j in range(4):
                    head(At(j, 4, i), At(j - 1, 4, i))
            last = At(HEADS - 1)
            kv(last)
            output(last)
            sums(last)

        def hgrn_act(act):
            def gate(p):
                r = head_result(p, 4)
                wait(act, mm_done, head_chunk(p, 4) + 1)
                taken(act, r - 5)
                nc.scalar.activation(SZH[:], gres(r), ACT.Sigmoid).then_inc(hg_sc, 1)

            def keys(p):
                wait(act, hg_tr, p + 1)
                wait(act, hg_kv, p)
                nc.scalar.activation(KX[:], A[1][:].rearrange("p (d t m) -> p d t m", d=2, t=2), ACT.Copy).then_inc(hg_kx, 1)

            def square(p):
                wait(act, hg_o, p + 1)
                wait(act, hg_ss, p)
                nc.scalar.activation(SQ[:, 0, :], A[5][:, 0:T], ACT.Square).then_inc(hg_sq, 1)

            def root(p):
                wait(act, hg_ss, p + 1)
                wait(act, hg_rr, p)
                nc.scalar.activation(LR[:], A[4][:, T:2 * T], ACT.Ln, bias=EPSC, scale=1.0 / P).then_inc(hg_ln, 1)
                wait(act, hg_ln, p + 1)
                wait(act, hg_og, p)
                nc.scalar.activation(RR[:], LR[:], ACT.Exp, scale=-0.5).then_inc(hg_rr, 1)

            def head(h, p):
                c, r = head_chunk(h, 0), head_result(h, 0)
                split_hi(act, c + 2)
                if p:
                    gate(p)
                    keys(p)
                for d in range(2):
                    split_hi(act, c + 3 + d)
                    wait(act, mm_done, c + 1 + d)
                    wait(act, hg_qt, h)
                    nc.scalar.activation(SA[:, d, :], gres(r + d), ACT.Sigmoid, scale=-1.0).then_inc(g_free[(r + d).slot(NG)], 1)
                split_hi(act, c + 5)
                wait(act, mm_done, c + 3)
                wait(act, hg_qt, h)
                nc.scalar.activation(QC[:], gres(r + 2), ACT.Copy).then_inc(g_free[(r + 2).slot(NG)], 1)
                for d in range(2):
                    taken(act, r + d)
                    wait(act, hg_d, h.times(4))
                    nc.scalar.activation(LF[:, d, :], SA[:, d, :], ACT.Ln, bias=1.0,
                                         scale=omn(d, h)).then_inc(hg_lf, 1)
                if p:
                    square(p)
                wait(act, hg_d, h.times(4) + 4)
                wait(act, hg_st, h)
                nc.scalar.activation(EQ[:], DB[:], ACT.Exp).then_inc(hg_exp, 1)
                nc.scalar.activation(EK[:], DB[:], ACT.Exp, scale=-1.0).then_inc(hg_exp, 1)
                for d in range(2):
                    src = BC[:, d, :].rearrange("p (c n) -> p c n", c=NCH)[:, :, (mid(d), end(d))[d]::CH // 2]
                    ins = nc.scalar.activation(E2[:, d, :, :], src, ACT.Exp)
                ins.then_inc(hg_exp, 1)
                split_hi(act, c + 6)
                wait(act, mm_done, c + 4)
                wait(act, hg_tr, h)
                nc.scalar.activation(VF[:], gres(r + 3), ACT.Copy).then_inc(g_free[(r + 3).slot(NG)], 1)
                if p:
                    root(p)

            def omn(d, h):
                v = h.v
                return OMN[:, d, v:v + 1] if isinstance(v, int) else OMN[:, d, bass.ds(v, 1)]

            act.wait_ge(hg_lb, 2)
            nc.scalar.activation(OML[:], OMN[:], ACT.Sigmoid).then_inc(hg_oml, 1)
            act.wait_ge(hg_oml, 2)
            for j in range(4):
                head(At(j), At(j - 1) if j else None)
            with act.Fori(1, 4) as i:
                for j in range(4):
                    head(At(j, 4, i), At(j - 1, 4, i))
            last = At(HEADS - 1)
            def high(g):
                act.wait_ge(mm_done, C_HGO)
                act.wait_ge(hg_y, GRP * (g + 1))
                nc.scalar.activation(HH[:, g * GRP:(g + 1) * GRP, :], Y[:, g * GRP:(g + 1) * GRP, :], ACT.Copy).then_inc(hg_hh, 1)

            gate(last)
            keys(last)
            high(0)
            high(1)
            square(last)
            root(last)
            high(2)
            high(3)

        def hgrn_dve(dve):
            def values(p):
                wait(dve, hg_tr, p + 1)
                wait(dve, hg_o, p)
                nc.vector.tensor_copy(VT[:], A[4][:, 0:T].rearrange("p (t m) -> p t m", t=2)).then_inc(hg_vt, 1)

            def mask(p):
                wait(dve, hg_s, p + 1)
                nc.vector.scalar_tensor_tensor(SM[:].rearrange("p d t m -> p (d t m)"), A[0][:], BIG, con("tri"),
                                               ALU.min, ALU.mult).then_inc(hg_sm, 1)

            def gate(p):
                r = head_result(p, 4)
                wait(dve, hg_sc, p + 1)
                wait(dve, hg_y, p)
                nc.vector.tensor_tensor(ZG[:], gres(r), SZH[:], ALU.mult).then_inc(g_free[r.slot(NG)], 1)

            def states(p, st):
                wait(dve, hg_kv, p + 1)
                wait(dve, hg_exp, p.times(3) + 3)
                at_end = [EQ[:, d, :].rearrange("p (c n) -> p c n", c=NCH)[:, :, end(d)] for d in range(2)]
                done = {}
                n_mid = [0, 1]
                for s in range(3):
                    for d in range(2):
                        c = order(d, s)
                        e = at_end[d][:, c:c + 1]
                        if s == 0:
                            done[d] = st.done(nc.vector.tensor_scalar(ST[:, d, 0, :], kv_product(d, 0), e, None, ALU.mult))
                        else:
                            st.wait(done[d])
                            done[d] = st.done(nc.vector.tensor_scalar(SD[:, d, :], ST[:, d, s - 1, :],
                                                                      E2[:, d, c, 1 - n_mid[d]:2 - n_mid[d]], None, ALU.mult))
                    if s:
                        for d in range(2):
                            c = order(d, s)
                            st.wait(done[d])
                            done[d] = st.done(nc.vector.scalar_tensor_tensor(ST[:, d, s, :], kv_product(d, s),
                                                                             at_end[d][:, c:c + 1], SD[:, d, :], ALU.mult, ALU.add))
                    for d in range(2):
                        c = order(d, s + 1)
                        st.wait(done[d])
                        ins = nc.vector.tensor_scalar(SP_[:, d, s, :], ST[:, d, s, :],
                                                      E2[:, d, c, n_mid[d]:n_mid[d] + 1], None, ALU.mult)
                        if s == 2 and d == 1:
                            ins.then_inc(hg_st, 1)
                        else:
                            st.done(ins)

            def sums(h):
                for d in range(2):
                    wait(dve, hg_lf, h.times(2) + 1 + d)
                    wait(dve, hg_exp, h.times(3))
                    keep = con("keep", d * T, (d + 1) * T)
                    rev = (lambda v: v) if d == 0 else (lambda v: v[:, ::-1])
                    nc.vector.tensor_tensor_scan(rev(BC[:, d, :]), rev(keep), rev(LF[:, d, :]), 0.0, ALU.mult, ALU.add).then_inc(hg_d, 1)
                for d in range(2):
                    wait(dve, hg_d, h.times(4) + 1 + d)
                    b = BC[:, d, :].rearrange("p (c n) -> p c n", c=NCH)
                    m = b[:, :, mid(d):mid(d) + 1].broadcast_to([P, NCH, CH])
                    nc.vector.tensor_tensor(DB[:, d, :].rearrange("p (c n) -> p c n", c=NCH), b, m, ALU.subtract).then_inc(hg_d, 1)

            def decayed(h):
                r = head_result(h, 2)
                taken(dve, r)
                wait(dve, hg_exp, h.times(3) + 3)
                wait(dve, hg_o, h)
                wait(dve, hg_s, h)
                nc.vector.tensor_tensor(QT[:], QC[:].unsqueeze(1).broadcast_to([P, 2, T]), EQ[:], ALU.mult)
                for d in range(2):
                    v = h.v
                    one = OML[:, d, v:v + 1] if isinstance(v, int) else OML[:, d, bass.ds(v, 1)]
                    ins = nc.vector.scalar_tensor_tensor(KD[:, d, :], SA[:, d, :], one, EK[:, d, :], ALU.mult, ALU.mult)
                ins.then_inc(hg_qt, 1)

            def finish(p):
                wait(dve, hg_rr, p + 1)
                nc.vector.scalar_tensor_tensor(OG[:], A[5][:, 0:T], vec("o_norm"), RR[:], ALU.mult, ALU.mult).then_inc(hg_og, 1)
                wait(dve, hg_og, p + 1)
                taken(dve, head_result(p, 4))
                nc.vector.tensor_tensor(tile(Y, p), OG[:], ZG[:], ALU.mult).then_inc(hg_y, 1)

            def head(h, p, st):
                c = head_chunk(h, 0)
                split_lo(dve, c + 2)
                if p:
                    gate(p)
                    mask(p)
                    values(p)
                split_lo(dve, c + 3)
                if p:
                    states(p, st)
                split_lo(dve, c + 4)
                split_lo(dve, c + 5)
                sums(h)
                split_lo(dve, c + 6)
                decayed(h)
                if p:
                    finish(p)

            for d, n in enumerate(("lbf", "lbb")):
                a0, a1 = V_AT[n + "0"], V_AT[n + "1"]
                nc.vector.tensor_tensor(OMN[:, d, :], VEC[:, a0:a0 + HEADS], VEC[:, a1:a1 + HEADS], ALU.subtract).then_inc(hg_lb, 1)
            dve.wait_ge(hg_oml, 1)
            nc.vector.tensor_scalar(OMN[:], OML[:], -1.0, None, ALU.mult).then_inc(hg_oml, 1)
            st = Steps(dve, hg_stp)
            for j in range(4):
                head(At(j), At(j - 1) if j else None, st)
            with dve.Fori(1, 4) as i:
                st2 = Steps(dve, hg_stp, 4 * STEPS_ST, i, st.n - 4 * STEPS_ST)
                for j in range(4):
                    head(At(j, 4, i), At(j - 1, 4, i), st2)
                st2.end()
            last = At(HEADS - 1)
            gate(last)
            mask(last)
            values(last)
            states(last, Steps(dve, hg_stp, base=st.n + 3 * 4 * STEPS_ST))
            for g in range(2):
                lo_part(dve, hg_hh, Y[:, g * GRP:(g + 1) * GRP, :], g)
            finish(last)
            for g in range(2, KT // GRP):
                lo_part(dve, hg_hh, Y[:, g * GRP:(g + 1) * GRP, :], g)

        at = Layout(AFTER_HN)
        YN = at("YN", [P, 8, T])
        OTH_AT = at.at
        OTH = at("OTH", [P, 24, T])
        AFTER_OTH = at.at
        KN = at("KN", [P, 4, T])
        VW = at("VW", [P, 4, 2, P])
        VC = at("VC", [P, 2, P])
        KC = at("KC", [P, 2 * N_CMP])
        KCR = at("KCR", [P, 2, 2 * N_CMP])
        GT = at("GT", [P, 2, 24])
        PTC = at("PTC", [P, T])
        QCN = at("QCN", [P, T])
        QN = at("QN", [P, T])
        LO2 = at("LO2", [P, T])
        RO = at("RO", [P, T])
        ON = at("ON", [P, T])
        MX = at("MX", [P, 2, 3])
        NM = at("NM", [P, 2, 3])
        SL = at("SL", [P, 2, 3])
        RC = at("RC", [P, 2, 3])
        CF = at("CF", [P, 2, 3])
        HS = at("HS", [P, 2, 2, 2 * N_CMP])
        HT = at("HT", [P, 2, 2 * P])
        at = Layout(nc.sbuf_usable_end // 32 * 32 - 2 * T * 4)
        AL = at("AL", [P, T])
        RM = at("RM", [P, T])
        at = Layout(nc.sbuf_usable_end // 32 * 32 - (2 + KT) * T * 4)
        MB = at("MB", [P, KT, T])
        at = Layout(OTH_AT)
        BLH = at("BLH", [P, 2, CMP_LEN, 2 * N_CMP], F32R)
        BLL = at("BLL", [P, 2, CMP_LEN, 2 * N_CMP], F32R)
        UC = at("UC", [P, 4, T])
        LK = UC
        BT = at("BT", [P, 2, CMP_LEN, N_CMP])
        assert at.at <= AFTER_OTH
        at = Layout(AFTER_HN)
        VF4 = at("VF4", [P, 4, T])
        GF = at("GF", [P, T])
        at = Layout(WORK)
        PB = at("PB", [P, 2, 528])
        PTS = at("PTS", [P, 384])
        PTW = at("PTW", [P, 384])
        assert at.at <= AFTER_HN

        (mx_uc, mx_bt, mx_bh, mx_bl, mx_cmp, mx_hs, mx_c2, mx_kc, mx_vc, mx_ksq, mx_kss, mx_kln, mx_krr, mx_kn, mx_vtr,
         mx_vw, mx_gf, mx_gtr, mx_gt, mx_zero, mx_mr, mx_ht) = (
            sem(f"mx_{s}") for s in ("uc", "bt", "bh", "bl", "cmp", "hs", "c2", "kc", "vc", "ksq", "kss", "kln", "krr", "kn",
                                     "vtr", "vw", "gf", "gtr", "gt", "zero", "mr", "ht"))
        norm_mem = Norm("g_mem", H_MEM, C_MEM - 1, 5)
        raw_tiles = {"ks0": (KN, 0), "ks1": (KN, 1), "kw0": (KN, 2), "kw1": (KN, 3), "vs0": (VF4, 0), "vs1": (VF4, 1),
                     "vw0": (VF4, 2), "vw1": (VF4, 3), "kc0": (UC, 0), "kc1": (UC, 1), "vc0": (UC, 2), "vc1": (UC, 3)}
        results = [n for n in MIXA if n[0] not in "KV"]

        def mixa_chunk(name):
            return At(C_MIXA + MIXA.index(name))

        def mixa_result(name):
            return At(R_MIXA + results.index(name))

        squares_after, sums_after = ["kc1", "vc0", "vc1", "K0"], ["vc0", "vc1", "K0", "ks0"]

        def mixa_pe(pe):
            for n, name in enumerate(MIXA):
                c = At(C_MIXA + n)
                if n == 0:
                    gemm_two(pe, c, mixa_result(name), H_MIX)
                elif n == 1:
                    pass
                elif name[0] not in "KV":
                    gemm(pe, c, mixa_result(name))
                else:
                    kv, part = "KV".index(name[0]), int(name[1])
                    wait(pe, lo_ready, c + 1)
                    wait(pe, mx_bl, 2 * kv + 2)
                    for pos in range(8):
                        w = slice(2 * pos * P, (2 * pos + 2) * P)
                        res, l = A[2 * kv][0:2 * N_CMP, 0:2 * P], 8 * part + pos
                        nc.tensor.matmul(res, BLH[:, kv, l, :], HI[:, c.slot(RING), w], start=(l == 0), stop=False)
                        nc.tensor.matmul(res, BLL[:, kv, l, :], HI[:, c.slot(RING), w], start=False, stop=False)
                        mm = nc.tensor.matmul(res, BLH[:, kv, l, :], LO[:, c.slot(RING), w], start=False, stop=(l == CMP_LEN - 1))
                    mm.then_inc(mm_done, 1)
                if name in sums_after:
                    g = sums_after.index(name)
                    pe.wait_ge(n_sq, norm_mem.sq(GRP * (g + 1)))
                    for k in range(GRP):
                        nc.tensor.matmul(A[5][:, 0:T], ONES, HN[:, g % 2, k, :], start=(g == 0 and k == 0),
                                         stop=(g * GRP + k == KT - 1)).then_inc(n_ss, 1)
                if name in ("kw0", "vw1"):
                    kv = int(name == "vw1")
                    pe.wait_ge(mx_ht, 2 * kv + 1)
                    for m in range(2):
                        tr = nc.tensor.transpose(A[2 * kv + 1][:, 32 * m:32 * m + 2 * N_CMP], HT[0:2 * N_CMP, kv, m * P:(m + 1) * P],
                                                 IDENT[0:2 * N_CMP, 0:2 * N_CMP])
                    tr.then_inc(mx_ht, 1)
                if name == "V1":
                    pe.wait_ge(mx_hs, 1)
                    for m in range(2):
                        mm = nc.tensor.matmul(A[4][:, 0:2 * N_CMP], vecs("ck2", m * P, P), HS[:, 0, m, :], start=(m == 0), stop=(m == 1))
                    mm.then_inc(mx_c2, 1)
                if name == "V2":
                    pe.wait_ge(mx_ksq, 1)
                    nc.tensor.matmul(A[4][:, 0:2 * N_CMP], ONES, KCR[:, 1, :], start=True, stop=True).then_inc(mx_kss, 1)
                    for n4 in range(4):
                        pe.wait_ge(mx_ksq, 2 + n4)
                        mm = nc.tensor.matmul(A[n4 // 2][:, (n4 % 2) * T:(n4 % 2 + 1) * T], ONES, SQ[:, n4 % 2, :],
                                              start=True, stop=True).then_inc(mx_kss, 1)
            pe.wait_ge(mx_hs, 2)
            for head in range(2):
                for m in range(2):
                    mm = nc.tensor.matmul(A[5][0:N_CMP, head * P:(head + 1) * P], HS[:, 1, m, head * N_CMP:(head + 1) * N_CMP],
                                          vecs("cv2", m * P, P), start=(m == 0), stop=(m == 1))
            mm.then_inc(mx_c2, 1)
            taken(pe, mixa_result("vw1"))
            for n4 in range(4):
                for tt in range(2):
                    tr = nc.tensor.transpose(A[2 + n4 // 2][:, ((n4 % 2) * 2 + tt) * P:((n4 % 2) * 2 + tt + 1) * P],
                                             VF4[:, n4, tt * P:(tt + 1) * P], IDENT)
            tr.then_inc(mx_vtr, 1)
            pe.wait_ge(mx_gf, 1)
            pe.wait_ge(mx_kln, 1)
            for tt in range(2):
                tr = nc.tensor.transpose(A[4][:, 32 * tt:32 * tt + 24], GF[0:24, tt * P:(tt + 1) * P], IDENT[0:24, 0:24])
            tr.then_inc(mx_gtr, 1)

        def vecs(name, a, n, rows=slice(0, P)):
            return VEC[rows, V_AT[name] + a:V_AT[name] + a + n]

        def mixa_act(act):
            def windows(kv):
                for head in range(2):
                    n = 2 * kv + head
                    act.wait_ge(mx_bt, n + 1)
                    nc.scalar.activation(BLH[:, kv, :, head * N_CMP:(head + 1) * N_CMP], BT[:, head], ACT.Copy).then_inc(mx_bh, 1)

            for n, name in enumerate(MIXA):
                c = At(C_MIXA + n)
                split_hi(act, c + 2)
                if name in ("V0", "vw1"):
                    kv = int(name == "vw1")
                    wait(act, mm_done, mixa_chunk("KV"[kv] + "3") + 1)
                    nc.scalar.activation(HT[0:2 * N_CMP, kv, :], A[2 * kv][0:2 * N_CMP, 0:2 * P], ACT.Silu).then_inc(mx_ht, 1)
                if name in raw_tiles:
                    buf, k = raw_tiles[name]
                    wait(act, mm_done, c + 1)
                    r = mixa_result(name)
                    nc.scalar.activation(buf[:, k, :], gres(r), ACT.Copy).then_inc(g_free[r.slot(NG)], 1)
                if name == "kc1":
                    windows(0)
                    act.wait_ge(s_mem, 16)
                    act.wait_ge(h_ready, H_MIX + 4)
                if name in squares_after:
                    g = squares_after.index(name)
                    wait(act, n_ss, norm_mem.sq(GRP * (g - 1)) if g > 1 else 0)
                    nc.scalar.activation(HN[:, g % 2], MB[:, g * GRP:(g + 1) * GRP, :], ACT.Square).then_inc(n_sq, GRP)
                if name == "K1":
                    act.wait_ge(n_ss, norm_mem.sq(KT))
                    nc.scalar.activation(LR[:], A[5][:, 0:T], ACT.Ln, bias=EPSC, scale=1.0 / D).then_inc(mx_mr, 1)
                    act.wait_ge(mx_mr, 1)
                    nc.scalar.activation(RM[:], LR[:], ACT.Exp, scale=-0.5).then_inc(mx_mr, 1)
                if name == "vc1":
                    windows(1)
                if name in ("V1", "gate"):
                    kv = int(name == "gate")
                    act.wait_ge(mx_ht, 2 * kv + 2)
                    nc.scalar.activation(HS[:, kv], A[2 * kv + 1][:, 0:64].rearrange("p (m n) -> p m n", m=2)[:, :, 0:2 * N_CMP],
                                         ACT.Copy).then_inc(mx_hs, 1)
                if name == "kw1":
                    act.wait_ge(mx_c2, 1)
                    nc.scalar.activation(KCR[:, 0, :], A[4][:, 0:2 * N_CMP], ACT.Copy).then_inc(mx_kc, 1)
                    act.wait_ge(mx_kc, 1)
                    nc.scalar.activation(KCR[:, 1, :], KCR[:, 0, :], ACT.Square).then_inc(mx_ksq, 1)
                if name == "kw1":
                    for n4, t in enumerate(("ks0", "ks1", "kw0", "kw1")):
                        taken(act, mixa_result(t))
                        wait(act, mx_kss, n4)
                        nc.scalar.activation(SQ[:, n4 % 2, :], KN[:, n4, :], ACT.Square).then_inc(mx_ksq, 1)
            r = mixa_result("gate")
            wait(act, mm_done, mixa_chunk("gate") + 1)
            nc.scalar.activation(GF[0:24, :], G[0:24, r.slot(NG), 0:T], ACT.Sigmoid, bias=vec("b_gate", 0, 24)).then_inc(mx_gf, 1)
            nc.scalar.activation(AL[32:48, :], G[32:48, r.slot(NG), 0:T], ACT.Copy).then_inc(g_free[r.slot(NG)], 1)
            act.wait_ge(mx_kss, 5)
            nc.scalar.activation(KCR[:, 1, :], A[4][:, 0:2 * N_CMP], ACT.Ln, bias=EPSC, scale=1.0 / P).then_inc(mx_kln, 1)
            for b in range(2):
                nc.scalar.activation(LK[:, 2 * b:2 * b + 2, :], A[b][:].rearrange("p (a t) -> p a t", a=2), ACT.Ln, bias=EPSC,
                                     scale=1.0 / P).then_inc(mx_kln, 1)
            act.wait_ge(mx_kln, 3)
            nc.scalar.activation(KCR[:, 1, :], KCR[:, 1, :], ACT.Exp, scale=-0.5).then_inc(mx_krr, 1)
            nc.scalar.activation(LK[:], LK[:], ACT.Exp, scale=-0.5).then_inc(mx_krr, 1)

        def mixa_dve(dve):
            nc.vector.memset(VC[:], 0.0).then_inc(mx_zero, 1)
            nc.vector.memset(PTC[:], 0.0).then_inc(mx_zero, 1)

            def windows(kv):
                for head in range(2):
                    n = 2 * kv + head
                    taken(dve, mixa_result("kv"[kv] + f"c{head}"))
                    wait(dve, mx_bl, n - 1)
                    u = UC[:, 2 * kv + head, :]
                    view = bass.AP(tensor=u.tensor, offset=u.offset, ap=[list(u.ap[0]), [1, CMP_LEN], [CMP_STRIDE, N_CMP]])
                    pe_ = vecs("pe_k" if kv == 0 else "pe_v", 0, CMP_LEN).unsqueeze(2).broadcast_to([P, CMP_LEN, N_CMP])
                    nc.vector.tensor_tensor(BT[:, head], view, pe_, ALU.add).then_inc(mx_bt, 1)
                    dve.wait_ge(mx_bh, n + 1)
                    dst = slice(head * N_CMP, (head + 1) * N_CMP)
                    nc.vector.tensor_tensor(BLL[:, kv, :, dst], BT[:, head], BLH[:, kv, :, dst].bitcast(F32), ALU.subtract).then_inc(mx_bl, 1)

            for n, name in enumerate(MIXA):
                split_lo(dve, At(C_MIXA + n + 2))
                if name == "kc1":
                    windows(0)
                if name == "vc1":
                    windows(1)
                if name in ("V0", "kw0", "V1", "kw1"):
                    g = ("V0", "kw0", "V1", "kw1").index(name)
                    dve.wait_ge(mx_mr, 2)
                    for k in range(g * GRP, (g + 1) * GRP):
                        ins = nc.vector.scalar_tensor_tensor(MB[:, k, :], MB[:, k, :], vec("g_mem", k), RM[:], ALU.mult, ALU.mult)
                    ins.then_inc(n_hn, 1)
            dve.wait_ge(mx_c2, 2)
            nc.vector.tensor_copy(VC[0:N_CMP, :, :], A[5][0:N_CMP, 0:2 * P].rearrange("p (a m) -> p a m", a=2)).then_inc(mx_vc, 1)
            dve.wait_ge(mx_vtr, 1)
            for b in range(2):
                nc.vector.tensor_copy(VW[:, 2 * b:2 * b + 2, :, :].rearrange("p a t m -> p (a t m)"), A[2 + b][:]).then_inc(mx_vw, 1)
            dve.wait_ge(mx_gtr, 1)
            for tt in range(2):
                nc.vector.tensor_copy(GT[:, tt, :], A[4][:, 32 * tt:32 * tt + 24]).then_inc(mx_gt, 1)
            dve.wait_ge(mx_gt, 2)
            nc.vector.tensor_scalar(GT[:, 0, 0:24:3], GT[:, 0, 0:24:3], con("rowok"), None, ALU.mult).then_inc(mx_gt, 1)
            dve.wait_ge(mx_krr, 2)
            nc.vector.scalar_tensor_tensor(KC[:], KCR[:, 0, :], vec("g_kc"), KCR[:, 1, :], ALU.mult, ALU.mult).then_inc(mx_kn, 1)
            for n4 in range(4):
                nc.vector.scalar_tensor_tensor(KN[:, n4, :], KN[:, n4, :], vec("g_ks" if n4 < 2 else "g_kw"), LK[:, n4, :],
                                               ALU.mult, ALU.mult).then_inc(mx_kn, 1)

        (ns_sqq, ns_ssq, ns_lq, ns_rq, ns_qn, ns_s, ns_st, ns_nm, ns_e, ns_p, ns_tr, ns_pta, ns_ptd, ns_o, ns_sqo, ns_sso,
         ns_lo, ns_ro, ns_y) = (
            sem(f"ns_{s}") for s in ("sqq", "ssq", "lq", "rq", "qn", "s", "st", "nm", "e", "p", "tr", "pta", "ptd", "o", "sqo",
                                     "sso", "lo", "ro", "y"))
        NS_STEPS = 6

        def mixb_chunk(j, m):
            return j.times(4) + (C_MIXB + m)

        def mixb_result(j, m):
            return j.times(4) + (R_MIXB + m)

        def mixb_pe(pe):
            def turn(p):
                wait(pe, ns_p, p + 1)
                wait(pe, ns_pta, p)
                wait(pe, ns_ptd, p)
                for b in range(2):
                    nc.tensor.transpose(A[2 + b][:, 0:P], PB[:, 0, b * P:(b + 1) * P], IDENT)
                    for tt in range(2):
                        nc.tensor.transpose(A[2 + b][:, (1 + tt) * P:(2 + tt) * P], PB[:, 1, b * T + tt * P:b * T + (tt + 1) * P], IDENT)
                    tr = nc.tensor.transpose(A[2 + b][0:N_CMP, 3 * P:4 * P], PB[:, b, 512:512 + N_CMP], IDENT)
                tr.then_inc(ns_tr, 1)

            def values(p, kvh):
                wait(pe, ns_pta, p + 1)
                wait(pe, ns_ptd, p + 1)
                wait(pe, ns_y, p)
                o, o1 = A[5][:, 0:T], A[5][:, P:T]
                nc.tensor.matmul(o, VW[:, kvh, 0, :], PTS[:, 0:T], start=True, stop=False)
                nc.tensor.matmul(o1, VW[:, kvh, 1, :], PTS[:, T:T + P], start=False, stop=False)
                nc.tensor.matmul(o1, VW[:, 2 + kvh, 1, :], PTW[:, T:T + P], start=False, stop=False)
                nc.tensor.matmul(o, VC[:, kvh, :], PTC[:], start=False, stop=False)
                nc.tensor.matmul(o, VW[:, 2 + kvh, 0, :], PTW[:, 0:T], start=False, stop=True).then_inc(ns_o, 1)

            def sum_q(j):
                wait(pe, ns_sqq, j + 1)
                wait(pe, ns_lo, j - 1)
                nc.tensor.matmul(A[4][:, 0:T], ONES, SQ[:, 0, :], start=True, stop=True).then_inc(ns_ssq, 1)

            def sum_o(p, j):
                wait(pe, ns_sqo, p + 1)
                wait(pe, ns_lq, j)
                nc.tensor.matmul(A[4][:, T:2 * T], ONES, SQ[:, 1, :], start=True, stop=True).then_inc(ns_sso, 1)

            def scores(j, kvh):
                wait(pe, ns_qn, j + 1)
                wait(pe, ns_nm, j)
                for tt in range(2):
                    q = QN[:, tt * P:(tt + 1) * P]
                    n = P * (tt + 1)
                    nc.tensor.matmul(A[tt][:, 0:n], q, KN[:, kvh, 0:n], start=True, stop=True)
                    nc.tensor.matmul(A[tt][:, n:2 * n], q, KN[:, 2 + kvh, 0:n], start=True, stop=True)
                    mm = nc.tensor.matmul(A[0][:, T + 16 * tt:T + 16 * tt + N_CMP], q, KC[:, kvh * N_CMP:(kvh + 1) * N_CMP],
                                          start=True, stop=True)
                mm.then_inc(ns_s, 1)

            def head(j, p, kvh, kvp):
                gemm(pe, mixb_chunk(j, 0), mixb_result(j, 0))
                if p:
                    turn(p)
                gemm(pe, mixb_chunk(j, 1), mixb_result(j, 1))
                if p:
                    values(p, kvp)
                sum_q(j)
                gemm(pe, mixb_chunk(j, 2), mixb_result(j, 2))
                if p:
                    sum_o(p, j + 1)
                scores(j, kvh)
                gemm(pe, mixb_chunk(j, 3), mixb_result(j, 3))

            pe.wait_ge(mx_kn, 5)
            pe.wait_ge(mx_vw, 2)
            pe.wait_ge(mx_vc, 1)
            pe.wait_ge(mx_gt, 2)
            for kvh in range(2):
                head(At(4 * kvh), At(3) if kvh else None, kvh, 0)
                with pe.Fori(4 * kvh + 1, 4 * kvh + 4) as i:
                    head(At(0, 1, i), At(-1, 1, i), kvh, kvh)
            turn(At(7))
            values(At(7), 1)
            sum_o(At(7), 8)

        def mixb_act(act):
            def other(j, m):
                r = mixb_result(j, m)
                wait(act, mm_done, mixb_chunk(j, m) + 1)
                nc.scalar.activation(tile(OTH, j.times(3) + (m - 1)), gres(r), ACT.Copy).then_inc(g_free[r.slot(NG)], 1)

            def turned(p):
                wait(act, ns_tr, p + 1)
                wait(act, ns_o, p)
                nc.scalar.activation(PTS[:], A[2][:, 0:384], ACT.Copy)
                nc.scalar.activation(PTC[0:N_CMP, 0:P], A[2][0:N_CMP, 384:512], ACT.Copy).then_inc(ns_pta, 1)

            def square_o(p):
                wait(act, ns_o, p + 1)
                nc.scalar.activation(SQ[:, 1, :], A[5][:, 0:T], ACT.Square).then_inc(ns_sqo, 1)

            def root(src, ln, lbuf, rr, rbuf, n, bias):
                nc.scalar.activation(lbuf, src, ACT.Ln, bias=EPSC, scale=1.0 / P).then_inc(ln, 1)
                wait(act, ln, n + 1)
                nc.scalar.activation(rbuf, lbuf, ACT.Exp, scale=-0.5, bias=bias).then_inc(rr, 1)

            def root_o(p):
                wait(act, ns_sso, p + 1)
                wait(act, ns_y, p)
                root(A[4][:, T:2 * T], ns_lo, LO2[:], ns_ro, RO[:], p, 0.0)

            def head(j, p):
                c = mixb_chunk(j, 0)
                r = mixb_result(j, 0)
                split_hi(act, c + 2)
                if p:
                    other(p, 3)
                split_hi(act, c + 3)
                wait(act, mm_done, c + 1)
                wait(act, ns_qn, j)
                nc.scalar.activation(QCN[:], gres(r), ACT.Copy).then_inc(g_free[r.slot(NG)], 1)
                taken(act, r)
                wait(act, ns_ssq, j)
                nc.scalar.activation(SQ[:, 0, :], QCN[:], ACT.Square).then_inc(ns_sqq, 1)
                if p:
                    turned(p)
                split_hi(act, c + 4)
                other(j, 1)
                wait(act, ns_ssq, j + 1)
                wait(act, ns_rq, j)
                root(A[4][:, 0:T], ns_lq, LR[:], ns_rq, RR[:], j, con("lnsc"))
                if p:
                    square_o(p)
                split_hi(act, c + 5)
                other(j, 2)
                if p:
                    root_o(p)
                wait(act, ns_nm, j + 1)
                wait(act, ns_p, j)
                for tt in range(2):
                    n = P * (tt + 1)
                    for b, w in enumerate((slice(512, 512 + N_CMP), slice(0, n), slice(n, 2 * n))):
                        e = nc.scalar.activation(PB[:, tt, w], PB[:, tt, w], ACT.Exp, bias=NM[:, tt, b:b + 1], accum_out=SL[:, tt, b:b + 1])
                e.then_inc(ns_e, 1)

            for kvh in range(2):
                head(At(4 * kvh), At(3) if kvh else None)
                with act.Fori(4 * kvh + 1, 4 * kvh + 4) as i:
                    head(At(0, 1, i), At(-1, 1, i))
            last = At(7)
            other(last, 3)
            turned(last)
            square_o(last)
            root_o(last)

        def mixb_dve(dve):
            def turned(p):
                wait(dve, ns_tr, p + 1)
                wait(dve, ns_o, p)
                nc.vector.tensor_copy(PTW[:], A[3][:, 0:384])
                nc.vector.tensor_copy(PTC[0:N_CMP, P:T], A[3][0:N_CMP, 384:512]).then_inc(ns_ptd, 1)

            def finish(p):
                wait(dve, ns_ro, p + 1)
                nc.vector.scalar_tensor_tensor(tile(YN, p), A[5][:, 0:T], vec("g_nsa"), RO[:], ALU.mult, ALU.mult).then_inc(ns_y, 1)

            def softmax(j, st):
                slope = con_at("slope", j)
                wait(dve, ns_s, j + 1)
                wait(dve, ns_tr, j)
                for tt in range(2):
                    n2 = 2 * P * (tt + 1)
                    nc.vector.scalar_tensor_tensor(PB[:, tt, 0:n2], con(f"dist{tt}"), slope, A[tt][:, 0:n2], ALU.mult, ALU.add)
                    k = st.done(nc.vector.scalar_tensor_tensor(PB[:, tt, 512:512 + N_CMP], con("distc", 16 * tt, 16 * tt + N_CMP), slope,
                                                               A[0][:, T + 16 * tt:T + 16 * tt + N_CMP], ALU.mult, ALU.add))
                st.wait(k)
                for tt in range(2):
                    n = P * (tt + 1)
                    nc.vector.tensor_reduce(MX[:, tt, 1:3], PB[:, tt, 0:2 * n].rearrange("p (b n) -> p b n", b=2), AX_X, ALU.max)
                    k = st.done(nc.vector.tensor_reduce(MX[:, tt, 0:1], PB[:, tt, 512:512 + N_CMP], AX_X, ALU.max))
                st.wait(k)
                nc.vector.tensor_scalar(NM[:], MX[:], -1.0, None, ALU.mult).then_inc(ns_nm, 1)

            def weigh(j, st):
                wait(dve, ns_e, j + 1)
                st.link(nc.vector.reciprocal(RC[:], SL[:]))
                v = j.v
                gates = GT[:, :, 3 * v:3 * v + 3] if isinstance(v, int) else GT[:, :, bass.ds(v * 3, 3)]
                st.link(nc.vector.tensor_tensor(CF[:], RC[:], gates, ALU.mult))
                for tt in range(2):
                    n = P * (tt + 1)
                    for b, w in enumerate((slice(512, 512 + N_CMP), slice(0, n), slice(n, 2 * n))):
                        ins = nc.vector.tensor_scalar(PB[:, tt, w], PB[:, tt, w], CF[:, tt, b:b + 1], None, ALU.mult)
                ins.then_inc(ns_p, 1)

            def head(j, p, st):
                c = mixb_chunk(j, 0)
                split_lo(dve, c + 2)
                split_lo(dve, c + 3)
                if p:
                    turned(p)
                split_lo(dve, c + 4)
                wait(dve, ns_rq, j + 1)
                wait(dve, ns_s, j)
                nc.vector.scalar_tensor_tensor(QN[:], QCN[:], vec("g_q"), RR[:], ALU.mult, ALU.mult).then_inc(ns_qn, 1)
                split_lo(dve, c + 5)
                if p:
                    finish(p)
                softmax(j, st)
                weigh(j, st)
                st.end()

            dve.wait_ge(mx_gt, 3)
            for kvh in range(2):
                head(At(4 * kvh), At(3) if kvh else None, Steps(dve, ns_st, 0, 0, 4 * kvh * NS_STEPS))
                with dve.Fori(4 * kvh + 1, 4 * kvh + 4) as i:
                    head(At(0, 1, i), At(-1, 1, i), Steps(dve, ns_st, NS_STEPS, i))
            turned(At(7))
            finish(At(7))

        def con_at(name, a):
            v = a.v
            return con(name, v, v + 1) if isinstance(v, int) else CON[:, bass.ds(v + K_AT[name], 1)]

        at = Layout(AFTER_OTH)
        GQT = at("GQT", [P, 2, T])
        GA = at("GA", [P, T])
        GL = RM
        GB = at("GB", [P, T])
        GD = at("GD", [P, T])
        GE = at("GE", [P, T])
        GM = at("GM", [P, 2, NCH, 3])
        GKD = at("GKD", [P, T])
        GKX = at("GKX", [P, 2, P])
        GVT = at("GVT", [P, 2, 2, P])
        GSM = at("GSM", [P, 2, T])
        GST = at("GST", [P, 2 * P])
        GSP = at("GSP", [P, 3, 2 * P])
        GO = at("GO", [P, 2, T])
        GSD = GO[:, 0, :]
        assert at.at <= nc.sbuf_usable_end // 32 * 32 - 2 * T * 4, at.at

        (gl_gk, gl_t, gl_ab, gl_ex, gl_ln, gl_la, gl_sc, gl_db, gl_exp, gl_ek, gl_qt, gl_tr, gl_s, gl_kx, gl_vt, gl_sm, gl_kv, gl_step,
         gl_st, gl_o, gl_sq, gl_ss, gl_lr, gl_rr, gl_og, gl_y, gl_r, mk_sq, mk_ss, mk_ln, mk_rr, mk_ck, mk_tr, mk_cv, my_hh, gl_zero) = (
            sem(s) for s in ("gl_gk gl_t gl_ab gl_ex gl_ln gl_la gl_sc gl_db gl_exp gl_ek gl_qt gl_tr gl_s gl_kx gl_vt gl_sm gl_kv gl_step "
                             "gl_st gl_o gl_sq gl_ss gl_lr gl_rr gl_og gl_y gl_r mk_sq mk_ss mk_ln mk_rr mk_ck mk_tr mk_cv my_hh gl_zero").split())
        norm_cross = Norm("g_cross", H_CROSS, C_CQ - 1, 5)
        CK = OTH[:, 0:4, :]
        CVR = OTH[:, 4:8, :]
        CVT = OTH[:, 8:12, :].rearrange("p h (t m) -> p h t m", t=2)
        CL = OTH[:, 12:16, :]

        def gla_product(s):
            return A[3][:, (s // 2) * T:(s // 2 + 1) * T] if s % 2 == 0 else A[4][:, T:2 * T]

        def gla_pe(pe):
            def gate(h):
                wait(pe, gl_t, h)
                wait(pe, gl_sm, h)
                nc.tensor.matmul(A[0][:, T:2 * T], vecs("gk2", h * P, P, slice(32, 48)), AL[32:48, :], start=True, stop=True).then_inc(gl_gk, 1)

            def turn(h):
                wait(pe, gl_qt, h + 1)
                wait(pe, gl_rr, h - 1)
                for tt in range(2):
                    w = slice(tt * P, (tt + 1) * P)
                    nc.tensor.transpose(A[1][:, w], GKD[:, w], IDENT)
                    for m in range(2):
                        tr = nc.tensor.transpose(A[2][:, (2 * tt + m) * P:(2 * tt + m + 1) * P], OTH[:, 8 + 2 * h + m, w], IDENT)
                tr.then_inc(gl_tr, 1)
                for tt in range(2):
                    w = slice(tt * P, (tt + 1) * P)
                    mm = nc.tensor.matmul(A[0][:, w], GKD[:, w], GQT[:, h % 2, w], start=True, stop=True)
                mm.then_inc(gl_s, 1)

            def kv(h):
                wait(pe, gl_kx, h + 1)
                wait(pe, gl_vt, h + 1)
                wait(pe, gl_st, h)
                for s in range(3):
                    rows = slice((s % 2) * CH, (s % 2) * CH + CH)
                    mm = nc.tensor.matmul(gla_product(s), GKX[rows, s // 2, :], GVT[rows, s // 2, :, :].rearrange("p m n -> p (m n)"),
                                          start=True, stop=True)
                mm.then_inc(gl_kv, 1)

            def output(h):
                wait(pe, gl_sm, h + 1)
                wait(pe, gl_st, h + 1)
                wait(pe, gl_og, h)
                for m in range(2):
                    o = A[5][:, m * T:(m + 1) * T]
                    nc.tensor.matmul(o, GVT[:, 0, m, :], GSM[:, 0, :], start=True, stop=False)
                    for c in range(1, NCH):
                        nc.tensor.matmul(A[5][:, m * T + c * CH:m * T + (c + 1) * CH], GSP[:, c - 1, m * P:(m + 1) * P],
                                         GQT[:, h % 2, c * CH:(c + 1) * CH], start=False, stop=False)
                    mm = nc.tensor.matmul(o, GVT[:, 1, m, :], GSM[:, 1, :], start=False, stop=True)
                mm.then_inc(gl_o, 1)

            def sums(h):
                wait(pe, gl_sq, h + 1)
                wait(pe, gl_kx, min(h + 2, MEMH))
                for m in range(2):
                    mm = nc.tensor.matmul(A[1][:, T:2 * T], ONES, SQ[:, m, :], start=(m == 0), stop=(m == 1))
                mm.then_inc(gl_ss, 1)

            pe.wait_ge(ns_nm, 8)
            gate(0)
            pe.wait_ge(ns_lo, 8)
            for h in range(MEMH):
                if h:
                    gemm(pe, At(C_MEM + 2 * h), At(R_MEM + 2 * h))
                else:
                    gemm_two(pe, At(C_MEM), At(R_MEM), H_MEM)
                if h:
                    output(h - 1)
                turn(h)
                if h:
                    sums(h - 1)
                if h:
                    gemm(pe, At(C_MEM + 2 * h + 1), At(R_MEM + 2 * h + 1))
                kv(h)
                if h + 1 < MEMH:
                    gate(h + 1)
            output(MEMH - 1)
            sums(MEMH - 1)

        def memory_pe(pe):
            wait(pe, mk_sq, 1)
            wait(pe, gl_rr, MEMH)
            for h in range(MEMH):
                mm = nc.tensor.matmul(A[h // 2][:, (h % 2) * T:(h % 2 + 1) * T], ONES, CL[:, h, :], start=True, stop=True)
            mm.then_inc(mk_ss, 1)
            for h in range(MEMH):
                for tt in range(2):
                    tr = nc.tensor.transpose(A[2 + h // 2][:, ((h % 2) * 2 + tt) * P:((h % 2) * 2 + tt + 1) * P],
                                             CVR[:, h, tt * P:(tt + 1) * P], IDENT)
            tr.then_inc(mk_tr, 1)

        def gla_act(act):
            def gates(h):
                wait(act, gl_t, h + 1)
                wait(act, gl_la, h)
                nc.scalar.activation(GL[:], GA[:], ACT.Abs).then_inc(gl_ab, 1)
                wait(act, gl_ab, h + 1)
                nc.scalar.activation(GL[:], GL[:], ACT.Exp, scale=-1.0).then_inc(gl_ex, 1)
                wait(act, gl_ex, h + 1)
                nc.scalar.activation(GL[:], GL[:], ACT.Ln, bias=1.0).then_inc(gl_ln, 1)

            def decays(h):
                wait(act, gl_db, h + 1)
                wait(act, gl_st, h - 1)
                b = GB[:].rearrange("p (c n) -> p c n", c=NCH)
                d = GD[:].rearrange("p (c n) -> p c n", c=NCH)
                nc.scalar.activation(GE[:], GD[:], ACT.Exp, scale=1.0 / 16)
                nc.scalar.activation(GM[:, h % 2, :, 0:2], b[:, :, CH // 2 - 1::CH // 2], ACT.Exp, scale=1.0 / 16)
                nc.scalar.activation(GM[:, h % 2, :, 2:3], d[:, :, CH - 1:CH], ACT.Exp, scale=1.0 / 16).then_inc(gl_exp, 1)
                wait(act, gl_exp, h + 1)
                nc.scalar.activation(GD[:], GD[:], ACT.Exp, scale=-1.0 / 16).then_inc(gl_ek, 1)

            def keep(h, m):
                r = At(R_MEM + 2 * h + m)
                wait(act, mm_done, C_MEM + 2 * h + m + 1)
                wait(act, gl_qt, h + 1)
                nc.scalar.activation(OTH[:, 4 * m + h, :], gres(r), ACT.Copy).then_inc(g_free[r.slot(NG)], 1)

            def square(h):
                wait(act, gl_o, h + 1)
                wait(act, gl_ss, h)
                nc.scalar.activation(SQ[:], A[5][:].rearrange("p (m t) -> p m t", m=2), ACT.Square).then_inc(gl_sq, 1)

            def root(h):
                wait(act, gl_ss, h + 1)
                wait(act, gl_og, h)
                nc.scalar.activation(LR[:], A[1][:, T:2 * T], ACT.Ln, bias=EPSC, scale=1.0 / T).then_inc(gl_lr, 1)
                wait(act, gl_lr, h + 1)
                nc.scalar.activation(RR[:], LR[:], ACT.Exp, scale=-0.5).then_inc(gl_rr, 1)

            act.wait_ge(n_hn, norm_mem.hn(KT // GRP))
            act.wait_ge(mm_done, C_MEM)
            for g in range(KT // GRP):
                nc.scalar.activation(HH[:, g * GRP:(g + 1) * GRP, :], MB[:, g * GRP:(g + 1) * GRP, :], ACT.Copy).then_inc(n_hh, 1)
            taken(act, mixb_result(At(7), 3))
            nc.scalar.activation(OTH[:, 16:24, :], OTH[:, 16:24, :], ACT.Silu).then_inc(gl_r, 1)
            gates(0)
            decays(0)
            for h in range(MEMH):
                split_hi(act, At(C_MEM + 2 * h + 2))
                keep(h, 0)
                wait(act, gl_tr, h + 1)
                nc.scalar.activation(GVT[:], A[2][:].rearrange("p (t m n) -> p t m n", t=2, m=2), ACT.Copy).then_inc(gl_vt, 1)
                if h:
                    square(h - 1)
                split_hi(act, At(C_MEM + 2 * h + 3))
                keep(h, 1)
                if h:
                    root(h - 1)
                if h + 1 < MEMH:
                    gates(h + 1)
                    decays(h + 1)
            high_mix(0)
            high_mix(1)
            square(MEMH - 1)
            root(MEMH - 1)
            taken(act, At(R_MEM + 2 * MEMH - 2))
            taken(act, At(R_MEM + 2 * MEMH - 1))
            wait(act, gl_tr, MEMH)
            nc.scalar.activation(CL, CK, ACT.Square).then_inc(mk_sq, 1)
            for g in range(2, KT // GRP):
                high_mix(g)

        def high_mix(g):
            if g == 0:
                nc.scalar.wait_ge(mm_done, C_MIXO)
            if g == 2:
                nc.scalar.wait_ge(gl_y, 2 * MEMH)
            nc.scalar.activation(HH[:, g * GRP:(g + 1) * GRP, :], mix_source(g), ACT.Copy).then_inc(my_hh, 1)

        def memory_act(act):
            wait(act, mk_ss, 1)
            for b in range(2):
                nc.scalar.activation(CL[:, 2 * b:2 * b + 2, :], A[b][:].rearrange("p (a t) -> p a t", a=2), ACT.Ln, bias=EPSC,
                                     scale=1.0 / P).then_inc(mk_ln, 1)
            act.wait_ge(mk_ln, 2)
            nc.scalar.activation(CL, CL, ACT.Exp, scale=-0.5).then_inc(mk_rr, 1)

        def mix_source(g):
            return YN[:, g * GRP:(g + 1) * GRP, :] if g < 2 else OTH[:, 8 + g * GRP:8 + (g + 1) * GRP, :]

        def gla_dve(dve):
            def gates(h):
                wait(dve, gl_gk, h + 1)
                wait(dve, gl_sc, h)
                nc.vector.tensor_scalar(GA[:], A[0][:, T:2 * T], vec("b_gk", h), None, ALU.add).then_inc(gl_t, 1)

            def decays(h):
                wait(dve, gl_ln, h + 1)
                nc.vector.scalar_tensor_tensor(GA[:], GA[:], 0.0, GL[:], ALU.min, ALU.subtract).then_inc(gl_la, 1)
                wait(dve, gl_la, h + 1)
                wait(dve, gl_exp, h)
                nc.vector.tensor_tensor_scan(GB[:], con("keep", 0, T), GA[:], 0.0, ALU.mult, ALU.add).then_inc(gl_sc, 1)
                wait(dve, gl_sc, h + 1)
                wait(dve, gl_qt, h)
                b = GB[:].rearrange("p (c n) -> p c n", c=NCH)
                nc.vector.tensor_tensor(GD[:].rearrange("p (c n) -> p c n", c=NCH), b,
                                        b[:, :, CH // 2 - 1:CH // 2].broadcast_to([P, NCH, CH]), ALU.subtract).then_inc(gl_db, 1)

            def decayed(h):
                wait(dve, gl_ek, h + 1)
                wait(dve, gl_o, h - 1)
                wait(dve, gl_s, h)
                nc.vector.scalar_tensor_tensor(GQT[:, h % 2, :], OTH[:, h, :], ATT_SCALE, GE[:], ALU.mult, ALU.mult)
                nc.vector.tensor_tensor(GKD[:], OTH[:, 4 + h, :], GD[:], ALU.mult).then_inc(gl_qt, 1)

            def turned(h):
                wait(dve, gl_tr, h + 1)
                nc.vector.tensor_copy(GKX[:], A[1][:, 0:T].rearrange("p (t m) -> p t m", t=2)).then_inc(gl_kx, 1)
                wait(dve, gl_s, h + 1)
                wait(dve, gl_o, h)
                for tt in range(2):
                    w = slice(tt * P, (tt + 1) * P)
                    ins = nc.vector.scalar_tensor_tensor(GSM[:, tt, w], A[0][:, w], BIG, con("tri", tt * P, (tt + 1) * P), ALU.min, ALU.mult)
                ins.then_inc(gl_sm, 1)

            def states(h, st):
                wait(dve, gl_kv, h + 1)
                wait(dve, gl_o, h)
                wait(dve, gl_y, 2 * (h - 1))
                e = GM[:, h % 2]
                for s in range(3):
                    if s == 0:
                        st.link(nc.vector.tensor_scalar(GST[:], gla_product(0), e[:, 0, 2:3], None, ALU.mult))
                    else:
                        st.link(nc.vector.tensor_scalar(GSD, GST[:], e[:, s, 1:2], None, ALU.mult))
                        st.link(nc.vector.scalar_tensor_tensor(GST[:], gla_product(s), e[:, s, 2:3], GSD, ALU.mult, ALU.add))
                    ins = nc.vector.tensor_scalar(GSP[:, s, :], GST[:], e[:, s + 1, 0:1], None, ALU.mult)
                    if s == 2:
                        ins.then_inc(gl_st, 1)
                    else:
                        st.link(ins)

            def finish(h):
                wait(dve, gl_rr, h + 1)
                wait(dve, gl_y, 2 * h)
                for m in range(2):
                    ins = nc.vector.scalar_tensor_tensor(GO[:, m, :], A[5][:, m * T:(m + 1) * T], vec("g_gla", m), RR[:], ALU.mult, ALU.mult)
                ins.then_inc(gl_og, 1)
                wait(dve, gl_og, h + 1)
                for m in range(2):
                    r = OTH[:, 16 + 2 * h + m, :]
                    nc.vector.tensor_tensor(r, r, GO[:, m, :], ALU.mult).then_inc(gl_y, 1)

            for g in range(KT // GRP):
                lo_part(dve, n_hh, MB[:, g * GRP:(g + 1) * GRP, :], g, norm_mem.hn(0))
            for tt in range(2):
                nc.vector.memset(GSM[:, tt, (1 - tt) * P:(2 - tt) * P], 0.0).then_inc(gl_zero, 1)
            dve.wait_ge(gl_zero, 2)
            st = Steps(dve, gl_step)
            gates(0)
            decays(0)
            decayed(0)
            dve.wait_ge(gl_r, 1)
            for h in range(MEMH):
                split_lo(dve, At(C_MEM + 2 * h + 2))
                turned(h)
                split_lo(dve, At(C_MEM + 2 * h + 3))
                if h + 1 < MEMH:
                    gates(h + 1)
                states(h, st)
                if h:
                    finish(h - 1)
                if h + 1 < MEMH:
                    decays(h + 1)
                    decayed(h + 1)
            for g in range(2):
                lo_part(dve, my_hh, mix_source(g), g)
            finish(MEMH - 1)
            for g in range(2, KT // GRP):
                lo_part(dve, my_hh, mix_source(g), g)

        def memory_dve(dve):
            dve.wait_ge(mk_tr, 1)
            for b in range(2):
                nc.vector.tensor_copy(CVT[:, 2 * b:2 * b + 2, :, :].rearrange("p a t m -> p (a t m)"), A[2 + b][:]).then_inc(mk_cv, 1)
            dve.wait_ge(mk_rr, 1)
            for h in range(MEMH):
                nc.vector.scalar_tensor_tensor(CK[:, h, :], CK[:, h, :], vec("g_ck"), CL[:, h, :], ALU.mult, ALU.mult).then_inc(mk_ck, 1)

        mix_out = Project(C_MIXO, R_MIXO, norm_cross, H_MIXY, aside=(memory_pe, memory_act, memory_dve))

        at = Layout(AFTER_HN)
        QX = at("QX", [P, MEMH, T])
        LX = at("LX", [P, MEMH, T])
        at = Layout(AFTER_OTH)
        PX = at("PX", [P, 2, 2, T])
        PXT = at("PXT", [P, 2, 2, T])
        MX2 = at("MX2", [P, 2, 2])
        NX = at("NX", [P, 2, 2])
        SX = at("SX", [P, 2, 2])
        RX = at("RX", [P, 2, 2])
        (cr_sq, cr_ss, cr_ln, cr_rr, cr_qn, cr_s, cr_mx, cr_nx, cr_e, cr_rx, cr_p, cr_tr, cr_pt, cr_o, cr_hh, cr_x) = (
            sem(f"cr_{s}") for s in "sq ss ln rr qn s mx nx e rx p tr pt o hh x".split())
        norm_ff = Norm("g_ffn", H_FF, C_FF - 1, 0)

        def cross_pe(pe):
            def scores(h):
                wait(pe, cr_qn, h + 1)
                wait(pe, cr_e, h - 1)
                for tt in range(2):
                    mm = nc.tensor.matmul(A[2 + h % 2][:, tt * T:(tt + 1) * T], QX[:, h, tt * P:(tt + 1) * P], CK[:, h, :], start=True, stop=True)
                mm.then_inc(cr_s, 1)

            def turn(h):
                wait(pe, cr_p, h + 1)
                wait(pe, cr_pt, h - 1)
                for tt in range(2):
                    for mt in range(2):
                        tr = nc.tensor.transpose(A[4 + h % 2][:, mt * T + tt * P:mt * T + (tt + 1) * P], PX[:, h % 2, tt, mt * P:(mt + 1) * P], IDENT)
                tr.then_inc(cr_tr, 1)

            def values(h):
                wait(pe, cr_pt, h + 1)
                for mt in range(2):
                    mm = nc.tensor.matmul(A[h // 2][:, (h % 2) * T:(h % 2 + 1) * T], CVT[:, h, mt, :], PXT[:, h % 2, mt, :],
                                          start=(mt == 0), stop=(mt == 1))
                mm.then_inc(cr_o, 1)

            def sums_x(g):
                pe.wait_ge(n_sq, norm_ff.sq(GRP * (g + 1)))
                for k in range(GRP):
                    nc.tensor.matmul(A[norm_ff.bank][:, 0:T], ONES, HN[:, g % 2, k, :], start=(g == 0 and k == 0),
                                     stop=(g * GRP + k == KT - 1), skip_group_check=True).then_inc(n_ss, 1)

            def sums(h):
                wait(pe, cr_sq, h + 1)
                nc.tensor.matmul(A[h // 2][:, (h % 2) * T:(h % 2 + 1) * T], ONES, SQ[:, h % 2, :], start=True, stop=True).then_inc(cr_ss, 1)

            for h in range(MEMH):
                if h == 0:
                    gemm_two(pe, At(C_CQ), At(R_CQ), H_CROSS)
                elif h >= 2:
                    gemm(pe, At(C_CQ + h), At(R_CQ + h))
                if h == 2:
                    sums(0)
                    sums(1)
            pe.wait_ge(mk_ck, MEMH)
            scores(0)
            sums(2)
            scores(1)
            sums(3)
            for h in range(MEMH):
                turn(h)
                if h + 2 < MEMH:
                    scores(h + 2)
                values(h)
            for cc in range(4):
                c = At(C_CO + cc)
                wait(pe, lo_ready, c + 1)
                if cc == 0:
                    pe.wait_ge(h_ready, H_CO + 1)
                wait(pe, cr_x, 2 * (cc - 1))
                for f in range(4):
                    res = A[2 + 2 * (cc % 2) + f // 2][:, (f % 2) * T:(f % 2 + 1) * T]
                    for k in range(4):
                        w = slice((f * 4 + k) * P, (f * 4 + k + 1) * P)
                        nc.tensor.matmul(res, HI[:, c.slot(RING), w], HH[:, k, :], start=(k == 0), stop=False)
                        nc.tensor.matmul(res, HI[:, c.slot(RING), w], HL[:, k, :], start=False, stop=False)
                        mm = nc.tensor.matmul(res, LO[:, c.slot(RING), w], HH[:, k, :], start=False, stop=(k == 3))
                mm.then_inc(mm_done, 1)
                if cc:
                    sums_x(cc - 1)
            sums_x(3)

        def cross_act(act):
            def root(b):
                lx = LX[:, 2 * b:2 * b + 2, :]
                act.wait_ge(cr_ss, 2 * b + 2)
                nc.scalar.activation(lx, A[b][:].rearrange("p (a t) -> p a t", a=2), ACT.Ln, bias=EPSC,
                                     scale=1.0 / P).then_inc(cr_ln, 1)
                act.wait_ge(cr_ln, b + 1)
                nc.scalar.activation(lx, lx, ACT.Exp, scale=-0.5, bias=con("lnsc")).then_inc(cr_rr, 1)

            for h in range(MEMH):
                r = At(R_CQ + h)
                split_hi(act, At(C_CQ + h + 2))
                if h == 2:
                    root(0)
                wait(act, mm_done, C_CQ + h + 1)
                nc.scalar.activation(QX[:, h, :], gres(r), ACT.Copy).then_inc(g_free[r.slot(NG)], 1)
                taken(act, r)
                wait(act, cr_ss, h - 1)
                nc.scalar.activation(SQ[:, h % 2, :], QX[:, h, :], ACT.Square).then_inc(cr_sq, 1)
            root(1)
            for h in range(MEMH):
                wait(act, cr_nx, h + 1)
                wait(act, cr_tr, h - 1)
                for tt in range(2):
                    e = nc.scalar.activation(PX[:, h % 2, tt, :], A[2 + h % 2][:, tt * T:(tt + 1) * T], ACT.Exp,
                                             bias=NX[:, h % 2, tt:tt + 1], accum_out=SX[:, h % 2, tt:tt + 1])
                e.then_inc(cr_e, 1)
                wait(act, cr_tr, h + 1)
                wait(act, cr_o, h - 1)
                nc.scalar.activation(PXT[:, h % 2], A[4 + h % 2][:].rearrange("p (a t) -> p a t", a=2), ACT.Copy).then_inc(cr_pt, 1)
            for b in range(2):
                act.wait_ge(cr_o, 2 * b + 2)
                ins = nc.scalar.activation(HH[:, 2 * b:2 * b + 2, :], A[b][:].rearrange("p (a t) -> p a t", a=2), ACT.Copy)
                ins.then_inc(cr_hh, 1)
            for cc in range(4):
                split_hi(act, At(C_CO + cc + 2))
                wait(act, cr_x, 2 * cc + 2)
                wait(act, n_ss, norm_ff.sq(GRP * (cc - 1)) if cc > 1 else 0)
                nc.scalar.activation(HN[:, cc % 2], X[:, GRP * cc:GRP * (cc + 1), :], ACT.Square).then_inc(n_sq, GRP)

        def cross_dve(dve):
            def scaled(h):
                dve.wait_ge(cr_rr, h // 2 + 1)
                nc.vector.scalar_tensor_tensor(QX[:, h, :], QX[:, h, :], vec("g_cq"), LX[:, h, :], ALU.mult, ALU.mult).then_inc(cr_qn, 1)

            def largest(h):
                wait(dve, cr_s, h + 1)
                wait(dve, cr_nx, h - 1)
                nc.vector.tensor_reduce(MX2[:, h % 2, :], A[2 + h % 2][:].rearrange("p (a t) -> p a t", a=2), AX_X, ALU.max).then_inc(cr_mx, 1)
                wait(dve, cr_mx, h + 1)
                wait(dve, cr_e, h - 1)
                nc.vector.tensor_scalar(NX[:, h % 2, :], MX2[:, h % 2, :], -1.0, None, ALU.mult).then_inc(cr_nx, 1)
            for h in range(3):
                split_lo(dve, At(C_CQ + h + 2))
            scaled(0)
            scaled(1)
            split_lo(dve, At(C_CQ + 5))
            largest(0)
            scaled(2)
            scaled(3)
            for h in range(MEMH):
                if h + 1 < MEMH:
                    largest(h + 1)
                wait(dve, cr_e, h + 1)
                wait(dve, cr_p, h - 1)
                nc.vector.reciprocal(RX[:, h % 2, :], SX[:, h % 2, :]).then_inc(cr_rx, 1)
                wait(dve, cr_rx, h + 1)
                for tt in range(2):
                    ins = nc.vector.tensor_scalar(PX[:, h % 2, tt, :], PX[:, h % 2, tt, :], RX[:, h % 2, tt:tt + 1], None, ALU.mult)
                ins.then_inc(cr_p, 1)
            dve.wait_ge(cr_hh, 2)
            for b in range(2):
                ins = nc.vector.tensor_tensor(HL[:, 2 * b:2 * b + 2, :], A[b][:].rearrange("p (a t) -> p a t", a=2),
                                              HH[:, 2 * b:2 * b + 2, :].bitcast(F32), ALU.subtract)
            ins.then_inc(h_ready, 1)
            for cc in range(4):
                split_lo(dve, At(C_CO + cc + 2))
                wait(dve, mm_done, C_CO + cc + 1)
                for b in range(2):
                    x = X[:, 4 * cc + 2 * b:4 * cc + 2 * b + 2, :]
                    nc.vector.tensor_tensor(x, x, A[2 + 2 * (cc % 2) + b][:].rearrange("p (a t) -> p a t", a=2), ALU.add).then_inc(cr_x, 1)

        at = Layout(AFTER_HN)
        FHI = at("FHI", [P, KT, T], F32R)
        FLO = at("FLO", [P, KT, T], F32R)
        FT = at("FT", [P, 2, T])
        SF = at("SF", [P, 2, T])
        ff_hi, ff_lo = sem("ff_hi"), sem("ff_lo")

        class Part:

            def __init__(self, n, f0, c, r):
                self.n, self.f0, self.c, self.r = n, f0, c, r
                self.down = Project(c + 2 * n, r + 2 * n, None, None, n, (FHI, FLO), f0 + n)

            def loops(self, eng, pair):
                for j in range(2):
                    pair(At(j), j == 0)
                with eng.Fori(1, self.n // 2) as i:
                    for j in range(2):
                        pair(At(j, 2, i), False)

            def pe(self, pe):
                def pair(k, first):
                    c, r = k.times(2) + self.c, k.times(2) + self.r
                    if first and self.f0 == 0:
                        gemm_two(pe, c, r, H_FF)
                    else:
                        gemm(pe, c, r)
                        gemm(pe, c + 1, r + 1)
                self.loops(pe, pair)
                self.down.pe(pe)

            def act(self, act):
                def high(k):
                    taken(act, k.times(2) + (self.r + 1))
                    nc.scalar.activation(tile(FHI, k), FT[:, k.slot(2), :], ACT.Copy).then_inc(ff_hi, 1)

                def pair(k, first):
                    c, r = k.times(2) + self.c, k.times(2) + self.r
                    split_hi(act, c + 2)
                    split_hi(act, c + 3)
                    wait(act, mm_done, c + 1)
                    if not (isinstance(k.v, int) and k.v < 2):
                        taken(act, r - 3)
                    nc.scalar.activation(SF[:, k.slot(2), :], gres(r), ACT.Silu).then_inc(g_free[r.slot(NG)], 1)
                    if not first:
                        high(k - 1)
                self.loops(act, pair)
                high(At(self.n - 1))
                self.down.act(act)

            def dve(self, dve):
                def gated(k):
                    c, r, g = k.times(2) + self.c, k.times(2) + self.r, k + self.f0
                    taken(dve, r)
                    wait(dve, mm_done, c + 2)
                    wait(dve, ff_lo, g - 1)
                    nc.vector.tensor_tensor(FT[:, k.slot(2), :], SF[:, k.slot(2), :], gres(r + 1), ALU.mult).then_inc(g_free[(r + 1).slot(NG)], 1)

                def low(k):
                    g = k + self.f0
                    wait(dve, ff_hi, g + 1)
                    nc.vector.tensor_tensor(tile(FLO, k), FT[:, k.slot(2), :], tile(FHI, k).bitcast(F32), ALU.subtract).then_inc(ff_lo, 1)

                def pair(k, first):
                    c = k.times(2) + self.c
                    split_lo(dve, c + 2)
                    if not first:
                        gated(k - 1)
                    split_lo(dve, c + 3)
                    if not first:
                        low(k - 1)
                self.loops(dve, pair)
                gated(At(self.n - 1))
                low(At(self.n - 1))
                self.down.dve(dve)

        parts, f0, c0, r0 = [], 0, C_FF, R_FF
        for n in FF_PARTS:
            parts.append(Part(n, f0, c0, r0))
            f0, c0, r0 = f0 + n, c0 + 2 * n + KT, r0 + 2 * n + KT
        R_END = r0

        block = ctx.enter_context(nc.Block())

        @block.sync
        def _(sp):
            sp.dma_start(CON[:, 0:K_FIRST], constants[:, 0:K_FIRST]).then_inc(s_x[0], 16)
            for g in range(0, KT, GRP):
                sp.dma_start(X[:, g:g + GRP, :], x_in[:, g:g + GRP, :]).then_inc(s_x[g // GRP], 16)
            sp.dma_start(VEC[:, 0:V_FIRST], vectors[:, 0:V_FIRST]).then_inc(s_vec, 16)
            for s in range(RING):
                sp.dma_start(RAW[:, s, :], stream[s]).then_inc(raw_ready[s], 16)
            sp.dma_start(CON[:, K_FIRST:], constants[:, K_FIRST:]).then_inc(s_rest, 16)
            sp.dma_start(VEC[:, V_FIRST:], vectors[:, V_FIRST:]).then_inc(s_rest, 16)
            sp.dma_start(MB[:], mem_in).then_inc(s_mem, 16)
            with sp.Fori(1, C_END // RING) as i:
                for s in range(RING):
                    c = At(s, RING, i)
                    wait(sp, mm_done, c - (RING - 1))
                    sp.dma_start(RAW[:, s, :], stream[c.v]).then_inc(raw_ready[s], 16)
            for c in range(C_END // RING * RING, C_END):
                sp.wait_ge(mm_done, c - (RING - 1))
                sp.dma_start(RAW[:, c % RING, :], stream[c]).then_inc(raw_ready[c % RING], 16)
            for g in range(0, KT, GRP):
                taken(sp, At(R_END - KT + g + GRP - 1))
                taken(sp, At(R_END - KT + g + GRP - 2))
                sp.dma_start(out[:, g:g + GRP, :], X[:, g:g + GRP, :]).then_inc(s_out, 16)
            sp.wait_ge(s_out, 16 * (KT // GRP))

        @block.tensor
        def _(pe):
            sums_first(pe, norm_conv)
            conv_pe(pe)
            conv_out.pe(pe)
            pe.wait_ge(s_rest, 32)
            hgrn_pe(pe)
            hgrn_out.pe(pe)
            mixa_pe(pe)
            mixb_pe(pe)
            gla_pe(pe)
            mix_out.pe(pe)
            cross_pe(pe)
            for part in parts:
                part.pe(pe)

        @block.scalar
        def _(act):
            squares_first(act, norm_conv)
            split_hi(act, At(0))
            norm_conv.root(act)
            norm_conv.high(act, lambda: split_hi(act, At(1)))
            split_hi(act, At(2))
            conv_act(act)
            conv_out.act(act)
            norm_hg.root(act)
            norm_hg.high(act)
            act.wait_ge(s_rest, 32)
            hgrn_act(act)
            hgrn_out.act(act)
            norm_mix.root(act)
            norm_mix.high(act)
            mixa_act(act)
            mixb_act(act)
            gla_act(act)
            mix_out.act(act)
            norm_cross.root(act)
            norm_cross.high(act)
            cross_act(act)
            norm_ff.root(act)
            norm_ff.high(act)
            for part in parts:
                part.act(act)

        @block.vector
        def _(dve):
            dve.wait_ge(s_vec, 16)
            for g, x in enumerate(s_x):
                dve.wait_ge(x, 16 if g else 32)
            split_lo(dve, At(0))
            norm_conv.scale(dve, lambda: split_lo(dve, At(1)))
            conv_dve(dve)
            conv_out.dve(dve)
            dve.wait_ge(s_rest, 32)
            norm_hg.scale(dve)
            hgrn_dve(dve)
            hgrn_out.dve(dve)
            norm_mix.scale(dve)
            mixa_dve(dve)
            mixb_dve(dve)
            gla_dve(dve)
            mix_out.dve(dve)
            norm_cross.scale(dve)
            cross_dve(dve)
            norm_ff.scale(dve)
            for part in parts:
                part.dve(dve)

        @block.gpsimd
        def _(pool):
            conv_pool(pool)


def _stream(g):
    def tiles(w, k=KT):
        w = np.asarray(w)
        f = w.shape[1] // P
        out = np.zeros((f, P, KT, P), np.float32)
        out[:, :, :k] = w.reshape(k, P, f, P).transpose(2, 1, 0, 3)
        return out.reshape(f, P, CW)

    out = np.empty((C_END, P, CW), np.float32)
    w = tiles(g["conv_w_in"][0])
    for n, part in enumerate((1, 0, 2)):
        out[C_CONV + n:C_CONVO:3] = w[part * KT:(part + 1) * KT]
    out[C_CONVO:C_HG] = tiles(g["conv_w_out"][0])
    w = tiles(g["hgrn_w_in"][0])
    for n, part in enumerate((1, 2, 0, 3, 4)):
        out[C_HG + n:C_HGO:5] = w[part * KT:(part + 1) * KT]
    out[C_HGO:C_MIXA] = tiles(g["hgrn_w_out"][0])
    w = np.asarray(g["w_in_2"][0])
    at = np.cumsum([0, 1024, 256, 256, 256, 256, 256, 256, 24, 512, 512, 1024, 16, 1024])
    part = {n: w[:, a:b] for n, a, b in zip(
        ["q", "kc", "vc", "ks", "vs", "kw", "vw", "gate", "ql", "kl", "vl", "al", "rl"], at, at[1:])}
    gate = np.zeros((D, P), np.float32)
    gate[:, 0:24] = part["gate"]
    gate[:, 32:48] = part["al"]
    for n, name in enumerate(MIXA):
        if name[0] in "KV":
            x = np.asarray(g["w_ck1_2" if name[0] == "K" else "w_cv1_2"][0]).reshape(4, 8, P, 256)
            out[C_MIXA + n] = x[int(name[1])].transpose(1, 0, 2).reshape(P, CW)
        elif name == "gate":
            out[C_MIXA + n] = tiles(gate)[0]
        else:
            k = int(name[2])
            out[C_MIXA + n] = tiles(part[name[:2]][:, k * P:(k + 1) * P])[0]
    q = tiles(part["q"])
    rest = np.concatenate([tiles(part[n]) for n in ("ql", "kl", "vl", "rl")])
    for j in range(8):
        out[C_MIXB + 4 * j] = q[j]
        out[C_MIXB + 4 * j + 1:C_MIXB + 4 * j + 4] = rest[3 * j:3 * j + 3]
    out[C_MEM:C_MIXO:2] = tiles(g["w_ck_2"][0])
    out[C_MEM + 1:C_MIXO:2] = tiles(g["w_cv_2"][0])
    out[C_MIXO:C_CQ] = tiles(g["w_out_2"][0])
    out[C_CQ:C_CO] = tiles(g["w_cq_2"][0])
    out[C_CO:C_FF] = np.asarray(g["w_co_2"][0]).reshape(4, P, 4, 4, P).transpose(2, 1, 3, 0, 4).reshape(4, P, CW)
    gu, down = np.asarray(g["w_gu_2"][0]), np.asarray(g["w_down_2"][0])
    c, f0 = C_FF, 0
    for n in FF_PARTS:
        out[c:c + 2 * n:2] = tiles(gu[:, f0 * P:(f0 + n) * P])
        out[c + 1:c + 2 * n:2] = tiles(gu[:, DFF + f0 * P:DFF + (f0 + n) * P])
        out[c + 2 * n:c + 2 * n + KT] = tiles(down[f0 * P:(f0 + n) * P], n)
        c += 2 * n + KT
        f0 += n
    return out


def _vectors(g):
    v = np.zeros((P, V_COLS), np.float32)

    def put(name, a):
        a = np.asarray(a, np.float32)
        v[:a.shape[0], V_AT[name]:V_AT[name] + a.shape[1]] = a

    def cols(a):
        return np.asarray(a).reshape(-1, P).T
    for name, src in [("conv_norm", "conv_norm"), ("dw_b", "conv_dw_b"), ("ln_g", "conv_ln_g"),
                      ("ln_b", "conv_ln_b"), ("hgrn_norm", "hgrn_norm"), ("o_norm", "hgrn_o_norm"),
                      ("g_mix", "g_mix_2"), ("g_q", "g_q_2"), ("g_kc", "g_kc_2"), ("g_ks", "g_ks_2"),
                      ("g_kw", "g_kw_2"), ("g_nsa", "g_nsa_out_2"), ("b_gk", "b_gk_2"),
                      ("g_gla", "g_gla_out_2"), ("g_cross", "g_cross_2"), ("g_mem", "g_mem_2"),
                      ("g_cq", "g_cq_2"), ("g_ck", "g_ck_2"), ("g_ffn", "g_ffn_2")]:
        put(name, cols(g[src][0]))
    put("dw", np.asarray(g["conv_dw"][0]).reshape(TAPS, KT, P).transpose(2, 1, 0).reshape(P, -1))
    for n in range(2):
        put(f"lbf{n}", cols(g["hgrn_lb_fwd"][n]))
        put(f"lbb{n}", cols(g["hgrn_lb_bwd"][n]))
    put("b_gate", np.asarray(g["b_nsa_gate_2"][0])[:, None])
    put("pe_k", np.asarray(g["pe_k_2"][0]).T)
    put("pe_v", np.asarray(g["pe_v_2"][0]).T)
    put("ck2", np.asarray(g["w_ck2_2"][0]).reshape(2, P, P).transpose(1, 0, 2).reshape(P, 256))
    put("cv2", np.asarray(g["w_cv2_2"][0]).reshape(2, P, P).transpose(1, 0, 2).reshape(P, 256))
    v[32:48, V_AT["gk2"]:V_AT["gk2"] + 512] = np.asarray(g["w_gk2_2"][0])
    return v


def _feature_major(a):
    return np.ascontiguousarray(np.asarray(a)[0].T.reshape(KT, P, T).transpose(1, 0, 2))


def kernel(**inputs):
    import concourse.bacc as _bacc
    from concourse.bass_utils import run_bass_kernel_spmd as _run

    nc = _bacc.Bacc("TRN2", target_bir_lowering=False, num_devices=1)
    arrays = {"x_dram": _feature_major(inputs["x"]), "mem_dram": _feature_major(inputs["mem_2"]),
              "stream_dram": _stream(inputs), "vectors_dram": _vectors(inputs),
              "constants_dram": make_constants()}
    args = [nc.dram_tensor(n, a.shape, F32, kind="ExternalInput").ap() for n, a in arrays.items()]
    out = nc.dram_tensor("out_dram", (P, KT, T), F32, kind="ExternalOutput").ap()
    build(nc, *args, out)
    r = _run(nc, [arrays], core_ids=[0])
    got = np.asarray(r.results[0]["out_dram"])
    return np.ascontiguousarray(got.transpose(1, 0, 2).reshape(D, T).T)[None]
```
